# Optimizing a Trainium2 kernel written in Bass

```python
import jax
import jax.numpy as jnp
from jax import lax
import numpy as np

D_MODEL = 1024
BATCH = 1
SEQ = 256
DEPTH = 2

MEM_LEN = 256
N_EVEN = (DEPTH + 1) // 2
N_ODD = DEPTH // 2
D_FF = 2816
NORM_EPS = 1e-6
ATTN_BLOCK = 128

RET_HEADS = 4
RET_DK = 128
RET_DV = 128
RET_CHUNK = 128
RET_ROPE_BASE = 10000.0

SSM_HEADS = 8
SSM_HEAD_DIM = 64
SSM_D_INNER = SSM_HEADS * SSM_HEAD_DIM
SSM_D_STATE = 64
SSM_GROUPS = 2
SSM_CONV = 4
SSM_CHUNK = 128
SSM_CONV_DIM = SSM_D_INNER + 2 * SSM_GROUPS * SSM_D_STATE

EVEN_SPLITS = (RET_HEADS * RET_DK, RET_HEADS * RET_DK, RET_HEADS * RET_DV, RET_HEADS * RET_DV, SSM_D_INNER, SSM_CONV_DIM, SSM_HEADS)
EVEN_IN = sum(EVEN_SPLITS)
EVEN_MIX = RET_HEADS * RET_DV + SSM_D_INNER

NSA_HEADS = 8
NSA_KV_HEADS = 2
NSA_HEAD_DIM = 64
NSA_CMP_BLOCK = 32
NSA_CMP_STRIDE = 16
NSA_CMP_HIDDEN = 256
NSA_SEL_BLOCK = 64
NSA_TOPN = 16
NSA_WINDOW = 512
NSA_SEL_QBLOCK = 64
NSA_FORCE_SCORE = 1e6

SWA_HEADS = 8
SWA_KV_HEADS = 2
SWA_HEAD_DIM = 64
SWA_WINDOW = 128

ODD_SPLITS = (NSA_HEADS * NSA_HEAD_DIM,) + (NSA_KV_HEADS * NSA_HEAD_DIM,) * 6 + (3 * NSA_HEADS, SWA_HEADS * SWA_HEAD_DIM, SWA_KV_HEADS * SWA_HEAD_DIM, SWA_KV_HEADS * SWA_HEAD_DIM)
ODD_IN = sum(ODD_SPLITS)
ODD_MIX = NSA_HEADS * NSA_HEAD_DIM + SWA_HEADS * SWA_HEAD_DIM

XATTN_HEADS = 4
XATTN_HEAD_DIM = D_MODEL // XATTN_HEADS

kernel_name = 'hybrid_retnet_mamba2_nsa_swa_macaron'

def split_last(t, sizes):
    cuts = [int(c) for c in np.cumsum(sizes)[:-1]]
    return jnp.split(t, cuts, axis=-1)

def rmsnorm(x, w):
    xf = x.astype(jnp.float32)
    y = xf * lax.rsqrt(jnp.mean(xf * xf, axis=-1, keepdims=True) + NORM_EPS)
    return (y * w.astype(jnp.float32)).astype(x.dtype)

def swiglu(h, w_gate, w_up, w_down):
    return (jax.nn.silu(h @ w_gate) * (h @ w_up)) @ w_down

def masked_softmax(s, mask):
    s = jnp.where(mask, s, -jnp.inf)
    m = jnp.max(s, axis=-1, keepdims=True)
    m = jnp.where(jnp.isfinite(m), m, 0.0)
    p = jnp.exp(s - m)
    return p / jnp.maximum(jnp.sum(p, axis=-1, keepdims=True), 1e-30)

def sink_softmax(s, mask, sink):
    s = jnp.where(mask, s, -jnp.inf)
    m = jnp.maximum(jnp.max(s, axis=-1, keepdims=True), sink)
    p = jnp.exp(s - m)
    return p / (jnp.sum(p, axis=-1, keepdims=True) + jnp.exp(sink - m))

def rotate_pairs(t, cos, sin):
    t1 = t[..., 0::2]
    t2 = t[..., 1::2]
    return jnp.stack([t1 * cos - t2 * sin, t1 * sin + t2 * cos], axis=-1).reshape(t.shape)

def retention(q, k, v):
    bsz, seq, nh, dk = q.shape
    dv = v.shape[-1]
    L = RET_CHUNK
    nc = seq // L
    cdt = q.dtype
    pos = jnp.arange(seq, dtype=jnp.float32)
    inv_freq = 1.0 / (RET_ROPE_BASE ** jnp.linspace(0.0, 1.0, dk // 2, dtype=jnp.float32))
    ang = pos[:, None] * inv_freq[None, :]
    cos = jnp.cos(ang)[:, None, :].astype(cdt)
    sin = jnp.sin(ang)[:, None, :].astype(cdt)
    q = rotate_pairs(q, cos, sin)
    k = rotate_pairs(k, cos, sin) * (dk ** -0.5)
    log_g = jnp.log1p(-jnp.exp2(-5.0 - jnp.arange(nh, dtype=jnp.float32)))
    idx = jnp.arange(L, dtype=jnp.float32)
    diff = idx[:, None] - idx[None, :]
    dmat = jnp.where(diff >= 0, jnp.exp(jnp.maximum(diff, 0.0)[None] * log_g[:, None, None]), 0.0).astype(cdt)
    zeta = jnp.exp((L - 1 - idx)[None, :] * log_g[:, None]).astype(cdt)
    xi = jnp.exp((idx + 1)[None, :] * log_g[:, None]).astype(cdt)
    chunk_decay = jnp.exp(L * log_g).astype(cdt)
    qc = q.reshape(bsz, nc, L, nh, dk)
    kc = k.reshape(bsz, nc, L, nh, dk)
    vc = v.reshape(bsz, nc, L, nh, dv)
    scores = jnp.einsum('bcihd,bcjhd->bchij', qc, kc) * dmat
    inner = jnp.einsum('bchij,bcjhe->bcihe', scores, vc)
    chunk_kv = jnp.einsum('bcjhd,hj,bcjhe->cbhde', kc, zeta, vc)

    def step(state, kv):
        return chunk_decay[None, :, None, None] * state + kv, state

    _, s_in = lax.scan(step, jnp.zeros((bsz, nh, dk, dv), chunk_kv.dtype), chunk_kv)
    cross = jnp.einsum('bcihd,hi,cbhde->bcihe', qc, xi, s_in)
    o = (inner + cross).reshape(bsz, seq, nh, dv).astype(jnp.float32)
    o = o * lax.rsqrt(jnp.mean(o * o, axis=-1, keepdims=True) + NORM_EPS)
    return o.astype(cdt)

def ssd_scan(xh, dt, a, bm, cm):
    bsz, seq, nh, hp = xh.shape
    ng, ns = bm.shape[2], bm.shape[3]
    ne = nh // ng
    L = SSM_CHUNK
    nc = seq // L
    cdt = xh.dtype
    cums = jnp.cumsum((dt * a).reshape(bsz, nc, L, ng, ne), axis=2)
    xdt = (xh * dt[..., None].astype(cdt)).reshape(bsz, nc, L, ng, ne, hp)
    bc = bm.reshape(bsz, nc, L, ng, ns)
    cc = cm.reshape(bsz, nc, L, ng, ns)
    idx = jnp.arange(L)
    causal = (idx[:, None] >= idx[None, :])[:, :, None, None]
    seg = cums[:, :, :, None] - cums[:, :, None, :]
    lmat = jnp.exp(jnp.where(causal, seg, -jnp.inf)).astype(cdt)
    cb = jnp.einsum('bclgn,bcsgn->bclsg', cc, bc)
    y_diag = jnp.einsum('bclsg,bclsge,bcsgep->bclgep', cb, lmat, xdt)
    decay_states = jnp.exp(cums[:, :, -1:] - cums).astype(cdt)
    states = jnp.einsum('bclgn,bclge,bclgep->cbgepn', bc, decay_states, xdt)
    chunk_decay = jnp.exp(cums[:, :, -1]).astype(cdt).transpose(1, 0, 2, 3)

    def step(state, inp):
        dec, st = inp
        return dec[..., None, None] * state + st, state

    _, s_in = lax.scan(step, jnp.zeros((bsz, ng, ne, hp, ns), states.dtype), (chunk_decay, states))
    y_off = jnp.einsum('bclgn,cbgepn,bclge->bclgep', cc, s_in, jnp.exp(cums).astype(cdt))
    return (y_diag + y_off).reshape(bsz, seq, nh, hp)

def even_mixer(h, w_in, w_out, conv_w, conv_b, dt_bias, a_log, d_skip, norm_w):
    bsz, seq, _ = h.shape
    q, k, v, g, z, xbc, dt_raw = split_last(h @ w_in, EVEN_SPLITS)
    o_ret = retention(q.reshape(bsz, seq, RET_HEADS, RET_DK), k.reshape(bsz, seq, RET_HEADS, RET_DK), v.reshape(bsz, seq, RET_HEADS, RET_DV))
    o_ret = jax.nn.silu(g) * o_ret.reshape(bsz, seq, RET_HEADS * RET_DV)
    xbc = lax.conv_general_dilated(xbc, conv_w[:, None, :].astype(xbc.dtype), window_strides=(1,), padding=[(SSM_CONV - 1, 0)], dimension_numbers=('NWC', 'WIO', 'NWC'), feature_group_count=SSM_CONV_DIM)
    xbc = jax.nn.silu(xbc + conv_b)
    xs, bm, cm = split_last(xbc, (SSM_D_INNER, SSM_GROUPS * SSM_D_STATE, SSM_GROUPS * SSM_D_STATE))
    dt = jax.nn.softplus(dt_raw.astype(jnp.float32) + dt_bias.astype(jnp.float32))
    a = -jnp.exp(a_log.astype(jnp.float32))
    xh = xs.reshape(bsz, seq, SSM_HEADS, SSM_HEAD_DIM)
    y = ssd_scan(xh, dt, a, bm.reshape(bsz, seq, SSM_GROUPS, SSM_D_STATE), cm.reshape(bsz, seq, SSM_GROUPS, SSM_D_STATE))
    y = (y + d_skip[:, None] * xh).reshape(bsz, seq, SSM_D_INNER)
    y = rmsnorm(y * jax.nn.silu(z), norm_w)
    return jnp.concatenate([o_ret, y], axis=-1) @ w_out

def banded_attention(q, k, v, window, sinks=None):
    bsz, ng, ne, seq, hd = q.shape
    qb_size = ATTN_BLOCK
    nb = seq // qb_size
    nprev = -(-(window - 1) // qb_size)
    nk = (nprev + 1) * qb_size

    def band(t):
        tb = jnp.pad(t.reshape(bsz, ng, nb, qb_size, hd), ((0, 0), (0, 0), (nprev, 0), (0, 0), (0, 0)))
        return jnp.concatenate([tb[:, :, j:j + nb] for j in range(nprev + 1)], axis=3)

    kb, vb = band(k), band(v)
    blk = jnp.arange(nb)
    qpos = blk[:, None] * qb_size + jnp.arange(qb_size)[None, :]
    kpos = (blk[:, None] - nprev) * qb_size + jnp.arange(nk)[None, :]
    rel = qpos[:, :, None] - kpos[:, None, :]
    mask = (rel >= 0) & (rel < window) & (kpos[:, None, :] >= 0)
    s = jnp.einsum('bgeiqd,bgikd->bgeiqk', q.reshape(bsz, ng, ne, nb, qb_size, hd), kb).astype(jnp.float32) * (hd ** -0.5)
    if sinks is None:
        p = masked_softmax(s, mask)
    else:
        p = sink_softmax(s, mask, sinks.astype(jnp.float32)[None, :, :, None, None, None])
    o = jnp.einsum('bgeiqk,bgikd->bgeiqd', p.astype(v.dtype), vb)
    return o.reshape(bsz, ng, ne, seq, hd)

def selected_block_attention(q, k, v, sel_idx):
    bsz, ng, ne, seq, hd = q.shape
    n = sel_idx.shape[-1]
    qb_size = NSA_SEL_QBLOCK
    nq = seq // qb_size
    kb = k.reshape(bsz, ng, seq // NSA_SEL_BLOCK, NSA_SEL_BLOCK, hd)
    vb = v.reshape(bsz, ng, seq // NSA_SEL_BLOCK, NSA_SEL_BLOCK, hd)
    q_ch = q.reshape(bsz, ng, ne, nq, qb_size, hd).transpose(3, 0, 1, 2, 4, 5)
    idx_ch = sel_idx.reshape(bsz, ng, nq, qb_size, n).transpose(2, 0, 1, 3, 4)
    t_ch = jnp.arange(seq).reshape(nq, qb_size)
    bi = jnp.arange(bsz)[:, None, None, None]
    gi = jnp.arange(ng)[None, :, None, None]
    offs = jnp.arange(NSA_SEL_BLOCK)
    scale = hd ** -0.5

    def body(args):
        qc, ic, tc = args
        kg = kb[bi, gi, ic].reshape(bsz, ng, qb_size, n * NSA_SEL_BLOCK, hd)
        vg = vb[bi, gi, ic].reshape(bsz, ng, qb_size, n * NSA_SEL_BLOCK, hd)
        s = jnp.einsum('bgeqd,bgqmd->bgeqm', qc, kg).astype(jnp.float32) * scale
        kpos = (ic[..., None] * NSA_SEL_BLOCK + offs).reshape(bsz, ng, qb_size, n * NSA_SEL_BLOCK)
        mask = (kpos <= tc[None, None, :, None])[:, :, None]
        p = masked_softmax(s, mask)
        return jnp.einsum('bgeqm,bgqmd->bgeqd', p.astype(vg.dtype), vg)

    o = lax.map(body, (q_ch, idx_ch, t_ch))
    return o.transpose(1, 2, 3, 0, 4, 5).reshape(bsz, ng, ne, seq, hd)

def native_sparse_attention(q, kc, vc, ks, vs, kw, vw, g, cmp_pe, cmp_w1, cmp_w2):
    bsz, ng, ne, seq, hd = q.shape
    scale = hd ** -0.5
    tpos = jnp.arange(seq)
    n_cmp = (seq - NSA_CMP_BLOCK) // NSA_CMP_STRIDE + 1
    starts = jnp.arange(n_cmp) * NSA_CMP_STRIDE
    tok = starts[:, None] + jnp.arange(NSA_CMP_BLOCK)[None, :]

    def compress(t, pe, w1, w2):
        blk = t[:, :, tok] + pe
        return jax.nn.silu(blk.reshape(bsz, ng, n_cmp, NSA_CMP_BLOCK * hd) @ w1) @ w2

    k_cmp = compress(kc, cmp_pe[0], cmp_w1[0], cmp_w2[0])
    v_cmp = compress(vc, cmp_pe[1], cmp_w1[1], cmp_w2[1])
    s_cmp = jnp.einsum('bgeqd,bgnd->bgeqn', q, k_cmp).astype(jnp.float32) * scale
    p_cmp = masked_softmax(s_cmp, (starts + NSA_CMP_BLOCK - 1)[None, :] <= tpos[:, None])
    o_cmp = jnp.einsum('bgeqn,bgnd->bgeqd', p_cmp.astype(vc.dtype), v_cmp)
    n_sel = seq // NSA_SEL_BLOCK
    sel_start = jnp.arange(n_sel) * NSA_SEL_BLOCK
    overlap = ((starts[:, None] < sel_start[None, :] + NSA_SEL_BLOCK) & (starts[:, None] + NSA_CMP_BLOCK > sel_start[None, :])).astype(jnp.float32)
    imp = jnp.einsum('bgqn,nj->bgqj', jnp.sum(p_cmp, axis=2), overlap)
    cur = (tpos // NSA_SEL_BLOCK)[:, None]
    jb = jnp.arange(n_sel)[None, :]
    valid = jb <= cur
    forced = valid & ((jb == 0) | (jb == cur) | (jb == cur - 1))
    score = jnp.where(forced, NSA_FORCE_SCORE, jnp.where(valid, imp, -jnp.inf))
    _, sel_idx = lax.top_k(score, min(NSA_TOPN, n_sel))
    o_sel = selected_block_attention(q, ks, vs, sel_idx)
    o_win = banded_attention(q, kw, vw, NSA_WINDOW)
    return g[..., 0:1] * o_cmp + g[..., 1:2] * o_sel + g[..., 2:3] * o_win

def odd_mixer(h, w_in, w_out, cmp_pe, cmp_w1, cmp_w2, sinks):
    bsz, seq, _ = h.shape
    q_n, kc, vc, ks, vs, kw, vw, gates, q_s, k_s, v_s = split_last(h @ w_in, ODD_SPLITS)

    def q_heads(t, nh, nkv, hd):
        return t.reshape(bsz, seq, nkv, nh // nkv, hd).transpose(0, 2, 3, 1, 4)

    def kv_heads(t, nkv, hd):
        return t.reshape(bsz, seq, nkv, hd).transpose(0, 2, 1, 3)

    def merge(o):
        return o.transpose(0, 3, 1, 2, 4).reshape(bsz, seq, -1)

    g = jax.nn.sigmoid(gates.astype(jnp.float32)).astype(h.dtype)
    g = g.reshape(bsz, seq, NSA_KV_HEADS, NSA_HEADS // NSA_KV_HEADS, 3).transpose(0, 2, 3, 1, 4)
    o_nsa = native_sparse_attention(
        q_heads(q_n, NSA_HEADS, NSA_KV_HEADS, NSA_HEAD_DIM),
        kv_heads(kc, NSA_KV_HEADS, NSA_HEAD_DIM), kv_heads(vc, NSA_KV_HEADS, NSA_HEAD_DIM),
        kv_heads(ks, NSA_KV_HEADS, NSA_HEAD_DIM), kv_heads(vs, NSA_KV_HEADS, NSA_HEAD_DIM),
        kv_heads(kw, NSA_KV_HEADS, NSA_HEAD_DIM), kv_heads(vw, NSA_KV_HEADS, NSA_HEAD_DIM),
        g, cmp_pe, cmp_w1, cmp_w2)
    o_swa = banded_attention(
        q_heads(q_s, SWA_HEADS, SWA_KV_HEADS, SWA_HEAD_DIM),
        kv_heads(k_s, SWA_KV_HEADS, SWA_HEAD_DIM), kv_heads(v_s, SWA_KV_HEADS, SWA_HEAD_DIM),
        SWA_WINDOW, sinks.reshape(SWA_KV_HEADS, SWA_HEADS // SWA_KV_HEADS))
    return jnp.concatenate([merge(o_nsa), merge(o_swa)], axis=-1) @ w_out

def cross_attention(h, memn, wq, wkv, wo):
    bsz, seq, _ = h.shape
    m = memn.shape[1]
    q = (h @ wq).reshape(bsz, seq, XATTN_HEADS, XATTN_HEAD_DIM)
    kv = (memn @ wkv).reshape(bsz, m, 2, XATTN_HEADS, XATTN_HEAD_DIM)
    s = jnp.einsum('bshd,bmhd->bhsm', q, kv[:, :, 0]).astype(jnp.float32) * (XATTN_HEAD_DIM ** -0.5)
    p = jax.nn.softmax(s, axis=-1).astype(h.dtype)
    o = jnp.einsum('bhsm,bmhd->bshd', p, kv[:, :, 1]).reshape(bsz, seq, XATTN_HEADS * XATTN_HEAD_DIM)
    return o @ wo

def setup_inputs(seed: int = 0) -> dict:
    key = jax.random.key(seed)
    keys = jax.random.split(key, 32)
    f32 = jnp.float32

    def nrm(k, shape, scale):
        return jax.random.normal(k, shape, f32) * scale

    dt0 = jnp.exp(jax.random.uniform(keys[16], (N_EVEN, SSM_HEADS), f32, float(np.log(1e-3)), float(np.log(1e-1))))
    return {
        'x': nrm(keys[0], (BATCH, SEQ, D_MODEL), 1.0),
        'mem': nrm(keys[1], (BATCH, MEM_LEN, D_MODEL), 1.0),
        'norm_w': 1.0 + nrm(keys[2], (DEPTH, 4, D_MODEL), 0.02),
        'final_norm_w': 1.0 + nrm(keys[3], (D_MODEL,), 0.02),
        'mem_norm_w': 1.0 + nrm(keys[4], (D_MODEL,), 0.02),
        'ffn_w_gate': nrm(keys[5], (DEPTH, 2, D_MODEL, D_FF), D_MODEL ** -0.5),
        'ffn_w_up': nrm(keys[6], (DEPTH, 2, D_MODEL, D_FF), D_MODEL ** -0.5),
        'ffn_w_down': nrm(keys[7], (DEPTH, 2, D_FF, D_MODEL), D_FF ** -0.5),
        'xattn_wq': nrm(keys[8], (DEPTH, D_MODEL, XATTN_HEADS * XATTN_HEAD_DIM), D_MODEL ** -0.5),
        'xattn_wkv': nrm(keys[9], (DEPTH, D_MODEL, 2 * XATTN_HEADS * XATTN_HEAD_DIM), D_MODEL ** -0.5),
        'xattn_wo': nrm(keys[10], (DEPTH, XATTN_HEADS * XATTN_HEAD_DIM, D_MODEL), (XATTN_HEADS * XATTN_HEAD_DIM) ** -0.5),
        'even_w_in': nrm(keys[11], (N_EVEN, D_MODEL, EVEN_IN), D_MODEL ** -0.5),
        'even_w_out': nrm(keys[12], (N_EVEN, EVEN_MIX, D_MODEL), EVEN_MIX ** -0.5),
        'ssm_conv_w': nrm(keys[13], (N_EVEN, SSM_CONV, SSM_CONV_DIM), SSM_CONV ** -0.5),
        'ssm_conv_b': nrm(keys[14], (N_EVEN, SSM_CONV_DIM), 0.01),
        'ssm_dt_bias': dt0 + jnp.log(-jnp.expm1(-dt0)),
        'ssm_a_log': jnp.log(jax.random.uniform(keys[17], (N_EVEN, SSM_HEADS), f32, 1.0, 16.0)),
        'ssm_d': 1.0 + nrm(keys[18], (N_EVEN, SSM_HEADS), 0.02),
        'ssm_norm_w': 1.0 + nrm(keys[19], (N_EVEN, SSM_D_INNER), 0.02),
        'odd_w_in': nrm(keys[20], (N_ODD, D_MODEL, ODD_IN), D_MODEL ** -0.5),
        'odd_w_out': nrm(keys[21], (N_ODD, ODD_MIX, D_MODEL), ODD_MIX ** -0.5),
        'nsa_cmp_pe': nrm(keys[22], (N_ODD, 2, NSA_CMP_BLOCK, NSA_HEAD_DIM), 0.02),
        'nsa_cmp_w1': nrm(keys[23], (N_ODD, 2, NSA_CMP_BLOCK * NSA_HEAD_DIM, NSA_CMP_HIDDEN), (NSA_CMP_BLOCK * NSA_HEAD_DIM) ** -0.5),
        'nsa_cmp_w2': nrm(keys[24], (N_ODD, 2, NSA_CMP_HIDDEN, NSA_HEAD_DIM), NSA_CMP_HIDDEN ** -0.5),
        'swa_sinks': nrm(keys[25], (N_ODD, SWA_HEADS), 0.5),
    }

def reference(x, mem, norm_w, final_norm_w, mem_norm_w, ffn_w_gate, ffn_w_up, ffn_w_down, xattn_wq, xattn_wkv, xattn_wo, even_w_in, even_w_out, ssm_conv_w, ssm_conv_b, ssm_dt_bias, ssm_a_log, ssm_d, ssm_norm_w, odd_w_in, odd_w_out, nsa_cmp_pe, nsa_cmp_w1, nsa_cmp_w2, swa_sinks):
    memn = rmsnorm(mem, mem_norm_w)
    for layer in range(DEPTH):
        i = layer // 2
        h = rmsnorm(x, norm_w[layer, 0])
        x = x + 0.5 * swiglu(h, ffn_w_gate[layer, 0], ffn_w_up[layer, 0], ffn_w_down[layer, 0])
        h = rmsnorm(x, norm_w[layer, 1])
        if layer % 2 == 0:
            x = x + even_mixer(h, even_w_in[i], even_w_out[i], ssm_conv_w[i], ssm_conv_b[i], ssm_dt_bias[i], ssm_a_log[i], ssm_d[i], ssm_norm_w[i])
        else:
            x = x + odd_mixer(h, odd_w_in[i], odd_w_out[i], nsa_cmp_pe[i], nsa_cmp_w1[i], nsa_cmp_w2[i], swa_sinks[i])
        h = rmsnorm(x, norm_w[layer, 2])
        x = x + cross_attention(h, memn, xattn_wq[layer], xattn_wkv[layer], xattn_wo[layer])
        h = rmsnorm(x, norm_w[layer, 3])
        x = x + 0.5 * swiglu(h, ffn_w_gate[layer, 1], ffn_w_up[layer, 1], ffn_w_down[layer, 1])
    return rmsnorm(x, final_norm_w)


_drawn_inputs = setup_inputs


def setup_inputs(seed=0):
    import zlib

    import numpy as np

    out = dict(_drawn_inputs(seed))
    spreads = {}
    factors = {'final_norm_w': 27.098,
     'mem_norm_w': 8.0,
     'ssm_conv_b': 8.0,
     'ssm_a_log': 25.584,
     'ssm_d': 5.425,
     'ssm_norm_w': 4.84,
     'nsa_cmp_pe': 47.331,
     'swa_sinks': 60.715}
    for name, (base, spread) in spreads.items():
        noise = np.random.default_rng([zlib.crc32(name.encode()), seed]).standard_normal(out[name].shape)
        drawn = base * np.exp(spread * noise) if base else spread * noise
        out[name] = jnp.asarray(drawn.astype(out[name].dtype))
    for name, factor in factors.items():
        out[name] = (out[name] * factor).astype(out[name].dtype)
    return out
```

```python
from contextlib import ExitStack

import numpy as np

import concourse.bass as bass
from concourse import mybir

F32 = mybir.dt.float32
F32R = mybir.dt.float32r
BF16 = mybir.dt.bfloat16
ALU = mybir.AluOpType
ACT = mybir.ActivationFunctionType
AX = mybir.AxisListType

P = 128
SEQ, MEM, D = 256, 256, 1024
TT = SEQ // P
KT = D // P
DFF = 2816
CW = 256
FJ = DFF // CW
CHUNK = KT * CW
EPS = 1e-6
RING = 3
BIG = 1e30

RET_H, DK = 4, 128
SSM_H, HP, NS, SSM_IN = 8, 64, 64, 512
CONV_CH, CONV_W = 768, 4
XT = CONV_CH // P
EVEN_IN = 3336
HD, NH = 64, 8
N_CMP, CMP_STRIDE, CMP_BLK = 15, 16, 32
CMP_PAIRS = CMP_BLK // 2
XH, XD = 4, 256

CONSTS = {}
_at = 0
for _name, _w in (("ident", P), ("upto", P), ("after", P), ("cos", TT * 64), ("sin", TT * 64),
                  ("decayT", RET_H * P), ("zeta", RET_H), ("xi", RET_H), ("pick", P),
                  ("cmpmask", TT * N_CMP), ("cmpbias", TT * N_CMP)):
    CONSTS[_name] = (_at, _w)
    _at += _w
CONST_W = _at
MASKS = {"causal0": (0, P), "causal1": (P, 2 * P), "band1": (3 * P, 2 * P), "eye": (5 * P, P)}
MASK_W = 6 * P


def shape_constants():
    f = np.float32
    c = np.zeros((P, CONST_W), f)

    def put(name, a):
        at, w = CONSTS[name]
        c[:, at:at + w] = np.asarray(a, f).reshape(P, w)

    i = np.arange(P)
    put("ident", np.eye(P))
    put("upto", i[:, None] <= i[None, :])
    put("after", i[:, None] > i[None, :])
    pos = np.arange(SEQ, dtype=f)
    inv = (f(1.0) / (f(10000.0) ** np.linspace(0.0, 1.0, DK // 2, dtype=f))).astype(f)
    ang = (pos[:, None] * inv[None, :]).astype(f).reshape(TT, P, 64).transpose(1, 0, 2)
    put("cos", np.cos(ang))
    put("sin", np.sin(ang))
    log_g = np.log1p(-np.exp2(-5.0 - np.arange(RET_H)))
    diff = i[None, :] - i[:, None]
    scale = DK ** -0.5
    put("decayT", np.where(diff[:, None, :] >= 0,
                           np.exp(np.maximum(diff, 0)[:, None, :] * log_g[None, :, None]), 0.0) * scale)
    put("zeta", np.exp((P - 1 - i)[:, None] * log_g[None, :]) * scale)
    put("xi", np.exp((i + 1)[:, None] * log_g[None, :]))
    pick = np.zeros((P, 2, P // 2))
    for par in range(2):
        pick[2 * np.arange(P // 2) + par, par, np.arange(P // 2)] = 1
    put("pick", pick)
    tok = np.arange(SEQ).reshape(TT, P).T
    seen = (np.arange(N_CMP) * CMP_STRIDE + CMP_BLK - 1)[None, None, :] <= tok[:, :, None]
    put("cmpmask", seen)
    put("cmpbias", np.where(seen, 0.0, -BIG))
    m = np.zeros((P, MASK_W), f)
    causal = np.where(i[:, None] >= i[None, :], 0.0, -BIG)
    m[:, 0:P] = causal
    m[:, 2 * P:3 * P] = causal
    m[:, 3 * P:4 * P] = np.where(i[None, :] > i[:, None], 0.0, -BIG)
    m[:, 4 * P:5 * P] = causal
    m[:, 5 * P:6 * P] = np.eye(P)
    return c, m


FFN_CHUNKS = 3 * FJ
EVEN_ORDER = ["x0", "x1", "x2", "q0", "q1", "k0", "k1", "v0", "v1", "g0", "g1", "z0", "z1"]
ODD_ORDER = ["s", "w", "c", "qn0", "qn1", "qs0", "qs1", "a"]


def chunk_plan():
    at, n = {}, 0

    def take(names):
        nonlocal n
        for x in names:
            at[x] = n
            n += 1

    for layer in range(2):
        at["ffn", layer, 0] = n
        n += FFN_CHUNKS
        kv = [("kv", layer, i) for i in range(8)]
        if layer == 0:
            take([("even", x) for x in EVEN_ORDER])
            take(kv)
            take([("mixout", layer, i) for i in range(4)])
        else:
            take([("odd", x) for x in ODD_ORDER])
            take([("cmp", i) for i in range(4)])
            take(kv)
            take([("mixout", layer, i) for i in range(4)])
        take([("wq", layer, i) for i in range(4)])
        take([("wo", layer, i) for i in range(4)])
        at["ffn", layer, 1] = n
        n += FFN_CHUNKS
    return at, n


def build(nc, d, out):
    at, n_chunks = chunk_plan()
    ctx = ExitStack()
    with ctx:
        def sb(name, shape, dt=F32):
            return ctx.enter_context(nc.sbuf_tensor(name, shape, dt))

        def sem(name):
            return ctx.enter_context(nc.semaphore(name))

        ps = ctx.enter_context(nc.psum_tensor("ps", [P, 8, 512], F32))
        x = sb("x", [P, TT, D])
        xn = sb("xn", [P, TT, D])
        hT_hi = sb("hT_hi", [P, KT, SEQ], F32R)
        hT_lo = sb("hT_lo", [P, KT, SEQ], F32R)
        memT_hi = sb("memT_hi", [P, KT, MEM], F32R)
        memT_lo = sb("memT_lo", [P, KT, MEM], F32R)
        raw = sb("raw", [P, RING, CHUNK])
        w_hi = sb("w_hi", [P, RING, CHUNK], F32R)
        w_lo = sb("w_lo", [P, RING, CHUNK], F32R)
        xk = sb("xk", [P, KT, MEM])
        xv = sb("xv", [P, TT, D])
        norm_w = sb("norm_w_rows", [P, D])
        consts = sb("consts", [P, CONST_W])
        masks_f = xk[:, 0:3, :].rearrange("p a b -> p (a b)")
        masks = sb("masks", [P, MASK_W], BF16)
        ssq = sb("ssq", [P, 2])
        msq = sb("msq", [P, 16])
        rstd = sb("rstd", [P, 2])
        neg_half = sb("neg_half", [P, 8])
        dt_w = sb("dt_w", [P, KT, SSM_H])
        dt_w_hi = sb("dt_w_hi", [P, KT, SSM_H], F32R)
        dt_w_lo = sb("dt_w_lo", [P, KT, SSM_H], F32R)
        gate_w = sb("gate_w", [P, KT, 3 * NH])
        gate_w_hi = sb("gate_w_hi", [P, KT, 3 * NH], F32R)
        gate_w_lo = sb("gate_w_lo", [P, KT, 3 * NH], F32R)
        conv_w = sb("conv_w", [P, CONV_W, XT])
        conv_b = sb("conv_b", [P, XT])
        head_rows = sb("head_rows", [P, 4, SSM_H])
        w2 = sb("w2", [P, 2, 2, HD])
        pe_pairs = sb("pe_pairs", [P, 2, CMP_PAIRS])
        ssm_nw = sb("ssm_nw", [P, SSM_IN])
        ARENA = 11896
        arena_r = sb("arena_r", [P, 2 * 2 * CMP_PAIRS * 2 * N_CMP], F32R)
        arena = sb("arena", [P, ARENA])

        def part(at_, shape, dt=F32):
            size = int(np.prod(shape))
            assert at_ + size <= ARENA, (at_, shape)
            v = arena[:, at_:at_ + size]
            if dt is not F32:
                v = v.bitcast(dt)
            if len(shape) == 1:
                return v
            names = "abcde"[:len(shape)]
            sizes = {k: s for k, s in zip(names[1:], shape[1:])}
            return v.rearrange(f"p ({' '.join(names)}) -> p {' '.join(names)}", **sizes)

        def const(name, *dims):
            a, w = CONSTS[name]
            v = consts[:, a:a + w]
            if len(dims) > 1:
                names = "abc"[:len(dims)]
                v = v.rearrange(f"p ({' '.join(names)}) -> p {' '.join(names)}",
                                **{k: s for k, s in zip(names[1:], dims[1:])})
            return v

        def mask(name):
            a, w = MASKS[name]
            return masks[:, a:a + w]

        ident = const("ident")
        mem_rows = xv[:, :, :]

        raw_in = [sem(f"raw_in{i}") for i in range(RING)]
        hi_done = sem("hi_done")
        lo_done = sem("lo_done")
        chunks_used = sem("chunks_used")
        small_in = sem("small_in")
        rows_in = sem("rows_in")
        norm_w_in = sem("norm_w_in")
        out_sent = sem("out_sent")
        consts_made = sem("consts_made")
        smalls_split = sem("smalls_split")
        neg_half_set = sem("neg_half_set")
        sq_done = sem("sq_done")
        ms_done = sem("ms_done")
        rstd_done = sem("rstd_done")
        xn_done = sem("xn_done")
        transposed = sem("transposed")
        hT_hi_done = sem("hT_hi_done")
        hT_done = sem("hT_done")
        x_added = sem("x_added")
        silu_done = sem("silu_done")
        mult_done = sem("mult_done")
        gu_hi_done = sem("gu_hi_done")
        gu_done = sem("gu_done")
        oT_hi_done = sem("oT_hi_done")
        oT_done = sem("oT_done")
        kv_read = sem("kv_read")
        act_step, dve_step, pool_step = sem("act_step"), sem("dve_step"), sem("pool_step")

        SETS = {"mem": 0, ("norm", 0, 0): 1, ("norm", 0, 1): 2, "mix0": 3, ("norm", 0, 2): 4,
                ("norm", 0, 3): 5, ("norm", 1, 0): 6, ("norm", 1, 1): 7, ("norm", 1, 2): 8,
                ("norm", 1, 3): 9}

        def norm_no(layer, i):
            return 1 + 4 * layer + i

        def w_view(ap):
            return ap.rearrange("(k p) c -> p k c", p=P)

        def pieces_of(name):
            kind = name[0]
            if kind == "even":
                s = name[1]
                col = {"q": 0, "k": 512, "v": 1024, "g": 1536, "z": 2048, "x": 2560}[s[0]] + CW * int(s[1])
                return [(("k", CW), w_view(d["even_w_in"][0][:, col:col + CW]))]
            if kind == "odd":
                s = name[1]
                if s[0] == "q":
                    base = {"n": 0, "s": 1304}[s[1]] + P * int(s[2])
                    return [(("run", i * P + g * HD), w_view(
                        d["odd_w_in"][0][:, base + g * 256 + i * HD:base + g * 256 + (i + 1) * HD]))
                        for i in range(2) for g in range(2)]
                col = {"c": 512, "s": 768, "w": 1024, "a": 1816}[s]
                return [(("k", CW), w_view(d["odd_w_in"][0][:, col:col + CW]))]
            if kind == "cmp":
                kv, half = name[1] // 2, name[1] % 2
                return [(("k", CW), d["nsa_cmp_w1"][0, kv].rearrange("(k p) c -> p k c", p=P)
                         [:, 8 * half:8 * half + 8, :])]
            layer, i = name[1], name[2]
            if kind == "kv":
                return [(("k", CW), w_view(d["xattn_wkv"][layer][:, i * CW:(i + 1) * CW]))]
            if kind == "wq":
                return [(("k", CW), w_view(d["xattn_wq"][layer][:, i * CW:(i + 1) * CW]))]
            src = d["xattn_wo"][layer] if kind == "wo" else d["even_w_out" if layer == 0 else "odd_w_out"][0]
            return [(("k", D), src[2 * P * i:2 * P * (i + 1), :].rearrange("(k p) c -> p k c", p=P))]

        order = sorted((v, k) for k, v in at.items() if k[0] != "ffn")
        named = {v: k for v, k in order}
        pieces = [len(pieces_of(named[n])) if n in named else 1 for n in range(n_chunks)]

        def landed(n):
            return 16 * sum(pieces[m] for m in range(n % RING, n + 1, RING))

        W_SLOT = CHUNK

        def slot_k(n, width):
            return raw[:, n % RING, :].rearrange("p (k c) -> p k c", c=width)

        g_act = part(0, [512])
        gu = part(512, [512])
        gu_hi = arena_r[:, 0:512].rearrange("p (k c) -> p k c", k=2)
        gu_lo = arena_r[:, 512:1024].rearrange("p (k c) -> p k c", k=2)

        class Even:
            xpad = part(0, [XT, SEQ + 3])
            ld = xk[:, :, :].rearrange("p k c -> p (k c)").rearrange("p (t h s) -> p t h s", t=TT, h=SSM_H)
            xbcT = part(1920, [XT, SEQ])
            q_rot = part(3456, [TT, RET_H, 2, 64])
            o = part(3456, [TT, RET_H, P])
            k_rot = part(4480, [TT, RET_H, 2, 64])
            s = part(4480, [TT, RET_H, P])
            rot = [part(5504 + 256 * i, [TT, 2, 64]) for i in range(4)]
            cbm = part(5504, [TT, 2, P])
            kz = part(6016, [RET_H, P])
            qT = part(6528, [TT, RET_H, P])
            kT = part(7552, [TT, RET_H, P])
            v = part(8576, [TT, RET_H * DK])
            xh = part(9600, [TT, SSM_H, HP])
            xdt = part(10624, [TT, SSM_H, HP])
            mt = xv[:, :, :].rearrange("p t (h s) -> p t h s", h=SSM_H)
            b_tok = part(11648, [P])
            small = part(11776, [112])
            dtr = small[:, 0:16]
            ln1p = small[:, 16:32]
            dt = small[:, 32:48]
            dta = small[:, 48:64]
            ea = small[:, 64:72]
            dec = small[:, 72:80]
            cum = small[:, 80:88]
            ssr = small[:, 88:90]
            rsr = small[:, 90:92]
            msr = small[:, 92:94]
            osq = small[:, 96:104]
            ors = small[:, 104:112]
            oms = msq[:, 8:16]
            yc = part(5504, [SSM_H, HP])
            xdtd = part(0, [SSM_H, HP])
            kv = part(512, [RET_H, P])
            sT = part(1024, [SSM_IN])
            dtr = small[:, 0:16]
        ev = Even

        even_sems = {}
        for name in ("xpad_zero", "act_read", "conv_done", "xbc_done", "dt_mm",
                     "dt_raw", "dt_done", "ln_done", "dta_done", "ea_done", "ld_done", "rot_read",
                     "rot_done", "xs_T", "xh_done", "cb_mm", "cbm_done", "dec_mm", "dec_done",
                     "seg_mm", "seg_exp", "mt_done", "xdt_done", "xdtd_done", "qk_T", "qkT_done",
                     "kz_done", "ret_s_mm", "s_done", "st_mm", "st_done", "ret_kv_mm", "kvs_done",
                     "y_mm", "yoff_mm", "y_read", "o_mm", "o_read", "dx_done", "y_sq", "o_sq", "o_ssq",
                     "y_rstd", "o_rstd", "mix_done", "y_ready"):
            even_sems[name] = sem("e_" + name)
        es = even_sems

        class Odd:
            qn = part(0, [4, SEQ])
            qs = part(1024, [4, SEQ])
            kT = part(2048, [3, SEQ])
            v = part(2816, [3, TT, P])
            kc = part(3584, [TT, 2 * P])
            xc = part(4608, [2, CMP_PAIRS, 2, N_CMP])
            xc_hi, xc_lo = (arena_r[:, i * 960:(i + 1) * 960].rearrange("p (k i n) -> p k i n", k=2, i=CMP_PAIRS)
                            for i in range(2))
            hid = part(6144, [2, 2, 2 * N_CMP])
            kcT = part(6272, [16])
            vc = part(6288, [2, HD])
            pc = part(6416, [TT, NH, N_CMP])
            pcT = part(6656, [NH, SEQ])
            p0 = part(8704, [4, P])
            p1 = part(9216, [4, SEQ])
            pT = [part(10240, [3, 4, P]), part(4608, [3, 4, P])]
            small = part(11776, [120])
            gates = small[:, 0:48]
            nmax = small[:, 48:56]
            rs = small[:, 56:64]
            fac = small[:, 64:72]
            es = small[:, 72:80]
            cmax = small[:, 80:96]
            csum = small[:, 96:112]
            nmax2 = small[:, 112:120]

        od = Odd
        os_ = {name: sem("o_" + name) for name in (
            "read", "gate_mm", "gates_done", "pick_mm", "xc_done", "xc_hi_done", "xc_lo_done",
            "hid_done", "c2_mm", "c2_read", "cs_mm", "cs_in", "cs_exp", "pc_done", "pc_T", "pcT_done",
            "s_mm", "nmax_done", "p_exp", "p_done", "p_T", "pT_act", "pT_dve", "pv_mm")}

        class Cross:
            q = part(0, [KT, SEQ])
            p = part(2048, [XH, TT, MEM])
            pT = part(4096, [XH, 2, SEQ])
            small = part(6144, [32])
            nmax = small[:, 0:8]
            rs = small[:, 8:16]
            fac = small[:, 16:24]

        cr = Cross
        xs_ = {name: sem("x_" + name) for name in (
            "q_read", "s_mm", "nmax", "p_exp", "p_done", "p_T", "pT_done", "pv_mm")}
        OT_BASE = {"cross0": 0, "odd": 4, "cross1": 8}
        UNITS = [(0, 0), (1, 0), (0, 1), (1, 1), (2, 0), (2, 1)]
        PV_AFTER = [1, 3, 4, 5]

        def pv_before(u):
            return 1 if u < 4 else 2

        block = ctx.enter_context(nc.Block())

        def small_loads():
            rows = [d["ssm_dt_bias"][0], d["ssm_a_log"][0], d["ssm_d"][0], d["swa_sinks"][0]]
            loads = [(consts[:, :], d["consts"]), (masks_f, d["masks"]),
                     (dt_w[:, :, :], w_view(d["even_w_in"][0][:, EVEN_IN - SSM_H:EVEN_IN])),
                     (gate_w[:, :, :], w_view(d["odd_w_in"][0][:, 1280:1304])),
                     (w2[:, 0, :, :], d["nsa_cmp_w2"][0, 0].rearrange("(t p) c -> p t c", p=P)),
                     (w2[:, 1, :, :], d["nsa_cmp_w2"][0, 1].rearrange("(t p) c -> p t c", p=P)),
                     (ssm_nw[:, :], d["ssm_norm_w"][0].partition_broadcast(P))]
            loads += [(head_rows[:, i, :], r.partition_broadcast(P)) for i, r in enumerate(rows)]
            return loads

        def strided_loads():
            loads = [(conv_b[:, :], d["ssm_conv_b"][0].rearrange("(t p) -> p t", p=P))]
            loads += [(conv_w[:, w, :], d["ssm_conv_w"][0, w].rearrange("(t p) -> p t", p=P))
                      for w in range(CONV_W)]
            loads += [(pe_pairs[:, kv, :], d["nsa_cmp_pe"][0, kv].rearrange("(i r) c -> (r c) i", r=2))
                      for kv in range(2)]
            return loads

        SMALL = 16 * (len(small_loads()) + len(strided_loads()))

        @block.sync
        def _(sp):
            def load(n, dst_view, src):
                if n >= RING:
                    sp.wait_ge(lo_done, n - RING + 1)
                sp.dma_start(dst_view, src).then_inc(raw_in[n % RING], 16)

            def named_chunks(first, last):
                for n in range(first, last):
                    if n >= RING:
                        sp.wait_ge(lo_done, n - RING + 1)
                    for (kind, arg), src in pieces_of(named[n]):
                        dst = slot_k(n, arg) if kind == "k" else slot_k(n, CW)[:, :, arg:arg + HD]
                        sp.dma_start(dst, src).then_inc(raw_in[n % RING], 16)

            def ffn(layer, which):
                base = at["ffn", layer, which]
                gate, up = (d[w][layer, which].rearrange("(k p) (j c) -> j p k c", p=P, c=CW)
                            for w in ("ffn_w_gate", "ffn_w_up"))
                down = d["ffn_w_down"][layer, which].rearrange("(j k p) c -> j p k c", k=2, p=P)
                load(base, slot_k(base, CW), gate[0])
                load(base + 1, slot_k(base + 1, CW), up[0])
                with sp.Fori(0, FJ - 1) as j:
                    for c, (w, width, row) in enumerate(((gate, CW, j + 1), (up, CW, j + 1), (down, D, j))):
                        n = base + 2 + c
                        sp.wait_ge(lo_done, j * 3 + (n - RING + 1))
                        sp.dma_start(slot_k(n, width), w[bass.ds(row, 1)].rearrange("a p k c -> (a p) k c"))\
                          .then_inc(raw_in[n % RING], 16)
                n = base + FFN_CHUNKS - 1
                load(n, slot_k(n, D), down[FJ - 1])

            sp.dma_start(mem_rows, d["mem"][0].rearrange("(t p) c -> p t c", p=P)).then_inc(rows_in, 16)
            sp.dma_start(x[:, :, :], d["x"][0].rearrange("(t p) c -> p t c", p=P)).then_inc(rows_in, 16)
            ffn(0, 0)
            named_chunks(at["ffn", 0, 0] + FFN_CHUNKS, at["ffn", 0, 1])
            ffn(0, 1)
            ffn(1, 0)
            named_chunks(at["ffn", 1, 0] + FFN_CHUNKS, at["ffn", 1, 1])
            ffn(1, 1)
            for t in range(TT):
                sp.wait_ge(xn_done, 2 * 9 + t + 1)
                sp.dma_start(out[0, t * P:(t + 1) * P, :], xn[:, t, :]).then_inc(out_sent, 16)
            sp.wait_ge(out_sent, 16 * TT)

        @block.scalar
        def _(act):
            made, steps = [0], [0]

            def step(ins):
                steps[0] += 1
                ins.then_inc(act_step, 1)
                act.wait_ge(act_step, steps[0])

            def hi_upto(limit):
                for n in range(made[0], min(limit, n_chunks)):
                    act.wait_ge(raw_in[n % RING], landed(n))
                    if n >= RING:
                        act.wait_ge(chunks_used, n - RING + 1)
                    nc.scalar.activation(w_hi[:, n % RING, :], raw[:, n % RING, :], ACT.Copy).then_inc(hi_done, 1)
                    made[0] = n + 1

            def squares(v, src, ready):
                for t in range(TT):
                    ready(t)
                    if 2 * v + t >= 1:
                        act.wait_ge(sq_done, 2 * v + t)
                    nc.scalar.activation(xn[:, t, :], src[:, t, :], ACT.Square,
                                         accum_out=ssq[:, t:t + 1]).then_inc(sq_done, 1)

            def evac_hi(w, dst):
                for t in range(TT):
                    for kh in range(2):
                        act.wait_ge(transposed, 4 * w + 2 * t + kh + 1)
                        nc.scalar.activation(dst[:, 4 * kh:4 * kh + 4, t * P:(t + 1) * P],
                                             ps[:, 2 * t + kh, :].rearrange("p (k c) -> p k c", c=P),
                                             ACT.Copy).then_inc(hT_hi_done, 1)

            def norm(layer, i):
                v = norm_no(layer, i)

                def ready(t):
                    if v == 1:
                        act.wait_ge(rows_in, 32)
                        if t == 0:
                            act.wait_ge(transposed, 4)
                    else:
                        act.wait_ge(x_added, 4 * (v - 2) + 2 * t + 2)
                squares(v, x, ready)
                evac_hi(SETS["norm", layer, i], hT_hi)

            def kv_chunk(layer, i):
                act.wait_ge(chunks_used, at["kv", layer, i] + 1)
                pv = ps[:, 3, :].rearrange("p (a c) -> p a c", a=2)
                dst = xk[:, 2 * i:2 * i + 2, :] if i < 4 else xv[:, :, (i - 4) * CW:(i - 3) * CW]
                nc.scalar.activation(dst, pv, ACT.Copy).then_inc(kv_read, 1)
                hi_upto(at["kv", layer, i] + 4)

            def ffn(layer, which):
                f, base = 2 * layer + which, at["ffn", layer, which]

                def silu(j, cell):
                    act.wait_ge(chunks_used, j * 3 + cell)
                    nc.scalar.activation(g_act, ps[:, 0, :], ACT.Silu).then_inc(silu_done, 1)

                def hidden(count, used):
                    act.wait_ge(mult_done, count)
                    act.wait_ge(chunks_used, used)
                    nc.scalar.activation(gu_hi, gu.rearrange("p (k c) -> p k c", k=2),
                                         ACT.Copy).then_inc(gu_hi_done, 1)

                hi_upto(base + 3)
                silu(0, base + 1)
                hi_upto(base + 5)
                hidden(f * FJ + 1, base + 1)
                last = base + FFN_CHUNKS == n_chunks
                turns = FJ - 2 if last else FJ - 1
                with act.Fori(1, turns + 1) as j:
                    for c in range(3):
                        n = base + 2 + c
                        if c == 0:
                            act.wait_ge(mult_done, j + f * FJ)
                            silu(j, base)
                        if c == 2:
                            hidden(j + (f * FJ + 1), j * 3 + (base + 2))
                        m = n + RING
                        act.wait_ge(raw_in[m % RING], (j - 1) * 16 + landed(m))
                        act.wait_ge(chunks_used, (j - 1) * 3 + (m - RING + 1))
                        nc.scalar.activation(w_hi[:, m % RING, :], raw[:, m % RING, :], ACT.Copy).then_inc(hi_done, 1)
                made[0] = base + 2 + 3 * turns + 3
                if last:
                    j = FJ - 1
                    act.wait_ge(mult_done, j + f * FJ)
                    silu(j, base)
                    hi_upto(n_chunks)
                    hidden(j + f * FJ + 1, j * 3 + base + 2)

            def cross(layer):
                u = 4 * layer
                wq, wo = at["wq", layer, 0], at["wo", layer, 0]
                for i in range(4):
                    act.wait_ge(chunks_used, wq + i + 1)
                    nc.scalar.activation(cr.q[:, 2 * i:2 * i + 2, :],
                                         ps[:, i % 3, :].rearrange("p (a c) -> p a c", a=2),
                                         ACT.Copy, scale=XD ** -0.5).then_inc(xs_["q_read"], 1)
                    if i < 3:
                        hi_upto(wq + i + 4)
                for h in range(XH):
                    act.wait_ge(xs_["nmax"], u + h + 1)
                    for t in range(TT):
                        ins = nc.scalar.activation(cr.p[:, h, t, :], ps[:, 4 + h, t * MEM:(t + 1) * MEM],
                                                   ACT.Exp, bias=cr.nmax[:, 2 * h + t:2 * h + t + 1],
                                                   accum_out=cr.rs[:, 2 * h + t:2 * h + t + 1])
                        ins.then_inc(xs_["p_exp"], 1)
                    if h >= 1:
                        probs_out(u, h - 1)
                probs_out(u, XH - 1)
                for h in range(XH):
                    act.wait_ge(xs_["pv_mm"], u + h + 1)
                    nc.scalar.activation(hT_hi[:, 2 * h:2 * h + 2, :],
                                         ps[:, 4 + h, :].rearrange("p (a c) -> p a c", a=2),
                                         ACT.Copy).then_inc(oT_hi_done, 1)
                hi_upto(wq + 4 + 3)
                for i in range(4):
                    hi_upto(wo + i + 4)

            def probs_out(u, h):
                act.wait_ge(xs_["p_T"], u + h + 1)
                nc.scalar.activation(cr.pT[:, h, :, :], ps[:, (3, 1, 2, 3)[h], :].rearrange("p (a c) -> p a c", a=2),
                                     ACT.Copy).then_inc(xs_["pT_done"], 1)

            def even():
                E = at["even", "x0"]
                for c in range(3):
                    act.wait_ge(chunks_used, E + c + 1)
                    if c == 0:
                        act.wait_ge(es["xpad_zero"], 1)
                    nc.scalar.activation(ev.xpad[:, 2 * c:2 * c + 2, CONV_W - 1:],
                                         ps[:, c, :].rearrange("p (a c) -> p a c", a=2),
                                         ACT.Copy)
                    for m in range(2):
                        k = 2 * c + m
                        ins = nc.scalar.activation(ev.xbcT[:, k, :], ps[:, c, m * SEQ:(m + 1) * SEQ], ACT.Identity,
                                                   bias=conv_b[:, k:k + 1], scale=conv_w[:, CONV_W - 1, k:k + 1])
                    ins.then_inc(es["act_read"], 1)
                    hi_upto(E + c + 4)
                    if c:
                        conv_silu(c - 1)
                conv_silu(2)
                act.wait_ge(es["dt_raw"], 1)
                step(nc.scalar.activation(ev.ln1p, ev.dtr, ACT.Abs))
                step(nc.scalar.activation(ev.ln1p, ev.ln1p, ACT.Exp, scale=-1.0))
                nc.scalar.activation(ev.ea, head_rows[:, 1, :], ACT.Exp).then_inc(es["ea_done"], 1)
                nc.scalar.activation(ev.ln1p, ev.ln1p, ACT.Ln, bias=1.0).then_inc(es["ln_done"], 1)
                for e in range(3, 7):
                    hi_upto(E + e + 4)
                for t in range(TT):
                    act.wait_ge(es["xs_T"], t + 1)
                    nc.scalar.activation(ev.xh[:, t, :, :], ps[:, 4 + t, :].rearrange("p (h c) -> p h c", h=SSM_H),
                                         ACT.Copy).then_inc(es["xh_done"], 1)
                act.wait_ge(es["xs_T"], 3)
                nc.scalar.activation(ev.b_tok, ps[:, 3, 0:P], ACT.Copy).then_inc(es["xh_done"], 1)
                for i, e in enumerate((7, 8)):
                    act.wait_ge(chunks_used, E + e + 1)
                    nc.scalar.activation(ev.v[:, :, i * CW:(i + 1) * CW],
                                         ps[:, e % 3, :].rearrange("p (a c) -> p a c", a=2),
                                         ACT.Copy).then_inc(es["act_read"], 1)
                    hi_upto(E + e + 4)
                act.wait_ge(es["dec_mm"], 1)
                nc.scalar.activation(ev.small[:, 72:88], ps[:, 3, P:P + 16], ACT.Exp).then_inc(es["dec_done"], 1)
                for q in range(4):
                    act.wait_ge(es["seg_mm"], q + 1)
                    nc.scalar.activation(ev.mt[:, q // 2, 4 * (q % 2):4 * (q % 2) + 4, :],
                                         ps[:, 4 + q, :].rearrange("p (a c) -> p a c", a=4),
                                         ACT.Exp).then_inc(es["seg_exp"], 1)
                for i, e in enumerate((9, 10)):
                    act.wait_ge(chunks_used, E + e + 1)
                    nc.scalar.activation(xn[:, :, i * CW:(i + 1) * CW],
                                         ps[:, e % 3, :].rearrange("p (a c) -> p a c", a=2),
                                         ACT.Silu).then_inc(es["act_read"], 1)
                    hi_upto(E + e + 4)
                for i, dst in enumerate((ev.qT, ev.kT)):
                    for t in range(TT):
                        act.wait_ge(es["qk_T"], 2 * i + t + 1)
                        nc.scalar.activation(dst[:, t, :, :], ps[:, 4 + 2 * i + t, :].rearrange("p (a c) -> p a c", a=4),
                                             ACT.Copy).then_inc(es["qkT_done"], 1)
                for i, e in enumerate((11, 12)):
                    act.wait_ge(chunks_used, E + e + 1)
                    nc.scalar.activation(xn[:, :, 512 + i * CW:512 + (i + 1) * CW],
                                         ps[:, e % 3, :].rearrange("p (a c) -> p a c", a=2),
                                         ACT.Silu).then_inc(es["act_read"], 1)
                    hi_upto(E + e + 4)
                act.wait_ge(es["st_mm"], 1)
                nc.scalar.activation(ev.sT, ps[:, 6, :], ACT.Copy).then_inc(es["st_done"], 1)
                kv_chunk(0, 0)
                act.wait_ge(es["ret_kv_mm"], 1)
                nc.scalar.activation(ev.kv, ps[:, 6, :].rearrange("p (a c) -> p a c", a=4),
                                     ACT.Copy).then_inc(es["kvs_done"], 1)
                kv_chunk(0, 1)
                for t in range(TT):
                    act.wait_ge(es["y_ready"], t + 1)
                    nc.scalar.activation(ev.xdt[:, t, :, :], ev.xh[:, t, :, :], ACT.Square,
                                         accum_out=ev.ssr[:, t:t + 1]).then_inc(es["y_sq"], 1)
                kv_chunk(0, 2)
                act.wait_ge(es["o_read"], 1)
                act.wait_ge(es["y_read"], 1)
                nc.scalar.activation(ev.mt[:, :, 0:4, :], ev.o, ACT.Square).then_inc(es["o_sq"], 1)
                kv_chunk(0, 3)
                act.wait_ge(es["o_ssq"], 1)
                for i in range(4, 8):
                    kv_chunk(0, i)
                evac_hi(SETS["mix0"], hT_hi)

            def conv_silu(c):
                act.wait_ge(es["conv_done"], c + 1)
                nc.scalar.activation(ev.xbcT[:, 2 * c:2 * c + 2, :], ev.xbcT[:, 2 * c:2 * c + 2, :],
                                     ACT.Silu).then_inc(es["xbc_done"], 1)

            def odd():
                O = at["odd", ODD_ORDER[0]]
                for c, name in enumerate(ODD_ORDER):
                    act.wait_ge(chunks_used, O + c + 1)
                    bank = ps[:, c % 3, :].rearrange("p (a c) -> p a c", a=2)
                    if name[0] == "q":
                        dst = od.qn if name[1] == "n" else od.qs
                        m = 2 * int(name[2])
                        nc.scalar.activation(dst[:, m:m + 2, :], bank, ACT.Copy, scale=HD ** -0.5)\
                          .then_inc(os_["read"], 1)
                    elif name == "c":
                        nc.scalar.activation(od.kc, bank, ACT.Copy).then_inc(os_["read"], 1)
                    else:
                        j = "swa".index(name)
                        nc.scalar.activation(od.kT[:, j, :], bank[:, 0, :], ACT.Copy)
                        nc.scalar.activation(od.v[:, j, :, :], bank[:, 1, :].rearrange("p (a c) -> p a c", a=2),
                                             ACT.Copy).then_inc(os_["read"], 1)
                    hi_upto(O + c + 4)
                    if c == 5:
                        act.wait_ge(os_["xc_done"], 1)
                        nc.scalar.activation(od.xc_hi, od.xc.rearrange("p k i g n -> p k i (g n)"), ACT.Copy)\
                          .then_inc(os_["xc_hi_done"], 1)
                act.wait_ge(os_["gate_mm"], 1)
                nc.scalar.activation(od.gates, ps[:, 3, 0:48], ACT.Exp, scale=-1.0).then_inc(os_["gates_done"], 1)
                C = at["cmp", 0]
                hi_upto(C + 4 + 3)
                act.wait_ge(chunks_used, C + 4)
                for ht in range(2):
                    ins = nc.scalar.activation(od.hid[:, :, ht, :],
                                               ps[:, 5 + ht, 0:64].rearrange("p (k c) -> p k c", k=2)[:, :, 0:30],
                                               ACT.Silu)
                ins.then_inc(os_["hid_done"], 1)
                act.wait_ge(os_["c2_mm"], 1)
                nc.scalar.activation(od.kcT[:, 0:N_CMP], ps[:, 7, 0:N_CMP], ACT.Copy)
                nc.scalar.activation(od.vc[0:N_CMP, :, :], ps[0:N_CMP, 7, 64:192].rearrange("p (g c) -> p g c", g=2),
                                     ACT.Copy).then_inc(os_["c2_read"], 1)
                kv_chunk(1, 0)
                act.wait_ge(os_["cs_in"], 1)
                nc.scalar.activation(od.pc, od.pc, ACT.Exp).then_inc(os_["cs_exp"], 1)
                kv_chunk(1, 1)
                fillers = iter(range(2, 8))
                unit_exp(0)
                for b in range(4):
                    act.wait_ge(os_["pc_T"], b + 1)
                    nc.scalar.activation(od.pcT[0:N_CMP, 2 * b:2 * b + 2, :],
                                         ps[0:N_CMP, 4 + b, :].rearrange("p (h c) -> p h c", h=2),
                                         ACT.Copy).then_inc(os_["pcT_done"], 1)
                for u in range(6):
                    for b in range(2):
                        act.wait_ge(os_["p_T"], 3 * u + b + 1)
                        if b == 0 and u >= 2:
                            act.wait_ge(os_["pv_mm"], pv_before(u))
                        nc.scalar.activation(od.pT[u % 2][:, b, :, :], ps[:, 4 + b, :].rearrange("p (h c) -> p h c", h=4),
                                             ACT.Copy).then_inc(os_["pT_act"], 1)
                    if u < 5:
                        unit_exp(u + 1)
                    kv_chunk(1, next(fillers))
                    if u in PV_AFTER:
                        r = PV_AFTER.index(u)
                        act.wait_ge(os_["pv_mm"], r + 1)
                        nc.scalar.activation(hT_hi[:, 2 * r:2 * r + 2, :],
                                             ps[:, 7, :].rearrange("p (a c) -> p a c", a=2),
                                             ACT.Copy).then_inc(oT_hi_done, 1)

            def unit_exp(u):
                act.wait_ge(os_["nmax_done"], u + 1)
                if u >= 1:
                    act.wait_ge(os_["p_T"], 3 * u)
                for h in range(4):
                    nc.scalar.activation(od.p0[:, h, :], ps[:, 0, h * P:(h + 1) * P], ACT.Exp,
                                         bias=od.nmax[:, h:h + 1],
                                         accum_out=od.rs[:, h:h + 1])
                for h in range(4):
                    ins = nc.scalar.activation(od.p1[:, h, :], ps[:, 1 + h // 2, (h % 2) * SEQ:(h % 2 + 1) * SEQ],
                                               ACT.Exp, bias=od.nmax[:, 4 + h:5 + h],
                                               accum_out=od.rs[:, 4 + h:5 + h])
                if u >= 4:
                    ins = nc.scalar.activation(od.es, od.es, ACT.Exp)
                ins.then_inc(os_["p_exp"], 1)

            for dst, src in small_loads():
                act.dma_start(dst, src).then_inc(small_in, 16)
            with nc.allow_non_contiguous_dma(reason="a few KB of per-channel columns"):
                for dst, src in strided_loads():
                    act.dma_start(dst, src).then_inc(small_in, 16)
            hi_upto(2)
            act.wait_ge(rows_in, 32)
            squares(0, mem_rows, lambda t: None)
            act.wait_ge(small_in, SMALL)
            nc.scalar.activation(dt_w_hi[:, :, :], dt_w[:, :, :], ACT.Copy)
            nc.scalar.activation(gate_w_hi[:, :, :], gate_w[:, :, :], ACT.Copy)
            nc.scalar.activation(masks[:, :], masks_f, ACT.Copy).then_inc(consts_made, 1)
            evac_hi(SETS["mem"], memT_hi)
            norm(0, 0)
            ffn(0, 0)
            norm(0, 1)
            hi_upto(at["even", "x0"] + 3)
            even()
            hi_upto(at["wq", 0, 0] + 3)
            norm(0, 2)
            cross(0)
            norm(0, 3)
            ffn(0, 1)
            norm(1, 0)
            ffn(1, 0)
            norm(1, 1)
            hi_upto(at["odd", ODD_ORDER[0]] + 3)
            odd()
            hi_upto(at["wq", 1, 0] + 3)
            norm(1, 2)
            cross(1)
            norm(1, 3)
            ffn(1, 1)
            squares(9, x, lambda t: act.wait_ge(x_added, 4 * 7 + 2 * t + 2))

        @block.vector
        def _(dve):
            made, steps = [0], [0]
            V = nc.vector

            def step(ins):
                steps[0] += 1
                ins.then_inc(dve_step, 1)
                dve.wait_ge(dve_step, steps[0])

            def lo_upto(limit):
                for n in range(made[0], min(limit, n_chunks)):
                    dve.wait_ge(hi_done, n + 1)
                    V.tensor_tensor(w_lo[:, n % RING, :], raw[:, n % RING, :],
                                    w_hi[:, n % RING, :].bitcast(F32), ALU.subtract).then_inc(lo_done, 1)
                    made[0] = n + 1

            def norm_rows(v, src):
                for t in range(TT):
                    if t == 0:
                        dve.wait_ge(norm_w_in, 16 * (v + 1))
                    dve.wait_ge(rstd_done, 2 * v + t + 1)
                    V.scalar_tensor_tensor(xn[:, t, :], src[:, t, :], rstd[:, t:t + 1], norm_w[:, :],
                                           ALU.mult, ALU.mult).then_inc(xn_done, 1)

            def evac_lo(w, hi, lo):
                for t in range(TT):
                    for kh in range(2):
                        dve.wait_ge(hT_hi_done, 4 * w + 2 * t + kh + 1)
                        ks, ts = slice(4 * kh, 4 * kh + 4), slice(t * P, (t + 1) * P)
                        V.tensor_tensor(lo[:, ks, ts], ps[:, 2 * t + kh, :].rearrange("p (k c) -> p k c", c=P),
                                        hi[:, ks, ts].bitcast(F32), ALU.subtract).then_inc(hT_done, 1)

            def norm(layer, i):
                norm_rows(norm_no(layer, i), x)
                evac_lo(SETS["norm", layer, i], hT_hi, hT_lo)

            def oT_lo(count, k0, bank):
                dve.wait_ge(oT_hi_done, count)
                V.tensor_tensor(hT_lo[:, k0:k0 + 2, :], ps[:, bank, :].rearrange("p (a c) -> p a c", a=2),
                                hT_hi[:, k0:k0 + 2, :].bitcast(F32), ALU.subtract).then_inc(oT_done, 1)

            def add_residual(last_chunk, coef):
                dve.wait_ge(chunks_used, last_chunk + 1)
                for t in range(TT):
                    for h in range(2):
                        xs = x[:, t, h * 512:(h + 1) * 512]
                        V.scalar_tensor_tensor(xs, ps[:, 4 + 2 * t + h, :], coef, xs,
                                               ALU.mult, ALU.add).then_inc(x_added, 1)

            def ffn(layer, which):
                f, base = 2 * layer + which, at["ffn", layer, which]

                def product(j, used):
                    dve.wait_ge(silu_done, j + (f * FJ + 1))
                    dve.wait_ge(chunks_used, used)
                    V.tensor_tensor(gu, g_act, ps[:, 1, :], ALU.mult).then_inc(mult_done, 1)

                def hidden_lo(j):
                    dve.wait_ge(gu_hi_done, j + (f * FJ + 1))
                    V.tensor_tensor(gu_lo, gu.rearrange("p (k c) -> p k c", k=2), gu_hi.bitcast(F32),
                                    ALU.subtract).then_inc(gu_done, 1)

                lo_upto(base + 4)
                product(0, base + 2)
                lo_upto(base + 5)
                hidden_lo(0)
                last = base + FFN_CHUNKS == n_chunks
                turns = FJ - 2 if last else FJ - 1
                with dve.Fori(1, turns + 1) as j:
                    for c in range(3):
                        m = base + 2 + c + RING
                        if c == 1:
                            dve.wait_ge(gu_done, j + f * FJ)
                            product(j, j * 3 + (base + 1))
                        if c == 2:
                            hidden_lo(j)
                        dve.wait_ge(hi_done, (j - 1) * 3 + (m + 1))
                        V.tensor_tensor(w_lo[:, m % RING, :], raw[:, m % RING, :],
                                        w_hi[:, m % RING, :].bitcast(F32), ALU.subtract).then_inc(lo_done, 1)
                made[0] = base + 2 + 3 * turns + 3
                if last:
                    j = FJ - 1
                    dve.wait_ge(gu_done, j + f * FJ)
                    product(j, j * 3 + base + 1)
                    lo_upto(n_chunks)
                    hidden_lo(j)
                add_residual(base + FFN_CHUNKS - 1, 0.5)

            def cross(layer):
                u = 4 * layer
                wq, wo = at["wq", layer, 0], at["wo", layer, 0]
                for i in range(3):
                    lo_upto(wq + i + 4)
                for h in range(XH):
                    dve.wait_ge(xs_["s_mm"], u + h + 1)
                    V.tensor_reduce(cr.nmax[:, 2 * h:2 * h + 2], ps[:, 4 + h, :].rearrange("p (t c) -> p t c", t=2),
                                    axis=AX.X, op=ALU.max, negate=True).then_inc(xs_["nmax"], 1)
                for h in range(XH):
                    dve.wait_ge(xs_["p_exp"], 2 * (u + h + 1))
                    step(V.reciprocal(cr.fac[:, 2 * h:2 * h + 2], cr.rs[:, 2 * h:2 * h + 2]))
                    V.tensor_tensor(cr.p[:, h, :, :], cr.p[:, h, :, :],
                                    cr.fac[:, 2 * h:2 * h + 2].unsqueeze(2).to_broadcast([P, 2, MEM]),
                                    ALU.mult).then_inc(xs_["p_done"], 1)
                for h in range(XH):
                    oT_lo(OT_BASE[f"cross{layer}"] + h + 1, 2 * h, 4 + h)
                for i in range(-1, 4):
                    lo_upto(wo + i + 4)
                add_residual(wo + 3, 1.0)

            def rotate(e, i):
                E = at["even", "x0"]
                dve.wait_ge(chunks_used, E + e + 1)
                if i:
                    dve.wait_ge(es["rot_done"], i)
                pair = ps[:, e % 3, :].rearrange("p (t h i two) -> p t h i two", t=TT, h=2, two=2)
                cosr, sinr = const("cos", TT, 64), const("sin", TT, 64)
                for t in range(TT):
                    c, s = (v[:, t, :].unsqueeze(1).to_broadcast([P, 2, 64]) for v in (cosr, sinr))
                    for r, (which, table) in enumerate(((0, c), (1, s), (0, s), (1, c))):
                        ins = V.tensor_tensor(ev.rot[r][:, t, :, :],
                                              pair[:, t, :, :, which], table, ALU.mult)
                ins.then_inc(es["rot_read"], 1)

            def even():
                E = at["even", "x0"]
                for c in range(3):
                    dve.wait_ge(es["act_read"], c + 1)
                    for tap in (2, 1, 0):
                        for m in range(2):
                            k = 2 * c + m
                            ins = V.scalar_tensor_tensor(ev.xbcT[:, k, :], ev.xpad[:, k, tap:tap + SEQ],
                                                         conv_w[:, tap, k:k + 1], ev.xbcT[:, k, :],
                                                         ALU.mult, ALU.add)
                            if tap:
                                if m:
                                    step(ins)
                            elif m:
                                ins.then_inc(es["conv_done"], 1)
                    lo_upto(E + c + 4)
                dve.wait_ge(es["dt_mm"], 1)
                V.tensor_tensor(ev.dtr.rearrange("p (t h) -> p t h", t=TT),
                                ps[:, 3, 0:16].rearrange("p (t h) -> p t h", t=TT),
                                head_rows[:, 0, :].unsqueeze(1).to_broadcast([P, TT, SSM_H]),
                                ALU.add).then_inc(es["dt_raw"], 1)
                dve.wait_ge(es["ln_done"], 1)
                step(V.scalar_tensor_tensor(ev.dt, ev.dtr, 0.0, ev.ln1p, ALU.max, ALU.add))
                dve.wait_ge(es["ea_done"], 1)
                V.scalar_tensor_tensor(ev.dta.rearrange("p (t h) -> p t h", t=TT),
                                       ev.dt.rearrange("p (t h) -> p t h", t=TT), -1.0,
                                       ev.ea.unsqueeze(1).to_broadcast([P, TT, SSM_H]),
                                       ALU.mult, ALU.mult).then_inc(es["dta_done"], 1)
                for i in range(4):
                    rotate(3 + i, i)
                    lo_upto(E + 3 + i + 4)
                dve.wait_ge(es["xh_done"], TT)
                dve.wait_ge(es["rot_done"], 4)
                V.tensor_tensor(ev.xdt.rearrange("p t h c -> p (t h) c"), ev.xh.rearrange("p t h c -> p (t h) c"),
                                ev.dt.unsqueeze(2).to_broadcast([P, TT * SSM_H, HP]),
                                ALU.mult).then_inc(es["xdt_done"], 1)
                lo_upto(E + 7 + 4)
                for g in range(2):
                    dve.wait_ge(es["cb_mm"], g + 1)
                    V.tensor_tensor(ev.cbm[:, :, g, :], ps[:, 6 + g, 0:2 * P].rearrange("p (c l) -> p c l", c=TT),
                                    const("upto").unsqueeze(1).to_broadcast([P, TT, P]),
                                    ALU.mult).then_inc(es["cbm_done"], 1)
                lo_upto(E + 8 + 4)
                for q in range(4):
                    dve.wait_ge(es["seg_exp"], q + 1)
                    m = ev.mt[:, q // 2, 4 * (q % 2):4 * (q % 2) + 4, :]
                    V.tensor_tensor(m, m, ev.cbm[:, q // 2, q % 2, :].unsqueeze(1).to_broadcast([P, 4, P]),
                                    ALU.mult).then_inc(es["mt_done"], 1)
                dve.wait_ge(es["dec_done"], 1)
                V.tensor_tensor(ev.xdtd, ev.xdt[:, 0, :, :], ev.dec.unsqueeze(2).to_broadcast([P, SSM_H, HP]),
                                ALU.mult).then_inc(es["xdtd_done"], 1)
                for e in range(9, 13):
                    lo_upto(E + e + 4)
                dve.wait_ge(es["qkT_done"], 4)
                dve.wait_ge(es["kz_done"], 1)
                for t, bank in enumerate((7, 1)):
                    dve.wait_ge(es["ret_s_mm"], t + 1)
                    V.tensor_tensor(ev.s[:, t, :, :], ps[:, bank, :].rearrange("p (h i) -> p h i", h=RET_H),
                                    const("decayT", RET_H, P), ALU.mult).then_inc(es["s_done"], 1)
                dve.wait_ge(es["dx_done"], 1)
                hc = "p (h c) -> p h c"
                dve.wait_ge(es["y_mm"], 1)
                step(V.tensor_tensor(ev.xh[:, 0, :, :], ev.xh[:, 0, :, :], ps[:, 4, :].rearrange(hc, h=SSM_H), ALU.add))
                dve.wait_ge(es["act_read"], 9)
                V.tensor_tensor(ev.xh[:, 0, :, :], ev.xh[:, 0, :, :], xn[:, 0, 512:].rearrange(hc, h=SSM_H),
                                ALU.mult).then_inc(es["y_ready"], 1)
                dve.wait_ge(es["y_mm"], 2)
                step(V.tensor_tensor(ev.xh[:, 1, :, :], ev.xh[:, 1, :, :], ps[:, 5, :].rearrange(hc, h=SSM_H), ALU.add))
                dve.wait_ge(es["yoff_mm"], 1)
                for g, bank in enumerate((0, 2)):
                    ins = V.tensor_tensor(ev.yc[:, 4 * g:4 * g + 4, :], ps[:, bank, 0:256].rearrange(hc, h=4),
                                          ev.cum[:, 4 * g:4 * g + 4].unsqueeze(2).to_broadcast([P, 4, HP]), ALU.mult)
                step(ins)
                step(V.tensor_tensor(ev.xh[:, 1, :, :], ev.xh[:, 1, :, :], ev.yc, ALU.add))
                V.tensor_tensor(ev.xh[:, 1, :, :], ev.xh[:, 1, :, :], xn[:, 1, 512:].rearrange(hc, h=SSM_H),
                                ALU.mult).then_inc(es["y_ready"], 1)
                lo_upto(at["kv", 0, 0] + 4)
                dve.wait_ge(es["o_mm"], 1)
                V.tensor_copy(ev.o[:, 0, :, :], ps[:, 7, :].rearrange("p (h e) -> p h e", h=RET_H))\
                 .then_inc(es["y_read"], 1)
                dve.wait_ge(es["o_mm"], 2)
                step(V.tensor_tensor(ev.o[:, 1, :, :], ps[:, 4, :].rearrange("p (h e) -> p h e", h=RET_H),
                                     const("xi").unsqueeze(2).to_broadcast([P, RET_H, P]), ALU.mult))
                V.tensor_tensor(ev.o[:, 1, :, :], ev.o[:, 1, :, :], ps[:, 1, :].rearrange("p (h e) -> p h e", h=RET_H),
                                ALU.add).then_inc(es["o_read"], 1)
                dve.wait_ge(es["o_sq"], 1)
                V.tensor_reduce(ev.osq.rearrange("p (t h) -> p t h", t=TT),
                                ev.mt[:, :, 0:4, :], axis=AX.X, op=ALU.add).then_inc(es["o_ssq"], 1)
                lo_upto(at["kv", 0, 1] + 4)
                dve.wait_ge(es["y_rstd"], 1)
                for t in range(TT):
                    V.scalar_tensor_tensor(xn[:, t, 512:], ev.xh[:, t, :, :].rearrange("p h c -> p (h c)"),
                                           ev.rsr[:, t:t + 1], ssm_nw[:, :], ALU.mult, ALU.mult)
                dve.wait_ge(es["o_rstd"], 1)
                for t in range(TT):
                    ins = V.tensor_tensor(ev.o[:, t, :, :], ev.o[:, t, :, :],
                                          ev.ors[:, 4 * t:4 * t + 4].unsqueeze(2).to_broadcast([P, RET_H, P]), ALU.mult)
                step(ins)
                for t in range(TT):
                    g = xn[:, t, 0:512]
                    V.tensor_tensor(g, g, ev.o[:, t, :, :].rearrange("p h e -> p (h e)"), ALU.mult)\
                     .then_inc(es["mix_done"], 1)
                for i in range(2, 8):
                    lo_upto(at["kv", 0, i] + 4)
                evac_lo(SETS["mix0"], hT_hi, hT_lo)
                for i in range(4):
                    lo_upto(at["mixout", 0, i] + 3)
                add_residual(at["mixout", 0, 3], 1.0)

            def odd():
                O = at["odd", ODD_ORDER[0]]
                for c in range(8):
                    lo_upto(O + c + 4)
                    if c == 5:
                        compress_in()
                C = at["cmp", 0]
                lo_upto(C + 4 + 3)
                dve.wait_ge(os_["gates_done"], 1)
                step(V.tensor_scalar(od.gates, od.gates, 1.0, None, ALU.add))
                step(V.reciprocal(od.gates, od.gates))
                cm, cb = const("cmpmask", TT, N_CMP), const("cmpbias", TT, N_CMP)
                dve.wait_ge(os_["cs_mm"], 1)
                for g in range(2):
                    for t in range(TT):
                        ins = V.tensor_tensor(od.pc[:, t, 4 * g:4 * g + 4, :],
                                              ps[:, 4 + g, t * 64:t * 64 + 60].rearrange("p (h n) -> p h n", h=4),
                                              cm[:, t, :].unsqueeze(1).to_broadcast([P, 4, N_CMP]), ALU.mult)
                step(ins)
                for t in range(TT):
                    ins = V.tensor_tensor(od.pc[:, t, :, :], od.pc[:, t, :, :],
                                          cb[:, t, :].unsqueeze(1).to_broadcast([P, NH, N_CMP]), ALU.add)
                step(ins)
                pcf = od.pc.rearrange("p t h n -> p (t h) n")
                step(V.tensor_reduce(od.cmax, pcf, axis=AX.X, op=ALU.max, negate=True))
                V.tensor_tensor(pcf, pcf, od.cmax.unsqueeze(2).to_broadcast([P, 16, N_CMP]), ALU.add)\
                 .then_inc(os_["cs_in"], 1)
                dve.wait_ge(os_["cs_exp"], 1)
                for t in range(TT):
                    ins = V.tensor_tensor(od.pc[:, t, :, :], od.pc[:, t, :, :],
                                          cm[:, t, :].unsqueeze(1).to_broadcast([P, NH, N_CMP]), ALU.mult)
                step(ins)
                step(V.tensor_reduce(od.csum, pcf, axis=AX.X, op=ALU.add))
                step(V.tensor_scalar(od.csum, od.csum, 1e-30, None, ALU.max))
                step(V.reciprocal(od.csum, od.csum))
                g3 = od.gates.rearrange("p (q b) -> p q b", b=3)
                step(V.tensor_tensor(od.csum, od.csum, g3[:, :, 0], ALU.mult))
                V.tensor_tensor(pcf, pcf, od.csum.unsqueeze(2).to_broadcast([P, 16, N_CMP]), ALU.mult)\
                 .then_inc(os_["pc_done"], 1)
                lo_upto(at["kv", 1, 0] + 4)
                lo_upto(at["kv", 1, 1] + 4)
                fillers = iter(range(2, 8))
                unit(0)
                for u in range(6):
                    dve.wait_ge(os_["p_T"], 3 * u + 3)
                    if u >= 2:
                        dve.wait_ge(os_["pv_mm"], pv_before(u))
                    V.tensor_copy(od.pT[u % 2][:, 2, :, :], ps[:, 6, :].rearrange("p (h c) -> p h c", h=4))\
                     .then_inc(os_["pT_dve"], 1)
                    if u < 5:
                        unit(u + 1)
                    lo_upto(at["kv", 1, next(fillers)] + 4)
                    if u in PV_AFTER:
                        r = PV_AFTER.index(u)
                        oT_lo(OT_BASE["odd"] + r + 1, 2 * r, 7)
                for i in range(4):
                    lo_upto(at["mixout", 1, i] + 3)
                add_residual(at["mixout", 1, 3], 1.0)

            def unit(u):
                a, g = UNITS[u]
                dve.wait_ge(os_["s_mm"], u + 1)
                V.tensor_reduce(od.nmax2[:, 0:4], ps[:, 0, :].rearrange("p (h c) -> p h c", h=4),
                                axis=AX.X, op=ALU.max, negate=True)
                ins = V.tensor_reduce(od.nmax2[:, 4:8], ps[:, 1:3, :].rearrange("p b (h c) -> p (b h) c", h=2),
                                      axis=AX.X, op=ALU.max, negate=True)
                step(ins)
                nm = od.nmax.rearrange("p (t h) -> p t h", t=TT)
                nm2 = od.nmax2.rearrange("p (t h) -> p t h", t=TT)
                if a == 2:
                    sink = head_rows[:, 3, 4 * g:4 * g + 4].unsqueeze(1).to_broadcast([P, TT, 4])
                    step(V.scalar_tensor_tensor(nm, sink, -1.0, nm2, ALU.mult, ALU.min))
                    V.tensor_tensor(od.es.rearrange("p (t h) -> p t h", t=TT), nm, sink, ALU.add)\
                     .then_inc(os_["nmax_done"], 1)
                else:
                    V.tensor_copy(od.nmax, od.nmax2).then_inc(os_["nmax_done"], 1)
                dve.wait_ge(os_["p_exp"], u + 1)
                if a == 2:
                    step(V.tensor_tensor(od.rs, od.rs, od.es, ALU.add))
                step(V.reciprocal(od.fac, od.rs))
                if a < 2:
                    gate = od.gates.rearrange("p (t h b) -> p t h b", t=TT, b=3)[:, :, 4 * g:4 * g + 4, 1 + a]
                    fac = od.fac.rearrange("p (t h) -> p t h", t=TT)
                    step(V.tensor_tensor(fac, fac, gate, ALU.mult))
                V.tensor_tensor(od.p0, od.p0, od.fac[:, 0:4].unsqueeze(2).to_broadcast([P, 4, P]), ALU.mult)
                V.tensor_tensor(od.p1, od.p1, od.fac[:, 4:8].unsqueeze(2).to_broadcast([P, 4, SEQ]),
                                ALU.mult).then_inc(os_["p_done"], 1)

            def compress_in():
                dve.wait_ge(os_["pick_mm"], 1)
                for kv in range(2):
                    pairs = ps[:, 4, kv * 256:(kv + 1) * 256].rearrange("p (g n i) -> p g n i", g=2, i=8)
                    for half in range(2):
                        for g in range(2):
                            ins = V.tensor_tensor(
                                od.xc[:, kv, 8 * half:8 * half + 8, g, :],
                                pairs[:, g, half:half + N_CMP, :].rearrange("p n i -> p i n"),
                                pe_pairs[:, kv, 8 * half:8 * half + 8].unsqueeze(2).to_broadcast([P, 8, N_CMP]),
                                ALU.add)
                ins.then_inc(os_["xc_done"], 1)
                dve.wait_ge(os_["xc_hi_done"], 1)
                V.tensor_tensor(od.xc_lo, od.xc.rearrange("p k i g n -> p k i (g n)"), od.xc_hi.bitcast(F32),
                                ALU.subtract).then_inc(os_["xc_lo_done"], 1)

            dve.wait_ge(consts_made, 1)
            V.tensor_tensor(dt_w_lo[:, :, :], dt_w[:, :, :], dt_w_hi[:, :, :].bitcast(F32), ALU.subtract)
            V.tensor_tensor(gate_w_lo[:, :, :], gate_w[:, :, :], gate_w_hi[:, :, :].bitcast(F32),
                            ALU.subtract).then_inc(smalls_split, 1)
            lo_upto(2)
            norm_rows(0, mem_rows)
            evac_lo(SETS["mem"], memT_hi, memT_lo)
            norm(0, 0)
            lo_upto(3)
            ffn(0, 0)
            norm(0, 1)
            lo_upto(at["even", "x0"] + 3)
            even()
            norm(0, 2)
            lo_upto(at["wq", 0, 0] + 3)
            cross(0)
            norm(0, 3)
            ffn(0, 1)
            norm(1, 0)
            ffn(1, 0)
            norm(1, 1)
            lo_upto(at["odd", ODD_ORDER[0]] + 3)
            odd()
            norm(1, 2)
            lo_upto(at["wq", 1, 0] + 3)
            cross(1)
            norm(1, 3)
            ffn(1, 1)
            norm_rows(9, x)

        @block.gpsimd
        def _(pool):
            G = nc.gpsimd
            steps = [0]

            def step(ins):
                steps[0] += 1
                ins.then_inc(pool_step, 1)
                pool.wait_ge(pool_step, steps[0])

            def load_norm_w(v):
                if v:
                    pool.wait_ge(xn_done, 2 * v)
                src = d["mem_norm_w"] if v == 0 else d["final_norm_w"] if v == 9 else \
                    d["norm_w"][(v - 1) // 4, (v - 1) % 4]
                pool.dma_start(norm_w[:, :], src.partition_broadcast(P)).then_inc(norm_w_in, 16)

            def inv_rms(dst, tmp, src, width, count):
                step(G.tensor_scalar(tmp, src, 1.0 / count, EPS, ALU.mult, ALU.add))
                return G.tensor_tensor(dst, tmp, neg_half[:, 0:width], ALU.pow)

            def norm(v):
                for t in range(TT):
                    pool.wait_ge(sq_done, 2 * v + t + 1)
                    inv_rms(rstd[:, t:t + 1], msq[:, t:t + 1], ssq[:, t:t + 1], 1, D).then_inc(rstd_done, 1)
                if v < 9:
                    load_norm_w(v + 1)

            def even():
                pool.wait_ge(x_added, 4)
                G.memset(ev.xpad[:, :, 0:CONV_W - 1], 0.0).then_inc(es["xpad_zero"], 1)
                for i in range(4):
                    pool.wait_ge(es["rot_read"], i + 1)
                    a, b, c, e = ev.rot
                    dst = ev.q_rot if i < 2 else ev.k_rot
                    for t in range(TT):
                        hs = slice(2 * (i % 2), 2 * (i % 2) + 2)
                        r = [v[:, t, :, :] for v in (a, b, c, e)]
                        G.tensor_tensor(dst[:, t, hs, 0, :], r[0], r[1], ALU.subtract)
                        ins = G.tensor_tensor(dst[:, t, hs, 1, :], r[2], r[3], ALU.add)
                    ins.then_inc(es["rot_done"], 1)
                    if i == 1:
                        seg_weights()
                pool.wait_ge(es["rot_done"], 4)
                G.tensor_tensor(ev.kz, ev.k_rot[:, 0, :, :, :].rearrange("p h a b -> p h (a b)"),
                                const("zeta").unsqueeze(2).to_broadcast([P, RET_H, P]),
                                ALU.mult).then_inc(es["kz_done"], 1)
                pool.wait_ge(es["xdt_done"], 1)
                G.tensor_tensor(ev.xh.rearrange("p t h c -> p t h c")[:, 0], ev.xh[:, 0],
                                head_rows[:, 2, :].unsqueeze(2).to_broadcast([P, SSM_H, HP]), ALU.mult)
                G.tensor_tensor(ev.xh[:, 1], ev.xh[:, 1],
                                head_rows[:, 2, :].unsqueeze(2).to_broadcast([P, SSM_H, HP]),
                                ALU.mult).then_inc(es["dx_done"], 1)
                pool.wait_ge(es["y_sq"], 2)
                inv_rms(ev.rsr, ev.msr, ev.ssr, 2, SSM_IN).then_inc(es["y_rstd"], 1)
                pool.wait_ge(es["o_ssq"], 1)
                inv_rms(ev.ors, ev.oms, ev.osq, 8, DK).then_inc(es["o_rstd"], 1)

            def seg_weights():
                pool.wait_ge(es["conv_done"], 3)
                pool.wait_ge(es["dta_done"], 1)
                for t in range(TT):
                    for h in range(SSM_H):
                        G.tensor_scalar(ev.ld[:, t, h, :], const("after"),
                                        ev.dta[:, 8 * t + h:8 * t + h + 1], None, ALU.mult)\
                         .then_inc(es["ld_done"], 1)

            load_norm_w(0)
            G.memset(neg_half[:, :], -0.5).then_inc(neg_half_set, 1)
            pool.wait_ge(neg_half_set, 1)
            norm(0)
            norm(1)
            norm(2)
            even()
            for v in range(3, 10):
                norm(v)

        @block.tensor
        def _(pe):
            mm = nc.tensor.matmul

            def product3(dst, l_hi, l_lo, r_hi, r_lo, start, stop):
                mm(dst, l_hi, r_hi, start=start, stop=False)
                mm(dst, l_hi, r_lo, start=False, stop=False)
                return mm(dst, l_lo, r_hi, start=False, stop=stop)

            def cols(w, n, k, width, lo, hi):
                return w[:, n % RING, k * width + lo:k * width + hi]

            def to_features(n, dst, a_hi, a_lo, tiles=2, col0=0):
                for m in range(tiles):
                    lo, hi = col0 + m * P, col0 + (m + 1) * P
                    for k in range(KT):
                        last = product3(dst[:, m * SEQ:(m + 1) * SEQ],
                                        cols(w_hi, n, k, CW, lo, hi), cols(w_lo, n, k, CW, lo, hi),
                                        a_hi[:, k, :], a_lo[:, k, :], k == 0, k == KT - 1)
                return last

            def to_tokens(n, dst, width, a_hi, a_lo, col0=0):
                for t in range(TT):
                    ts = slice(t * P, (t + 1) * P)
                    for k in range(KT):
                        last = product3(dst[:, t * width:(t + 1) * width], a_hi[:, k, ts], a_lo[:, k, ts],
                                        cols(w_hi, n, k, CW, col0, col0 + width),
                                        cols(w_lo, n, k, CW, col0, col0 + width), k == 0, k == KT - 1)
                return last

            def down(n, a_hi, a_lo, first, final):
                for k in range(2):
                    for t in range(TT):
                        ts = slice(t * P, (t + 1) * P)
                        for h in range(2):
                            last = product3(ps[:, 4 + 2 * t + h, :], a_hi[:, k, ts], a_lo[:, k, ts],
                                            cols(w_hi, n, k, D, h * 512, (h + 1) * 512),
                                            cols(w_lo, n, k, D, h * 512, (h + 1) * 512),
                                            first and k == 0, final and k == 1)
                return last

            def used(ins):
                return ins.then_inc(chunks_used, 1)

            def transposes(ready):
                for t in range(TT):
                    ready(t)
                    for kh in range(2):
                        for k in range(4):
                            c = (4 * kh + k) * P
                            last = nc.tensor.transpose(ps[:, 2 * t + kh, k * P:(k + 1) * P],
                                                       xn[:, t, c:c + P], ident)
                        last.then_inc(transposed, 1)

            def norm(v, key):
                transposes(lambda t: pe.wait_ge(xn_done, 2 * v + t + 1))
                if key is not None:
                    pe.wait_ge(hT_done, 4 * SETS[key] + 4)

            def ffn(layer, which):
                f, base = 2 * layer + which, at["ffn", layer, which]

                def hidden_down(j, n, first, final):
                    pe.wait_ge(gu_done, j)
                    used(down(n, gu_hi_all, gu_lo_all, first, final))

                gu_hi_all, gu_lo_all = gu_hi, gu_lo
                pe.wait_ge(lo_done, base + 1)
                used(to_features(base, ps[:, 0, :], hT_hi, hT_lo))
                pe.wait_ge(lo_done, base + 2)
                used(to_features(base + 1, ps[:, 1, :], hT_hi, hT_lo))

                def turn(j, first):
                    n = base + 2
                    pe.wait_ge(silu_done, j + f * FJ)
                    pe.wait_ge(lo_done, j * 3 + (n + 1 - 3))
                    used(to_features(n, ps[:, 0, :], hT_hi, hT_lo))
                    pe.wait_ge(mult_done, j + f * FJ)
                    pe.wait_ge(lo_done, j * 3 + (n + 2 - 3))
                    used(to_features(n + 1, ps[:, 1, :], hT_hi, hT_lo))
                    pe.wait_ge(lo_done, j * 3 + (n + 3 - 3))
                    hidden_down(j + f * FJ, n + 2, first, False)

                turn(1, True)
                with pe.Fori(2, FJ) as j:
                    turn(j, False)
                n = base + FFN_CHUNKS - 1
                pe.wait_ge(lo_done, n + 1)
                hidden_down((f + 1) * FJ, n, False, True)

            def kv_chunk(layer, i):
                n = at["kv", layer, i]
                pe.wait_ge(lo_done, n + 1)
                if layer or i:
                    pe.wait_ge(kv_read, 8 * layer + i)
                if i < 4:
                    used(to_features(n, ps[:, 3, :], memT_hi, memT_lo))
                else:
                    used(to_tokens(n, ps[:, 3, :], CW, memT_hi, memT_lo))

            def out_chunks(first_n, waits=None):
                for i in range(4):
                    if waits:
                        waits(i)
                    pe.wait_ge(lo_done, first_n + i + 1)
                    used(down(first_n + i, hT_hi[:, 2 * i:2 * i + 2, :], hT_lo[:, 2 * i:2 * i + 2, :],
                              i == 0, i == 3))

            def cross(layer):
                u = 4 * layer
                wq, wo = at["wq", layer, 0], at["wo", layer, 0]

                def project(i):
                    pe.wait_ge(lo_done, wq + i + 1)
                    if i == 3:
                        pe.wait_ge(xs_["q_read"], u + 1)
                    used(to_features(wq + i, ps[:, i % 3, :], hT_hi, hT_lo))

                def scores(h):
                    pe.wait_ge(xs_["q_read"], u + h + 1)
                    pe.wait_ge(kv_read, 8 * layer + 8)
                    for t in range(TT):
                        for k in range(2):
                            last = mm(ps[:, 4 + h, t * MEM:(t + 1) * MEM],
                                      cr.q[:, 2 * h + k, t * P:(t + 1) * P], xk[:, 2 * h + k, :],
                                      start=k == 0, stop=k == 1)
                    last.then_inc(xs_["s_mm"], 1)

                def turned(h):
                    pe.wait_ge(xs_["p_done"], u + h + 1)
                    pe.wait_ge(xs_["q_read"], u + 4)
                    if h == 3:
                        pe.wait_ge(xs_["pT_done"], u + 1)
                    bank = (3, 1, 2, 3)[h]
                    for kb in range(2):
                        for t in range(TT):
                            last = nc.tensor.transpose(ps[:, bank, kb * SEQ + t * P:kb * SEQ + (t + 1) * P],
                                                       cr.p[:, h, t, kb * P:(kb + 1) * P], ident)
                    last.then_inc(xs_["p_T"], 1)

                def values(h):
                    pe.wait_ge(xs_["pT_done"], u + h + 1)
                    for m in range(2):
                        for kb in range(2):
                            last = mm(ps[:, 4 + h, m * SEQ:(m + 1) * SEQ],
                                      xv[:, kb, h * XD + m * P:h * XD + (m + 1) * P], cr.pT[:, h, kb, :],
                                      start=kb == 0, stop=kb == 1)
                    last.then_inc(xs_["pv_mm"], 1)

                project(0)
                project(1)
                scores(0)
                project(2)
                scores(1)
                project(3)
                scores(2)
                scores(3)
                for h in range(XH):
                    turned(h)
                    if h:
                        values(h - 1)
                values(XH - 1)
                b = OT_BASE[f"cross{layer}"]
                pe.wait_ge(oT_done, b + 4)
                out_chunks(wo)

            def even():
                E = at["even", "x0"]

                def project(e, bank_free=None):
                    n = E + e
                    pe.wait_ge(lo_done, n + 1)
                    if bank_free:
                        pe.wait_ge(es[bank_free[0]], bank_free[1])
                    if e < 3:
                        used(to_features(n, ps[:, e % 3, :], hT_hi, hT_lo))
                    else:
                        used(to_tokens(n, ps[:, e % 3, :], CW, hT_hi, hT_lo))

                for e in range(3):
                    project(e)
                for t in range(TT):
                    ts = slice(t * P, (t + 1) * P)
                    for k in range(KT):
                        last = product3(ps[:, 3, 8 * t:8 * t + 8], hT_hi[:, k, ts], hT_lo[:, k, ts],
                                        dt_w_hi[:, k, :], dt_w_lo[:, k, :], k == 0, k == KT - 1)
                last.then_inc(es["dt_mm"], 1)
                project(3, ("act_read", 1))
                project(4, ("act_read", 2))
                project(5, ("act_read", 3))
                project(6, ("rot_read", 1))
                pe.wait_ge(es["xbc_done"], 3)
                pe.wait_ge(es["dt_raw"], 1)
                for t in range(TT):
                    for k in range(4):
                        last = nc.tensor.transpose(ps[:, 4 + t, k * P:(k + 1) * P],
                                                   ev.xbcT[:, k, t * P:(t + 1) * P], ident)
                    last.then_inc(es["xs_T"], 1)
                nc.tensor.transpose(ps[:, 3, 0:P], ev.xbcT[:, 4, 0:P], ident).then_inc(es["xs_T"], 1)
                for g in range(2):
                    gs = slice(64 * g, 64 * g + 64)
                    for c in range(TT):
                        cs = slice(c * P, (c + 1) * P)
                        last = mm(ps[:, 6 + g, cs], ev.xbcT[gs, 4, cs], ev.xbcT[gs, 5, cs], start=True, stop=True)
                    last.then_inc(es["cb_mm"], 1)
                project(7, ("rot_read", 2))
                pe.wait_ge(es["dta_done"], 1)
                pe.wait_ge(es["xh_done"], 3)
                mm(ps[:, 3, P:P + 8], const("after"), ev.dta[:, 0:8], start=True, stop=True)
                mm(ps[:, 3, P + 8:P + 16], const("upto"), ev.dta[:, 8:16], start=True, stop=True)\
                    .then_inc(es["dec_mm"], 1)
                for q in range(4):
                    pe.wait_ge(es["ld_done"], 4 * q + 4)
                    if q == 2:
                        pe.wait_ge(es["cbm_done"], 2)
                    for h in range(4):
                        last = mm(ps[:, 4 + q, h * P:(h + 1) * P], ev.ld[:, q // 2, 4 * (q % 2) + h, :],
                                  const("upto"), start=True, stop=True)
                    last.then_inc(es["seg_mm"], 1)
                project(8, ("rot_read", 3))
                project(9, ("rot_read", 4))
                project(10, ("act_read", 4))
                pe.wait_ge(es["rot_done"], 4)
                for i, src in enumerate((ev.q_rot, ev.k_rot)):
                    for t in range(TT):
                        pe.wait_ge(es["seg_exp"], 2 * i + t + 1)
                        for h in range(RET_H):
                            last = nc.tensor.transpose(ps[:, 4 + 2 * i + t, h * P:(h + 1) * P],
                                                       src[:, t, h, :, :].rearrange("p a b -> p (a b)"), ident)
                        last.then_inc(es["qk_T"], 1)
                project(11, ("act_read", 5))
                project(12, ("act_read", 6))
                for t in range(TT):
                    pe.wait_ge(es["mt_done"], 2 * t + 2)
                    pe.wait_ge(es["qkT_done"], t + 1)
                    for h in range(SSM_H):
                        last = mm(ps[:, 4 + t, h * HP:(h + 1) * HP], ev.mt[:, t, h, :], ev.xdt[:, t, h, :],
                                  start=True, stop=True)
                    last.then_inc(es["y_mm"], 1)
                pe.wait_ge(es["xdtd_done"], 1)
                pe.wait_ge(es["qkT_done"], 4)
                mm(ps[:, 6, :], ev.b_tok, ev.xdtd.rearrange("p h c -> p (h c)"), start=True, stop=True)\
                    .then_inc(es["st_mm"], 1)
                for t, bank in enumerate((7, 1)):
                    if t:
                        pe.wait_ge(es["act_read"], 7)
                    for h in range(RET_H):
                        last = mm(ps[:, bank, h * P:(h + 1) * P], ev.kT[:, t, h, :], ev.qT[:, t, h, :],
                                  start=True, stop=True)
                    last.then_inc(es["ret_s_mm"], 1)
                pe.wait_ge(es["dec_done"], 1)
                kv_chunk(0, 0)
                pe.wait_ge(es["st_done"], 1)
                pe.wait_ge(es["act_read"], 9)
                for g, bank in enumerate((0, 2)):
                    gs = slice(64 * g, 64 * g + 64)
                    last = mm(ps[:, bank, 0:256], ev.xbcT[gs, 5, P:2 * P], ev.sT[gs, 256 * g:256 * g + 256],
                              start=True, stop=True)
                last.then_inc(es["yoff_mm"], 1)
                pe.wait_ge(es["kz_done"], 1)
                for h in range(RET_H):
                    last = mm(ps[:, 6, h * P:(h + 1) * P], ev.kz[:, h, :], ev.v[:, 0, h * P:(h + 1) * P],
                              start=True, stop=True)
                last.then_inc(es["ret_kv_mm"], 1)
                kv_chunk(0, 1)
                for t, bank in enumerate((7, 1)):
                    pe.wait_ge(es["s_done"], t + 1)
                    for h in range(RET_H):
                        last = mm(ps[:, bank, h * P:(h + 1) * P], ev.s[:, t, h, :], ev.v[:, t, h * P:(h + 1) * P],
                                  start=True, stop=True)
                    if t == 0:
                        last.then_inc(es["o_mm"], 1)
                pe.wait_ge(es["kvs_done"], 1)
                pe.wait_ge(es["y_ready"], 1)
                for h in range(RET_H):
                    last = mm(ps[:, 4, h * P:(h + 1) * P], ev.qT[:, 1, h, :], ev.kv[:, h, :], start=True, stop=True)
                last.then_inc(es["o_mm"], 1)
                for i in range(2, 8):
                    kv_chunk(0, i)
                pe.wait_ge(kv_read, 8)
                transposes(lambda t: pe.wait_ge(es["mix_done"], t + 1))
                pe.wait_ge(hT_done, 4 * SETS["mix0"] + 4)
                out_chunks(at["mixout", 0, 0])

            def odd():
                O = at["odd", ODD_ORDER[0]]
                for c, name in enumerate(ODD_ORDER):
                    n, bank = O + c, ps[:, c % 3, :]
                    pe.wait_ge(lo_done, n + 1)
                    if c >= 3:
                        pe.wait_ge(os_["read"], c - 2)
                    if name[0] == "q":
                        last = to_features(n, bank, hT_hi, hT_lo)
                    elif name == "c":
                        last = to_tokens(n, bank, CW, hT_hi, hT_lo)
                    else:
                        to_features(n, bank, hT_hi, hT_lo, tiles=1)
                        last = to_tokens(n, bank[:, SEQ:], P, hT_hi, hT_lo, col0=P)
                    used(last)
                    if c == 4:
                        pe.wait_ge(os_["read"], 3)
                        for kv in range(2):
                            for g in range(2):
                                for t in range(TT):
                                    for par in range(2):
                                        c0 = (2 * kv + g) * P + t * 64
                                        f0 = kv * P + g * HD
                                        last = mm(ps[64 * par:64 * par + 64, 4, c0:c0 + 64],
                                                  od.kc[:, t, f0:f0 + HD],
                                                  const("pick", 2, 64)[:, par, :], start=True, stop=True)
                        last.then_inc(os_["pick_mm"], 1)
                for t in range(TT):
                    ts = slice(t * P, (t + 1) * P)
                    for k in range(KT):
                        last = product3(ps[:, 3, 24 * t:24 * t + 24], hT_hi[:, k, ts], hT_lo[:, k, ts],
                                        gate_w_hi[:, k, :], gate_w_lo[:, k, :], k == 0, k == KT - 1)
                last.then_inc(os_["gate_mm"], 1)
                pe.wait_ge(os_["xc_lo_done"], 1)
                for i in range(4):
                    kv, half = i // 2, i % 2
                    n = at["cmp", i]
                    pe.wait_ge(lo_done, n + 1)
                    for ht in range(2):
                        for k in range(8):
                            pair = 8 * half + k
                            last = product3(ps[:, 5 + ht, 32 * kv:32 * kv + 30],
                                            cols(w_hi, n, k, CW, ht * P, ht * P + P),
                                            cols(w_lo, n, k, CW, ht * P, ht * P + P),
                                            od.xc_hi[:, kv, pair, :], od.xc_lo[:, kv, pair, :],
                                            pair == 0, pair == 15)
                    used(last)
                scores(0)
                pe.wait_ge(os_["hid_done"], 1)
                for g in range(2):
                    for ht in range(2):
                        last = mm(ps[64 * g:64 * g + 64, 7, 0:N_CMP], w2[:, 0, ht, :],
                                  od.hid[:, 0, ht, g * N_CMP:(g + 1) * N_CMP], start=ht == 0, stop=ht == 1)
                for g in range(2):
                    for ht in range(2):
                        last = mm(ps[0:N_CMP, 7, 64 + 64 * g:128 + 64 * g],
                                  od.hid[:, 1, ht, g * N_CMP:(g + 1) * N_CMP], w2[:, 1, ht, :],
                                  start=ht == 0, stop=ht == 1)
                last.then_inc(os_["c2_mm"], 1)
                pe.wait_ge(os_["gates_done"], 1)
                kv_chunk(1, 0)
                pe.wait_ge(os_["c2_read"], 1)
                for g in range(2):
                    gs = slice(64 * g, 64 * g + 64)
                    for t in range(TT):
                        for m in range(4):
                            c0 = 64 * t + N_CMP * m
                            last = mm(ps[:, 4 + g, c0:c0 + N_CMP], od.qn[gs, m, t * P:(t + 1) * P],
                                      od.kcT[gs, 0:N_CMP], start=True, stop=True)
                last.then_inc(os_["cs_mm"], 1)
                kv_chunk(1, 1)
                pe.wait_ge(os_["pc_done"], 1)
                for b in range(4):
                    for i in range(2):
                        for t in range(TT):
                            last = nc.tensor.transpose(ps[0:N_CMP, 4 + b, i * SEQ + t * P:i * SEQ + (t + 1) * P],
                                                       od.pc[:, t, 2 * b + i, :], ident)
                    last.then_inc(os_["pc_T"], 1)
                fillers = iter(range(2, 8))
                for u in range(6):
                    if u < 5:
                        scores(u + 1)
                    turned(u)
                    if u < 6:
                        kv_chunk(1, next(fillers))
                    if u in PV_AFTER:
                        values(PV_AFTER.index(u))
                pe.wait_ge(oT_done, OT_BASE["odd"] + 4)
                out_chunks(at["mixout", 1, 0])

            def scores(u):
                a, g = UNITS[u]
                if u == 0:
                    pe.wait_ge(os_["read"], 8)
                else:
                    pe.wait_ge(os_["p_exp"], u)
                gs = slice(64 * g, 64 * g + 64)
                q = od.qs if a == 2 else od.qn
                eye = mask("eye")
                mm(ps[:, 0, :].rearrange("p (h c) -> p h c", h=4), eye,
                   mask("causal0").unsqueeze(1).to_broadcast([P, 4, P]), start=True, stop=False)
                for m in range(4):
                    mm(ps[:, 0, m * P:(m + 1) * P], q[gs, m, 0:P], od.kT[gs, a, 0:P], start=False, stop=m == 3)
                for b in range(2):
                    mm(ps[:, 1 + b, :].rearrange("p (h c) -> p h c", h=2), eye,
                       mask("band1" if a == 2 else "causal1").unsqueeze(1).to_broadcast([P, 2, SEQ]),
                       start=True, stop=False)
                    for i in range(2):
                        last = mm(ps[:, 1 + b, i * SEQ:(i + 1) * SEQ], q[gs, 2 * b + i, P:2 * P], od.kT[gs, a, :],
                                  start=False, stop=i == 1)
                last.then_inc(os_["s_mm"], 1)

            def turned(u):
                pe.wait_ge(os_["p_done"], u + 1)
                if u == 0:
                    pe.wait_ge(os_["pcT_done"], 4)
                else:
                    pe.wait_ge(os_["pT_act"], 2 * u)
                    pe.wait_ge(os_["pT_dve"], u)
                for b in range(3):
                    for h in range(4):
                        src = od.p0[:, h, :] if b == 0 else od.p1[:, h, (b - 1) * P:b * P]
                        last = nc.tensor.transpose(ps[:, 4 + b, h * P:(h + 1) * P], src, ident)
                    last.then_inc(os_["p_T"], 1)

            def values(r):
                u = PV_AFTER[r]
                pe.wait_ge(os_["pT_act"], 2 * (u + 1))
                pe.wait_ge(os_["pT_dve"], u + 1)
                if r:
                    pe.wait_ge(oT_done, OT_BASE["odd"] + r)
                a, g = UNITS[u]
                units = [u - 1, u] if a == 1 else [u]
                for h in range(4):
                    out_ps = ps[64 * (h % 2):64 * (h % 2) + 64, 7, (h // 2) * SEQ:(h // 2 + 1) * SEQ]
                    first = True
                    for w in units:
                        a_w = UNITS[w][0]
                        pT = od.pT[w % 2]
                        last_unit = w == units[-1] and a == 2
                        mm(out_ps, od.v[:, a_w, 0, g * HD:(g + 1) * HD], pT[:, 0:2, h, :], start=first, stop=False)
                        last = mm(out_ps[:, P:], od.v[:, a_w, 1, g * HD:(g + 1) * HD], pT[:, 2, h, :],
                                  start=False, stop=last_unit)
                        first = False
                    if a == 1:
                        last = mm(out_ps, od.vc[0:N_CMP, g, :], od.pcT[0:N_CMP, 4 * g + h, :], start=False, stop=True)
                last.then_inc(os_["pv_mm"], 1)

            pe.wait_ge(small_in, SMALL)
            norm(0, None)
            norm(1, ("norm", 0, 0))
            ffn(0, 0)
            norm(2, ("norm", 0, 1))
            pe.wait_ge(smalls_split, 1)
            even()
            norm(3, ("norm", 0, 2))
            cross(0)
            norm(4, ("norm", 0, 3))
            ffn(0, 1)
            norm(5, ("norm", 1, 0))
            ffn(1, 0)
            norm(6, ("norm", 1, 1))
            odd()
            norm(7, ("norm", 1, 2))
            cross(1)
            norm(8, ("norm", 1, 3))
            ffn(1, 1)


INPUTS = ["x", "mem", "norm_w", "final_norm_w", "mem_norm_w", "ffn_w_gate", "ffn_w_up", "ffn_w_down",
          "xattn_wq", "xattn_wkv", "xattn_wo", "even_w_in", "even_w_out", "ssm_conv_w", "ssm_conv_b",
          "ssm_dt_bias", "ssm_a_log", "ssm_d", "ssm_norm_w", "odd_w_in", "odd_w_out", "nsa_cmp_pe",
          "nsa_cmp_w1", "nsa_cmp_w2", "swa_sinks"]


def kernel(**inputs):
    import concourse.bacc as bacc
    from concourse.bass_utils import run_bass_kernel_spmd

    nc = bacc.Bacc("TRN2", target_bir_lowering=False, num_devices=1)
    arrays, d = {}, {}
    consts, masks = shape_constants()
    for name, a in [(n, inputs[n]) for n in INPUTS] + [("consts", consts), ("masks", masks)]:
        a = np.ascontiguousarray(a)
        arrays["in_" + name] = a
        d[name] = nc.dram_tensor("in_" + name, a.shape, mybir.dt.from_np(a.dtype), kind="ExternalInput").ap()
    out = nc.dram_tensor("out_0", (1, SEQ, D), F32, kind="ExternalOutput").ap()
    build(nc, d, out)
    r = run_bass_kernel_spmd(nc, [arrays], core_ids=[0])
    return r.results[0]["out_0"]
```

```python
from contextlib import ExitStack

import numpy as np

import concourse.bass as bass
from concourse import mybir

F32 = mybir.dt.float32
F32R = mybir.dt.float32r
BF16 = mybir.dt.bfloat16
ALU = mybir.AluOpType
ACT = mybir.ActivationFunctionType
AX = mybir.AxisListType

P = 128
SEQ, MEM, D = 256, 256, 1024
TT = SEQ // P
KT = D // P
DFF = 2816
CW = 256
FJ = DFF // CW
CHUNK = KT * CW
EPS = 1e-6
RING = 3
BIG = 1e30

RET_H, DK = 4, 128
SSM_H, HP, NS, SSM_IN = 8, 64, 64, 512
CONV_CH, CONV_W = 768, 4
XT = CONV_CH // P
EVEN_IN = 3336
HD, NH = 64, 8
N_CMP, CMP_STRIDE, CMP_BLK = 15, 16, 32
CMP_PAIRS = CMP_BLK // 2
XH, XD = 4, 256

CONSTS = {}
_at = 0
for _name, _w in (("ident", P), ("upto", P), ("after", P), ("cos", TT * 64), ("sin", TT * 64),
                  ("decayT", RET_H * P), ("zeta", RET_H), ("xi", RET_H), ("pick", P),
                  ("cmpmask", TT * N_CMP), ("cmpbias", TT * N_CMP)):
    CONSTS[_name] = (_at, _w)
    _at += _w
CONST_W = _at
MASKS = {"causal0": (0, P), "causal1": (P, 2 * P), "band1": (3 * P, 2 * P), "eye": (5 * P, P)}
MASK_W = 6 * P


def shape_constants():
    f = np.float32
    c = np.zeros((P, CONST_W), f)

    def put(name, a):
        at, w = CONSTS[name]
        c[:, at:at + w] = np.asarray(a, f).reshape(P, w)

    i = np.arange(P)
    put("ident", np.eye(P))
    put("upto", i[:, None] <= i[None, :])
    put("after", i[:, None] > i[None, :])
    pos = np.arange(SEQ, dtype=f)
    inv = (f(1.0) / (f(10000.0) ** np.linspace(0.0, 1.0, DK // 2, dtype=f))).astype(f)
    ang = (pos[:, None] * inv[None, :]).astype(f).reshape(TT, P, 64).transpose(1, 0, 2)
    put("cos", np.cos(ang))
    put("sin", np.sin(ang))
    log_g = np.log1p(-np.exp2(-5.0 - np.arange(RET_H)))
    diff = i[None, :] - i[:, None]
    scale = DK ** -0.5
    put("decayT", np.where(diff[:, None, :] >= 0,
                           np.exp(np.maximum(diff, 0)[:, None, :] * log_g[None, :, None]), 0.0) * scale)
    put("zeta", np.exp((P - 1 - i)[:, None] * log_g[None, :]) * scale)
    put("xi", np.exp((i + 1)[:, None] * log_g[None, :]))
    pick = np.zeros((P, 2, P // 2))
    for par in range(2):
        pick[2 * np.arange(P // 2) + par, par, np.arange(P // 2)] = 1
    put("pick", pick)
    tok = np.arange(SEQ).reshape(TT, P).T
    seen = (np.arange(N_CMP) * CMP_STRIDE + CMP_BLK - 1)[None, None, :] <= tok[:, :, None]
    put("cmpmask", seen)
    put("cmpbias", np.where(seen, 0.0, -BIG))
    m = np.zeros((P, MASK_W), f)
    causal = np.where(i[:, None] >= i[None, :], 0.0, -BIG)
    m[:, 0:P] = causal
    m[:, 2 * P:3 * P] = causal
    m[:, 3 * P:4 * P] = np.where(i[None, :] > i[:, None], 0.0, -BIG)
    m[:, 4 * P:5 * P] = causal
    m[:, 5 * P:6 * P] = np.eye(P)
    return c, m


FFN_CHUNKS = 3 * FJ
EVEN_ORDER = ["x0", "x1", "x2", "q0", "q1", "k0", "k1", "v0", "v1", "g0", "g1", "z0", "z1"]
ODD_ORDER = ["s", "w", "c", "qn0", "qn1", "qs0", "qs1"]


def chunk_plan():
    at, n = {}, 0

    def take(names):
        nonlocal n
        for x in names:
            at[x] = n
            n += 1

    for layer in range(2):
        at["ffn", layer, 0] = n
        n += FFN_CHUNKS
        kv = [("kv", layer, i) for i in range(8)]
        if layer == 0:
            take([("even", x) for x in EVEN_ORDER])
            take(kv)
            take([("mixout", layer, i) for i in range(4)])
        else:
            take([("odd", x) for x in ODD_ORDER])
            take([("cmp", i) for i in range(4)])
            take([("odd", "a")])
            take(kv)
            take([("mixout", layer, i) for i in range(4)])
        take([("wq", layer, i) for i in range(4)])
        take([("wo", layer, i) for i in range(4)])
        at["ffn", layer, 1] = n
        n += FFN_CHUNKS
    return at, n


def build(nc, d, out):
    at, n_chunks = chunk_plan()
    ctx = ExitStack()
    with ctx:
        def sb(name, shape, dt=F32):
            return ctx.enter_context(nc.sbuf_tensor(name, shape, dt))

        def sem(name):
            return ctx.enter_context(nc.semaphore(name))

        ps = ctx.enter_context(nc.psum_tensor("ps", [P, 8, 512], F32))
        x = sb("x", [P, TT, D])
        xn = sb("xn", [P, TT, D])
        hT_hi = sb("hT_hi", [P, KT, SEQ], F32R)
        hT_lo = sb("hT_lo", [P, KT, SEQ], F32R)
        memT_hi = sb("memT_hi", [P, KT, MEM], F32R)
        memT_lo = sb("memT_lo", [P, KT, MEM], F32R)
        raw = sb("raw", [P, RING, CHUNK])
        w_hi = sb("w_hi", [P, RING, CHUNK], F32R)
        w_lo = sb("w_lo", [P, RING, CHUNK], F32R)
        xk = sb("xk", [P, KT, MEM])
        xv = sb("xv", [P, TT, D])
        norm_w = sb("norm_w_rows", [P, D])
        consts = sb("consts", [P, CONST_W])
        masks_f = xk[:, 0:3, :].rearrange("p a b -> p (a b)")
        masks = sb("masks", [P, MASK_W], BF16)
        msum = sb("msum", [P, 4])
        msq = sb("msq", [P, 16])
        rstd = sb("rstd", [P, 2])
        neg_half = sb("neg_half", [P, 8])
        DT_AT, GATE_AT, SMALL_W = 0, KT * SSM_H, KT * SSM_H + KT * 3 * NH + 120
        small_w = xk[:, :, :].rearrange("p k c -> p (k c)")[:, 1024:1024 + SMALL_W]
        small_w_hi = sb("small_w_hi", [P, SMALL_W], F32R)
        small_w_lo = sb("small_w_lo", [P, SMALL_W], F32R)
        conv_w = sb("conv_w", [P, CONV_W, XT])
        conv_b = sb("conv_b", [P, XT])
        head_rows = sb("head_rows", [P, 4, SSM_H])
        w2 = sb("w2", [P, 2, 2, HD])
        pe_pairs = sb("pe_pairs", [P, 2, CMP_PAIRS])
        ssm_nw = sb("ssm_nw", [P, SSM_IN])
        ARENA = 11760
        XC_W = 2 * CMP_PAIRS * 2 * N_CMP + P - 2 * N_CMP + 2
        arena_r = sb("arena_r", [P, 2 * XC_W], F32R)
        arena = sb("arena", [P, ARENA])

        def part(at_, shape, dt=F32):
            size = int(np.prod(shape))
            assert at_ + size <= ARENA, (at_, shape)
            v = arena[:, at_:at_ + size]
            if dt is not F32:
                v = v.bitcast(dt)
            if len(shape) == 1:
                return v
            names = "abcde"[:len(shape)]
            sizes = {k: s for k, s in zip(names[1:], shape[1:])}
            return v.rearrange(f"p ({' '.join(names)}) -> p {' '.join(names)}", **sizes)

        def const(name, *dims):
            a, w = CONSTS[name]
            v = consts[:, a:a + w]
            if len(dims) > 1:
                names = "abc"[:len(dims)]
                v = v.rearrange(f"p ({' '.join(names)}) -> p {' '.join(names)}",
                                **{k: s for k, s in zip(names[1:], dims[1:])})
            return v

        def mask(name):
            a, w = MASKS[name]
            return masks[:, a:a + w]

        ident = const("ident")
        mem_rows = xv[:, :, :]

        raw_in = [sem(f"raw_in{i}") for i in range(RING)]
        hi_done = sem("hi_done")
        lo_done = sem("lo_done")
        chunks_used = sem("chunks_used")
        small_in = sem("small_in")
        x_in = [sem(f"x_in{t}") for t in range(TT)]
        ident_in = sem("ident_in")
        mem_in = sem("mem_in")
        norm_w_in = sem("norm_w_in")
        out_sent = sem("out_sent")
        consts_made = sem("consts_made")
        small_w_set = sem("small_w_set")
        row_done = sem("row_done")
        smalls_split = sem("smalls_split")
        neg_half_set = sem("neg_half_set")
        sq_done = sem("sq_done")
        ms_done = sem("ms_done")
        rstd_done = sem("rstd_done")
        xn_done = sem("xn_done")
        transposed = sem("transposed")
        hT_hi_done = sem("hT_hi_done")
        hT_done = sem("hT_done")
        x_added = sem("x_added")
        silu_done = sem("silu_done")
        mult_done = sem("mult_done")
        gu_hi_done = sem("gu_hi_done")
        gu_done = sem("gu_done")
        oT_hi_done = sem("oT_hi_done")
        oT_done = sem("oT_done")
        kv_read = sem("kv_read")
        act_step, dve_step, pool_step = sem("act_step"), sem("dve_step"), sem("pool_step")

        SETS = {("norm", 0, 0): 0, "mem": 1, ("norm", 0, 1): 2, "mix0": 3, ("norm", 0, 2): 4,
                ("norm", 0, 3): 5, ("norm", 1, 0): 6, ("norm", 1, 1): 7, ("norm", 1, 2): 8,
                ("norm", 1, 3): 9}

        def row_bank(w, t, kh):
            return 2 + kh if w == SETS["mem"] else 2 * t + kh

        def norm_no(layer, i):
            return 1 + 4 * layer + i if layer or i else 0

        def w_view(ap):
            return ap.rearrange("(k p) c -> p k c", p=P)

        def pieces_of(name):
            kind = name[0]
            if kind == "even":
                s = name[1]
                col = {"q": 0, "k": 512, "v": 1024, "g": 1536, "z": 2048, "x": 2560}[s[0]] + CW * int(s[1])
                return [(("k", CW), w_view(d["even_w_in"][0][:, col:col + CW]))]
            if kind == "odd":
                s = name[1]
                if s[0] == "q":
                    base = {"n": 0, "s": 1304}[s[1]] + P * int(s[2])
                    return [(("run", i * P + g * HD), w_view(
                        d["odd_w_in"][0][:, base + g * 256 + i * HD:base + g * 256 + (i + 1) * HD]))
                        for i in range(2) for g in range(2)]
                col = {"c": 512, "s": 768, "w": 1024, "a": 1816}[s]
                return [(("k", CW), w_view(d["odd_w_in"][0][:, col:col + CW]))]
            if kind == "cmp":
                kv, half = name[1] // 2, name[1] % 2
                return [(("k", CW), d["nsa_cmp_w1"][0, kv].rearrange("(k p) c -> p k c", p=P)
                         [:, 8 * half:8 * half + 8, :])]
            layer, i = name[1], name[2]
            if kind == "kv":
                return [(("k", CW), w_view(d["xattn_wkv"][layer][:, i * CW:(i + 1) * CW]))]
            if kind == "wq":
                return [(("k", CW), w_view(d["xattn_wq"][layer][:, i * CW:(i + 1) * CW]))]
            src = d["xattn_wo"][layer] if kind == "wo" else d["even_w_out" if layer == 0 else "odd_w_out"][0]
            return [(("k", D), src[2 * P * i:2 * P * (i + 1), :].rearrange("(k p) c -> p k c", p=P))]

        order = sorted((v, k) for k, v in at.items() if k[0] != "ffn")
        named = {v: k for v, k in order}
        pieces = [len(pieces_of(named[n])) if n in named else 1 for n in range(n_chunks)]

        def landed(n):
            return 16 * sum(pieces[m] for m in range(n % RING, n + 1, RING))

        W_SLOT = CHUNK

        def slot_k(n, width):
            return raw[:, n % RING, :].rearrange("p (k c) -> p k c", c=width)

        g_act = part(0, [512])
        gu = part(512, [512])
        gu_hi, gu_lo, gu_hi_last, gu_lo_last = (
            arena_r[:, i * 512:(i + 1) * 512].rearrange("p (k c) -> p k c", k=2) for i in range(4))

        class Even:
            xpad = part(0, [XT, SEQ + 3])
            ld = xk[:, :, :].rearrange("p k c -> p (k c)").rearrange("p (t h s) -> p t h s", t=TT, h=SSM_H)
            xbcT = part(1920, [XT, SEQ])
            q_rot = part(3456, [TT, RET_H, 2, 64])
            o = part(3456, [TT, RET_H, P])
            k_rot = part(4480, [TT, RET_H, 2, 64])
            s = part(4480, [TT, RET_H, P])
            rot = [part(5504 + 256 * i, [TT, 2, 64]) for i in range(4)]
            cbm = part(5504, [TT, 2, P])
            kz = part(6016, [RET_H, P])
            qT = part(6528, [TT, RET_H, P])
            kT = part(7552, [TT, RET_H, P])
            v = part(8576, [TT, RET_H * DK])
            xh = part(9600, [TT, SSM_H, HP])
            xdt = part(10624, [TT, SSM_H, HP])
            mt = xv[:, :, :].rearrange("p t (h s) -> p t h s", h=SSM_H)
            b_tok = part(1664, [P])
            dtT = part(4480, [SEQ])
            small = part(11648, [112])
            dtr = small[:, 0:16]
            ln1p = small[:, 16:32]
            dt = small[:, 32:48]
            dta = small[:, 48:64]
            ea = small[:, 64:72]
            dec = small[:, 72:80]
            cum = small[:, 80:88]
            ssr = small[:, 88:90]
            rsr = small[:, 90:92]
            msr = small[:, 92:94]
            osq = small[:, 96:104]
            ors = small[:, 104:112]
            oms = msq[:, 8:16]
            yc = part(5504, [SSM_H, HP])
            xdtd = part(0, [SSM_H, HP])
            kv = part(512, [RET_H, P])
            sT = part(1024, [SSM_IN])
            dtr = small[:, 0:16]
        ev = Even

        even_sems = {}
        for name in ("xpad_zero", "act_read", "conv_done", "xbc_done", "dt_mm", "dtT_done", "dt_T",
                     "dt_raw", "ln_done", "dta_done", "ea_done", "ld_done", "rot_read",
                     "rot_done", "xs_T", "xh_done", "cb_mm", "cbm_done", "dec_mm", "dec_done",
                     "seg_mm", "seg_exp", "mt_done", "xdt_done", "xdtd_done", "qk_T", "qkT_done",
                     "kz_done", "ret_s_mm", "s_done", "st_mm", "st_done", "ret_kv_mm", "kvs_done",
                     "y_mm", "yoff_mm", "y_read", "o_mm", "o_read", "dx_done", "y_sq", "o_sq", "o_ssq",
                     "y_rstd", "o_rstd", "mix_done", "y_ready"):
            even_sems[name] = sem("e_" + name)
        es = even_sems

        class Odd:
            qn = part(0, [4, SEQ])
            qs = part(1024, [4, SEQ])
            kT = part(2048, [3, SEQ])
            v = part(2816, [3, TT, P])
            kc = part(3584, [TT, 2 * P])
            xc = part(4096, [2, CMP_PAIRS, 2, N_CMP])
            xc_hi, xc_lo = (arena_r[:, i * XC_W:i * XC_W + 960] for i in range(2))
            xc_hi_wide, xc_lo_wide = (arena_r[:, i * XC_W:(i + 1) * XC_W] for i in range(2))
            hid = part(5632, [2, 2, 2 * N_CMP])
            kcT = part(5760, [16])
            vc = part(5776, [2, HD])
            pc = part(5904, [TT, NH, N_CMP])
            pcT = part(6144, [NH, SEQ])
            p0 = part(8192, [4, P])
            p1 = part(8704, [4, SEQ])
            hid_rows = part(8704, [2, 2 * P])
            gT = part(9216, [SEQ])
            pT = [part(9728, [3, 4, P]), part(4096, [3, 4, P])]
            small = part(11264, [120])
            gates = small[:, 0:48]
            nmax = small[:, 48:56]
            rs = small[:, 56:64]
            fac = small[:, 64:72]
            es = small[:, 72:80]
            cmax = small[:, 80:96]
            csum = small[:, 96:112]
            nmax2 = small[:, 112:120]

        od = Odd
        os_ = {name: sem("o_" + name) for name in (
            "read", "gate_mm", "gT_done", "gate_T", "gates_done", "xc_tail", "hr_done", "hid_T", "pick_mm", "xc_done", "xc_hi_done", "xc_lo_done",
            "hid_done", "c2_mm", "c2_read", "cs_mm", "cs_in", "cs_exp", "pc_done", "pc_T", "pcT_done",
            "s_mm", "nmax_done", "p_exp", "p_done", "p_T", "pT_act", "pT_dve", "pv_mm")}

        class Cross:
            q = part(0, [KT, SEQ])
            p = part(2048, [XH, TT, MEM])
            pT = part(4096, [XH, 2, SEQ])
            small = part(6144, [32])
            nmax = small[:, 0:8]
            rs = small[:, 8:16]
            fac = small[:, 16:24]

        cr = Cross
        xs_ = {name: sem("x_" + name) for name in (
            "q_read", "s_mm", "nmax", "p_exp", "p_done", "p_T", "pT_done", "pv_mm")}
        KV_BANK = [(3, 3, 5, 6, 5, 6, 5, 3), (3,) * 8]
        OT_BASE = {"cross0": 0, "odd": 4, "cross1": 8}
        UNITS = [(0, 0), (1, 0), (0, 1), (1, 1), (2, 0), (2, 1)]
        PV_AFTER = [1, 3, 4, 5]
        PV_BANK = [7, 7, 7, 0]

        def pv_before(u):
            return 1 if u < 4 else 2

        block = ctx.enter_context(nc.Block())

        def small_loads():
            rows = [d["ssm_dt_bias"][0], d["ssm_a_log"][0], d["ssm_d"][0], d["swa_sinks"][0]]
            w_in = {"dt": d["even_w_in"][0][:, EVEN_IN - SSM_H:EVEN_IN], "gate": d["odd_w_in"][0][:, 1280:1304]}
            loads = [(consts[:, P:], d["consts"][:, P:]), (masks_f, d["masks"]),
                     (small_w[:, DT_AT:GATE_AT].rearrange("p (k c) -> p k c", k=KT), w_view(w_in["dt"])),
                     (small_w[:, GATE_AT:GATE_AT + KT * 3 * NH].rearrange("p (k c) -> p k c", k=KT),
                      w_view(w_in["gate"])),
                     (w2[:, 0, :, :], d["nsa_cmp_w2"][0, 0].rearrange("(t p) c -> p t c", p=P)),
                     (w2[:, 1, :, :], d["nsa_cmp_w2"][0, 1].rearrange("(t p) c -> p t c", p=P)),
                     (ssm_nw[:, :], d["ssm_norm_w"][0].partition_broadcast(P))]
            loads += [(head_rows[:, i, :], r.partition_broadcast(P)) for i, r in enumerate(rows)]
            return loads

        def strided_loads():
            loads = [(conv_b[:, :], d["ssm_conv_b"][0].rearrange("(t p) -> p t", p=P))]
            loads += [(conv_w[:, w, :], d["ssm_conv_w"][0, w].rearrange("(t p) -> p t", p=P))
                      for w in range(CONV_W)]
            loads += [(pe_pairs[:, kv, :], d["nsa_cmp_pe"][0, kv].rearrange("(i r) c -> (r c) i", r=2))
                      for kv in range(2)]
            return loads

        SMALL = 16 * (len(small_loads()) + len(strided_loads()))

        @block.sync
        def _(sp):
            def load(n, dst_view, src):
                if n >= RING:
                    sp.wait_ge(lo_done, n - RING + 1)
                sp.dma_start(dst_view, src).then_inc(raw_in[n % RING], 16)

            def named_chunks(first, last):
                for n in range(first, last):
                    if n >= RING:
                        sp.wait_ge(lo_done, n - RING + 1)
                    for (kind, arg), src in pieces_of(named[n]):
                        dst = slot_k(n, arg) if kind == "k" else slot_k(n, CW)[:, :, arg:arg + HD]
                        sp.dma_start(dst, src).then_inc(raw_in[n % RING], 16)

            def ffn(layer, which, first=False):
                base = at["ffn", layer, which]
                gate, up = (d[w][layer, which].rearrange("(k p) (j c) -> j p k c", p=P, c=CW)
                            for w in ("ffn_w_gate", "ffn_w_up"))
                down = d["ffn_w_down"][layer, which].rearrange("(j k p) c -> j p k c", k=2, p=P)
                load(base, slot_k(base, CW), gate[0])
                load(base + 1, slot_k(base + 1, CW), up[0])

                def turn(j):
                    for c, (w, width, row) in enumerate(((gate, CW, j + 1), (up, CW, j + 1), (down, D, j))):
                        n = base + 2 + c
                        if not (first and isinstance(j, int) and c == 0):
                            sp.wait_ge(lo_done, j * 3 + (n - RING + 1))
                        sp.dma_start(slot_k(n, width), w[bass.ds(row, 1)].rearrange("a p k c -> (a p) k c"))\
                          .then_inc(raw_in[n % RING], 16)

                if first:
                    turn(0)
                    sp.dma_start(mem_rows, d["mem"][0].rearrange("(t p) c -> p t c", p=P)).then_inc(mem_in, 16)
                    for dst, src in small_loads():
                        sp.dma_start(dst, src).then_inc(small_in, 16)
                    with nc.allow_non_contiguous_dma(reason="a few KB of per-channel columns"):
                        for dst, src in strided_loads():
                            sp.dma_start(dst, src).then_inc(small_in, 16)
                with sp.Fori(1 if first else 0, FJ - 1) as j:
                    turn(j)
                n = base + FFN_CHUNKS - 1
                load(n, slot_k(n, D), down[FJ - 1])

            for t in range(TT):
                sp.dma_start(x[:, t, :], d["x"][0, t * P:(t + 1) * P, :]).then_inc(x_in[t], 16)
            ffn(0, 0, first=True)
            named_chunks(at["ffn", 0, 0] + FFN_CHUNKS, at["ffn", 0, 1])
            ffn(0, 1)
            ffn(1, 0)
            named_chunks(at["ffn", 1, 0] + FFN_CHUNKS, at["ffn", 1, 1])
            ffn(1, 1)
            for t in range(TT):
                for h in range(2):
                    sp.wait_ge(xn_done, 4 * 9 + 2 * t + h + 1)
                    hs = slice(h * 512, (h + 1) * 512)
                    sp.dma_start(out[0, t * P:(t + 1) * P, hs], xn[:, t, hs]).then_inc(out_sent, 16)
            sp.wait_ge(out_sent, 2 * 16 * TT)

        @block.scalar
        def _(act):
            made, steps = [0], [0]

            def step(ins):
                steps[0] += 1
                ins.then_inc(act_step, 1)
                act.wait_ge(act_step, steps[0])

            def hi_upto(limit):
                for n in range(made[0], min(limit, n_chunks)):
                    act.wait_ge(raw_in[n % RING], landed(n))
                    if n >= RING:
                        act.wait_ge(chunks_used, n - RING + 1)
                    nc.scalar.activation(w_hi[:, n % RING, :], raw[:, n % RING, :], ACT.Copy).then_inc(hi_done, 1)
                    made[0] = n + 1

            def squares(v, src, ready):
                for t in range(TT):
                    for h in range(2):
                        ready(t, h)
                        bank = 2 * t + h if v != 1 else 2 + h
                        if v == 1 and t:
                            act.wait_ge(sq_done, 4 * v + h + 1)
                        nc.scalar.activation(ps[:, bank, :], src[:, t, h * 512:(h + 1) * 512], ACT.Square,
                                             scale=D ** -0.5, accum_out=msum[:, 2 * t + h:2 * t + h + 1])\
                          .then_inc(sq_done, 1)

            def evac_hi(w, dst, tiles=(0, 1)):
                for t in tiles:
                    for kh in range(2):
                        act.wait_ge(transposed, 4 * w + 2 * t + kh + 1)
                        nc.scalar.activation(dst[:, 4 * kh:4 * kh + 4, t * P:(t + 1) * P],
                                             ps[:, row_bank(w, t, kh), :].rearrange("p (k c) -> p k c", c=P),
                                             ACT.Copy).then_inc(hT_hi_done, 1)

            def norm(layer, i):
                v = norm_no(layer, i)

                def ready(t, h):
                    if v == 0:
                        act.wait_ge(x_in[t], 16)
                    else:
                        act.wait_ge(x_added, 4 * (v - 2) + 2 * t + h + 1)
                squares(v, x, ready)
                evac_hi(SETS["norm", layer, i], hT_hi)

            def kv_chunk(layer, i):
                act.wait_ge(chunks_used, at["kv", layer, i] + 1)
                pv = ps[:, KV_BANK[layer][i], :].rearrange("p (a c) -> p a c", a=2)
                dst = xk[:, 2 * i:2 * i + 2, :] if i < 4 else xv[:, :, (i - 4) * CW:(i - 3) * CW]
                nc.scalar.activation(dst, pv, ACT.Copy).then_inc(kv_read, 1)
                hi_upto(at["kv", layer, i] + 4)

            def ffn(layer, which):
                f, base = 2 * layer + which, at["ffn", layer, which]

                def silu(j, cell):
                    act.wait_ge(chunks_used, j * 3 + cell)
                    nc.scalar.activation(g_act, ps[:, 0, :], ACT.Silu).then_inc(silu_done, 1)

                def hidden(count, dst):
                    act.wait_ge(mult_done, count)
                    nc.scalar.activation(dst, gu.rearrange("p (k c) -> p k c", k=2),
                                         ACT.Copy).then_inc(gu_hi_done, 1)

                def turn(j, between=lambda c: None):
                    for c in range(3):
                        n = base + 2 + c
                        if c == 0:
                            act.wait_ge(mult_done, j + f * FJ)
                            silu(j, base)
                        if c == 2:
                            act.wait_ge(chunks_used, j * 3 + (base + 2))
                            hidden(j + (f * FJ + 1), gu_hi)
                        m = n + RING
                        act.wait_ge(raw_in[m % RING], (j - 1) * 16 + landed(m))
                        act.wait_ge(chunks_used, (j - 1) * 3 + (m - RING + 1))
                        nc.scalar.activation(w_hi[:, m % RING, :], raw[:, m % RING, :], ACT.Copy).then_inc(hi_done, 1)
                        between(c)

                hi_upto(base + 3)
                silu(0, base + 1)
                hi_upto(base + 5)
                hidden(f * FJ + 1, gu_hi)
                if f == 0:
                    turn(1)
                    mem_rows_done()
                    turn(2, lambda c: c < 2 and evac_hi(SETS["mem"], memT_hi, tiles=(c,)))
                with act.Fori(1 if f else 3, FJ - 1) as j:
                    turn(j)
                made[0] = base + FFN_CHUNKS - 1
                act.wait_ge(mult_done, FJ - 1 + f * FJ)
                silu(FJ - 1, base)
                hi_upto(base + FFN_CHUNKS)
                hidden((f + 1) * FJ, gu_hi_last)
                hi_upto(base + FFN_CHUNKS + 2)

            def cross(layer):
                u = 4 * layer
                wq, wo = at["wq", layer, 0], at["wo", layer, 0]
                hi_upto(wq + 3)
                for i in range(4):
                    act.wait_ge(chunks_used, wq + i + 1)
                    nc.scalar.activation(cr.q[:, 2 * i:2 * i + 2, :],
                                         ps[:, i % 3, :].rearrange("p (a c) -> p a c", a=2),
                                         ACT.Copy, scale=XD ** -0.5).then_inc(xs_["q_read"], 1)
                    if i < 3:
                        hi_upto(wq + i + 4)
                for h in range(XH):
                    act.wait_ge(xs_["nmax"], u + h + 1)
                    for t in range(TT):
                        ins = nc.scalar.activation(cr.p[:, h, t, :], ps[:, 4 + h, t * MEM:(t + 1) * MEM],
                                                   ACT.Exp, bias=cr.nmax[:, 2 * h + t:2 * h + t + 1],
                                                   accum_out=cr.rs[:, 2 * h + t:2 * h + t + 1])
                        ins.then_inc(xs_["p_exp"], 1)
                    if h >= 1:
                        probs_out(u, h - 1)
                probs_out(u, XH - 1)
                for h in range(XH):
                    act.wait_ge(xs_["pv_mm"], u + h + 1)
                    nc.scalar.activation(hT_hi[:, 2 * h:2 * h + 2, :],
                                         ps[:, h, :].rearrange("p (a c) -> p a c", a=2),
                                         ACT.Copy).then_inc(oT_hi_done, 1)
                hi_upto(wq + 4 + 3)
                for i in range(3):
                    hi_upto(wo + i + 4)

            def probs_out(u, h):
                act.wait_ge(xs_["p_T"], u + h + 1)
                nc.scalar.activation(cr.pT[:, h, :, :], ps[:, (3, 1, 2, 3)[h], :].rearrange("p (a c) -> p a c", a=2),
                                     ACT.Copy).then_inc(xs_["pT_done"], 1)

            def even():
                E = at["even", "x0"]
                for c in range(3):
                    act.wait_ge(chunks_used, E + c + 1)
                    if c == 0:
                        act.wait_ge(es["xpad_zero"], 1)
                    nc.scalar.activation(ev.xpad[:, 2 * c:2 * c + 2, CONV_W - 1:],
                                         ps[:, c, :].rearrange("p (a c) -> p a c", a=2),
                                         ACT.Copy)
                    for m in range(2):
                        k = 2 * c + m
                        ins = nc.scalar.activation(ev.xbcT[:, k, :], ps[:, c, m * SEQ:(m + 1) * SEQ], ACT.Identity,
                                                   bias=conv_b[:, k:k + 1], scale=conv_w[:, CONV_W - 1, k:k + 1])
                    ins.then_inc(es["act_read"], 1)
                    hi_upto(E + c + 4)
                    if c:
                        conv_silu(c - 1)
                conv_silu(2)
                act.wait_ge(es["dt_raw"], 1)
                step(nc.scalar.activation(ev.ln1p, ev.dtr, ACT.Abs))
                step(nc.scalar.activation(ev.ln1p, ev.ln1p, ACT.Exp, scale=-1.0))
                nc.scalar.activation(ev.ea, head_rows[:, 1, :], ACT.Exp).then_inc(es["ea_done"], 1)
                nc.scalar.activation(ev.ln1p, ev.ln1p, ACT.Ln, bias=1.0).then_inc(es["ln_done"], 1)
                for e in range(3, 7):
                    hi_upto(E + e + 4)
                for t in range(TT):
                    act.wait_ge(es["xs_T"], t + 1)
                    nc.scalar.activation(ev.xh[:, t, :, :], ps[:, 4 + t, :].rearrange("p (h c) -> p h c", h=SSM_H),
                                         ACT.Copy).then_inc(es["xh_done"], 1)
                act.wait_ge(es["xs_T"], 3)
                nc.scalar.activation(ev.b_tok, ps[:, 3, 0:P], ACT.Copy).then_inc(es["xh_done"], 1)
                for i, e in enumerate((7, 8)):
                    act.wait_ge(chunks_used, E + e + 1)
                    nc.scalar.activation(ev.v[:, :, i * CW:(i + 1) * CW],
                                         ps[:, e % 3, :].rearrange("p (a c) -> p a c", a=2),
                                         ACT.Copy).then_inc(es["act_read"], 1)
                    hi_upto(E + e + 4)
                act.wait_ge(es["dec_mm"], 1)
                nc.scalar.activation(ev.small[:, 72:88], ps[:, 3, P:P + 16], ACT.Exp).then_inc(es["dec_done"], 1)
                for q in range(4):
                    act.wait_ge(es["seg_mm"], q + 1)
                    nc.scalar.activation(ev.mt[:, q // 2, 4 * (q % 2):4 * (q % 2) + 4, :],
                                         ps[:, 4 + q, :].rearrange("p (a c) -> p a c", a=4),
                                         ACT.Exp).then_inc(es["seg_exp"], 1)
                for i, e in enumerate((9, 10)):
                    act.wait_ge(chunks_used, E + e + 1)
                    nc.scalar.activation(xn[:, :, i * CW:(i + 1) * CW],
                                         ps[:, e % 3, :].rearrange("p (a c) -> p a c", a=2),
                                         ACT.Silu).then_inc(es["act_read"], 1)
                    hi_upto(E + e + 4)
                for i, dst in enumerate((ev.qT, ev.kT)):
                    for t in range(TT):
                        act.wait_ge(es["qk_T"], 2 * i + t + 1)
                        nc.scalar.activation(dst[:, t, :, :], ps[:, 4 + 2 * i + t, :].rearrange("p (a c) -> p a c", a=4),
                                             ACT.Copy).then_inc(es["qkT_done"], 1)
                for i, e in enumerate((11, 12)):
                    act.wait_ge(chunks_used, E + e + 1)
                    nc.scalar.activation(xn[:, :, 512 + i * CW:512 + (i + 1) * CW],
                                         ps[:, e % 3, :].rearrange("p (a c) -> p a c", a=2),
                                         ACT.Silu).then_inc(es["act_read"], 1)
                    hi_upto(E + e + 4)
                act.wait_ge(es["st_mm"], 1)
                nc.scalar.activation(ev.sT, ps[:, 6, :], ACT.Copy).then_inc(es["st_done"], 1)
                kv_chunk(0, 0)
                act.wait_ge(es["ret_kv_mm"], 1)
                nc.scalar.activation(ev.kv, ps[:, 6, :].rearrange("p (a c) -> p a c", a=4),
                                     ACT.Copy).then_inc(es["kvs_done"], 1)
                kv_chunk(0, 1)
                for t in range(TT):
                    act.wait_ge(es["y_ready"], t + 1)
                    nc.scalar.activation(ev.xdt[:, t, :, :], ev.xh[:, t, :, :], ACT.Square,
                                         accum_out=ev.ssr[:, t:t + 1]).then_inc(es["y_sq"], 1)
                kv_chunk(0, 2)
                act.wait_ge(es["o_read"], 1)
                act.wait_ge(es["y_read"], 1)
                nc.scalar.activation(ev.mt[:, :, 0:4, :], ev.o, ACT.Square).then_inc(es["o_sq"], 1)
                kv_chunk(0, 3)
                act.wait_ge(es["o_ssq"], 1)
                for i in range(4, 6):
                    kv_chunk(0, i)
                evac_hi(SETS["mix0"], hT_hi)
                for i in range(6, 8):
                    kv_chunk(0, i)

            def conv_silu(c):
                act.wait_ge(es["conv_done"], c + 1)
                nc.scalar.activation(ev.xbcT[:, 2 * c:2 * c + 2, :], ev.xbcT[:, 2 * c:2 * c + 2, :],
                                     ACT.Silu).then_inc(es["xbc_done"], 1)

            def odd():
                def read(c, name, b):
                    n = at["odd", name]
                    act.wait_ge(chunks_used, n + 1)
                    bank = ps[:, b, :].rearrange("p (a c) -> p a c", a=2)
                    if name[0] == "q":
                        dst = od.qn if name[1] == "n" else od.qs
                        m = 2 * int(name[2])
                        nc.scalar.activation(dst[:, m:m + 2, :], bank, ACT.Copy, scale=HD ** -0.5)\
                          .then_inc(os_["read"], 1)
                    elif name == "c":
                        nc.scalar.activation(od.kc, bank, ACT.Copy).then_inc(os_["read"], 1)
                    else:
                        j = "swa".index(name)
                        nc.scalar.activation(od.kT[:, j, :], bank[:, 0, :], ACT.Copy)
                        nc.scalar.activation(od.v[:, j, :, :], bank[:, 1, :].rearrange("p (a c) -> p a c", a=2),
                                             ACT.Copy).then_inc(os_["read"], 1)

                def weights_read(b):
                    act.wait_ge(os_["pc_T"], b + 1)
                    nc.scalar.activation(od.pcT[0:N_CMP, 2 * b:2 * b + 2, :],
                                         ps[0:N_CMP, 7, :].rearrange("p (h c) -> p h c", h=2),
                                         ACT.Copy).then_inc(os_["pcT_done"], 1)

                act.wait_ge(os_["gate_mm"], 1)
                nc.scalar.activation(od.gT[0:3 * NH, :], ps[0:3 * NH, 3, 0:SEQ], ACT.Copy).then_inc(os_["gT_done"], 1)
                for c, name in enumerate(ODD_ORDER):
                    read(c, name, c % 3)
                    hi_upto(at["odd", name] + 4)
                    if c == 1:
                        act.wait_ge(os_["gate_T"], 1)
                        nc.scalar.activation(od.gates, ps[:, 3, SEQ:SEQ + 48], ACT.Exp, scale=-1.0)\
                          .then_inc(os_["gates_done"], 1)
                    if c == 4:
                        act.wait_ge(os_["xc_done"], 1)
                        nc.scalar.activation(od.xc_hi, od.xc.rearrange("p k i g n -> p (k i g n)"), ACT.Copy)\
                          .then_inc(os_["xc_hi_done"], 1)
                C = at["cmp", 0]
                for kv in range(2):
                    act.wait_ge(chunks_used, C + 2 * kv + 2)
                    nc.scalar.activation(od.hid_rows[0:2 * N_CMP, kv, :], ps[0:2 * N_CMP, 5 + kv, 0:2 * P],
                                         ACT.Silu).then_inc(os_["hr_done"], 1)
                    hi_upto(C + 2 * kv + 5)
                read(7, "a", 3)
                act.wait_ge(os_["hid_T"], 1)
                nc.scalar.activation(od.hid.rearrange("p k t c -> p (k t) c"),
                                     ps[:, 4, 0:P].rearrange("p (q c) -> p q c", q=4)[:, :, 0:2 * N_CMP],
                                     ACT.Copy).then_inc(os_["hid_done"], 1)
                hi_upto(C + 8)
                act.wait_ge(os_["c2_mm"], 1)
                nc.scalar.activation(od.kcT[:, 0:N_CMP], ps[:, 7, 0:N_CMP], ACT.Copy)
                nc.scalar.activation(od.vc[0:N_CMP, :, :], ps[0:N_CMP, 7, 64:192].rearrange("p (g c) -> p g c", g=2),
                                     ACT.Copy).then_inc(os_["c2_read"], 1)
                unit_exp(0)
                kv_chunk(1, 0)
                act.wait_ge(os_["cs_in"], 1)
                nc.scalar.activation(od.pc, od.pc, ACT.Exp).then_inc(os_["cs_exp"], 1)
                kv_chunk(1, 1)
                for u in range(6):
                    for b in range(2):
                        act.wait_ge(os_["p_T"], 3 * u + b + 1)
                        if b == 0 and u >= 2:
                            act.wait_ge(os_["pv_mm"], pv_before(u))
                        nc.scalar.activation(od.pT[u % 2][:, b, :, :], ps[:, 4 + b, :].rearrange("p (h c) -> p h c", h=4),
                                             ACT.Copy).then_inc(os_["pT_act"], 1)
                    if u in (0, 2):
                        weights_read(u)
                    if u < 5:
                        unit_exp(u + 1)
                    kv_chunk(1, u + 2)
                    if u in (0, 2):
                        weights_read(u + 1)
                    if u in PV_AFTER:
                        r = PV_AFTER.index(u)
                        act.wait_ge(os_["pv_mm"], r + 1)
                        nc.scalar.activation(hT_hi[:, 2 * r:2 * r + 2, :],
                                             ps[:, PV_BANK[r], :].rearrange("p (a c) -> p a c", a=2),
                                             ACT.Copy).then_inc(oT_hi_done, 1)

            def unit_exp(u):
                act.wait_ge(os_["nmax_done"], u + 1)
                if u >= 1:
                    act.wait_ge(os_["p_T"], 3 * u)
                for h in range(4):
                    nc.scalar.activation(od.p0[:, h, :], ps[:, 0, h * P:(h + 1) * P], ACT.Exp,
                                         bias=od.nmax[:, h:h + 1],
                                         accum_out=od.rs[:, h:h + 1])
                for h in range(4):
                    ins = nc.scalar.activation(od.p1[:, h, :], ps[:, 1 + h // 2, (h % 2) * SEQ:(h % 2 + 1) * SEQ],
                                               ACT.Exp, bias=od.nmax[:, 4 + h:5 + h],
                                               accum_out=od.rs[:, 4 + h:5 + h])
                if u >= 4:
                    ins = nc.scalar.activation(od.es, od.es, ACT.Exp)
                ins.then_inc(os_["p_exp"], 1)

            def mem_rows_done():
                squares(1, mem_rows, lambda t, h: act.wait_ge(mem_in, 16))
                act.wait_ge(small_in, SMALL)
                act.wait_ge(small_w_set, 1)
                nc.scalar.activation(small_w_hi[:, :], small_w, ACT.Copy)
                nc.scalar.activation(masks[:, :], masks_f, ACT.Copy).then_inc(consts_made, 1)

            act.dma_start(consts[:, 0:P], d["consts"][:, 0:P]).then_inc(ident_in, 16)
            norm(0, 0)
            ffn(0, 0)
            norm(0, 1)
            hi_upto(at["even", "x0"] + 3)
            even()
            hi_upto(at["wq", 0, 0] + 2)
            norm(0, 2)
            cross(0)
            norm(0, 3)
            ffn(0, 1)
            norm(1, 0)
            ffn(1, 0)
            norm(1, 1)
            hi_upto(at["odd", ODD_ORDER[0]] + 3)
            odd()
            hi_upto(at["wq", 1, 0] + 2)
            norm(1, 2)
            cross(1)
            norm(1, 3)
            ffn(1, 1)
            squares(9, x, lambda t, h: act.wait_ge(x_added, 4 * 7 + 2 * t + h + 1))

        @block.vector
        def _(dve):
            made, steps, r = [0], [0], [0]
            V = nc.vector

            def step(ins):
                steps[0] += 1
                ins.then_inc(dve_step, 1)
                dve.wait_ge(dve_step, steps[0])

            def lo_upto(limit):
                for n in range(made[0], min(limit, n_chunks)):
                    dve.wait_ge(hi_done, n + 1)
                    V.tensor_tensor(w_lo[:, n % RING, :], raw[:, n % RING, :],
                                    w_hi[:, n % RING, :].bitcast(F32), ALU.subtract).then_inc(lo_done, 1)
                    made[0] = n + 1

            def norm_rows(v):
                src = mem_rows if v == 1 else x
                dve.wait_ge(norm_w_in, 16 * (v + 1))
                for t in range(TT):
                    dve.wait_ge(rstd_done, 2 * v + t + 1)
                    if v == 1:
                        dve.wait_ge(transposed, 2 * t + 2)
                    for h in range(2):
                        hs = slice(h * 512, (h + 1) * 512)
                        V.scalar_tensor_tensor(xn[:, t, hs], src[:, t, hs], rstd[:, t:t + 1], norm_w[:, hs],
                                               ALU.mult, ALU.mult).then_inc(xn_done, 1)

            def evac_lo(w, hi, lo, tiles=(0, 1)):
                for t in tiles:
                    for kh in range(2):
                        dve.wait_ge(hT_hi_done, 4 * w + 2 * t + kh + 1)
                        ks, ts = slice(4 * kh, 4 * kh + 4), slice(t * P, (t + 1) * P)
                        V.tensor_tensor(lo[:, ks, ts], ps[:, row_bank(w, t, kh), :].rearrange("p (k c) -> p k c", c=P),
                                        hi[:, ks, ts].bitcast(F32), ALU.subtract).then_inc(hT_done, 1)

            def norm(layer, i):
                norm_rows(norm_no(layer, i))
                evac_lo(SETS["norm", layer, i], hT_hi, hT_lo)

            def oT_lo(count, k0, bank):
                dve.wait_ge(oT_hi_done, count)
                V.tensor_tensor(hT_lo[:, k0:k0 + 2, :], ps[:, bank, :].rearrange("p (a c) -> p a c", a=2),
                                hT_hi[:, k0:k0 + 2, :].bitcast(F32), ALU.subtract).then_inc(oT_done, 1)

            def add_residual(last_chunk, coef):
                r[0] += 1
                for t in range(TT):
                    for h in range(2):
                        if t == 0 or h == 0:
                            dve.wait_ge(row_done, 3 * (r[0] - 1) + 2 * t + h + 1)
                        else:
                            dve.wait_ge(chunks_used, last_chunk + 1)
                        xs = x[:, t, h * 512:(h + 1) * 512]
                        V.scalar_tensor_tensor(xs, ps[:, 4 + 2 * t + h, :], coef, xs,
                                               ALU.mult, ALU.add).then_inc(x_added, 1)

            def ffn(layer, which):
                f, base = 2 * layer + which, at["ffn", layer, which]

                def product(j, used):
                    dve.wait_ge(silu_done, j + (f * FJ + 1))
                    dve.wait_ge(chunks_used, used)
                    V.tensor_tensor(gu, g_act, ps[:, 1, :], ALU.mult).then_inc(mult_done, 1)

                def hidden_lo(j, hi, lo):
                    dve.wait_ge(gu_hi_done, j + (f * FJ + 1))
                    V.tensor_tensor(lo, gu.rearrange("p (k c) -> p k c", k=2), hi.bitcast(F32),
                                    ALU.subtract).then_inc(gu_done, 1)

                def turn(j, between=lambda c: None):
                    for c in range(3):
                        m = base + 2 + c + RING
                        if c == 1:
                            dve.wait_ge(gu_done, j + f * FJ)
                            product(j, j * 3 + (base + 1))
                        if c == 2:
                            hidden_lo(j, gu_hi, gu_lo)
                        dve.wait_ge(hi_done, (j - 1) * 3 + (m + 1))
                        V.tensor_tensor(w_lo[:, m % RING, :], raw[:, m % RING, :],
                                        w_hi[:, m % RING, :].bitcast(F32), ALU.subtract).then_inc(lo_done, 1)
                        between(c)

                lo_upto(base + 4)
                product(0, base + 2)
                lo_upto(base + 5)
                hidden_lo(0, gu_hi, gu_lo)
                if f == 0:
                    turn(1)
                    mem_rows_done()
                    turn(2, lambda c: c < 2 and evac_lo(SETS["mem"], memT_hi, memT_lo, tiles=(c,)))
                with dve.Fori(1 if f else 3, FJ - 1) as j:
                    turn(j)
                made[0] = base + FFN_CHUNKS - 1
                j = FJ - 1
                dve.wait_ge(gu_done, j + f * FJ)
                lo_upto(base + FFN_CHUNKS)
                product(j, j * 3 + base + 1)
                hidden_lo(j, gu_hi_last, gu_lo_last)
                lo_upto(base + FFN_CHUNKS + 1)
                add_residual(base + FFN_CHUNKS - 1, 0.5)

            def cross(layer):
                u = 4 * layer
                wq, wo = at["wq", layer, 0], at["wo", layer, 0]
                for i in range(3):
                    lo_upto(wq + i + 4)
                for h in range(XH):
                    dve.wait_ge(xs_["s_mm"], u + h + 1)
                    V.tensor_reduce(cr.nmax[:, 2 * h:2 * h + 2], ps[:, 4 + h, :].rearrange("p (t c) -> p t c", t=2),
                                    axis=AX.X, op=ALU.max, negate=True).then_inc(xs_["nmax"], 1)
                for h in range(XH):
                    dve.wait_ge(xs_["p_exp"], 2 * (u + h + 1))
                    step(V.reciprocal(cr.fac[:, 2 * h:2 * h + 2], cr.rs[:, 2 * h:2 * h + 2]))
                    V.tensor_tensor(cr.p[:, h, :, :], cr.p[:, h, :, :],
                                    cr.fac[:, 2 * h:2 * h + 2].unsqueeze(2).to_broadcast([P, 2, MEM]),
                                    ALU.mult).then_inc(xs_["p_done"], 1)
                for h in range(XH):
                    oT_lo(OT_BASE[f"cross{layer}"] + h + 1, 2 * h, h)
                lo_upto(wo + 5)
                add_residual(wo + 3, 1.0)

            def rotate(e, i):
                E = at["even", "x0"]
                dve.wait_ge(chunks_used, E + e + 1)
                if i:
                    dve.wait_ge(es["rot_done"], i)
                pair = ps[:, e % 3, :].rearrange("p (t h i two) -> p t h i two", t=TT, h=2, two=2)
                cosr, sinr = const("cos", TT, 64), const("sin", TT, 64)
                for t in range(TT):
                    c, s = (v[:, t, :].unsqueeze(1).to_broadcast([P, 2, 64]) for v in (cosr, sinr))
                    for r, (which, table) in enumerate(((0, c), (1, s), (0, s), (1, c))):
                        ins = V.tensor_tensor(ev.rot[r][:, t, :, :],
                                              pair[:, t, :, :, which], table, ALU.mult)
                ins.then_inc(es["rot_read"], 1)

            def even():
                E = at["even", "x0"]
                dve.wait_ge(es["dt_mm"], 1)
                V.tensor_copy(ev.dtT[0:SSM_H, :], ps[0:SSM_H, 3, 0:SEQ]).then_inc(es["dtT_done"], 1)
                for c in range(3):
                    dve.wait_ge(es["act_read"], c + 1)
                    for tap in (2, 1, 0):
                        for m in range(2):
                            k = 2 * c + m
                            ins = V.scalar_tensor_tensor(ev.xbcT[:, k, :], ev.xpad[:, k, tap:tap + SEQ],
                                                         conv_w[:, tap, k:k + 1], ev.xbcT[:, k, :],
                                                         ALU.mult, ALU.add)
                            if tap:
                                if m:
                                    step(ins)
                            elif m:
                                ins.then_inc(es["conv_done"], 1)
                    lo_upto(E + c + 4)
                    if c == 0:
                        dve.wait_ge(es["dt_T"], 1)
                        V.tensor_tensor(ev.dtr.rearrange("p (t h) -> p t h", t=TT),
                                        ps[:, 3, SEQ:SEQ + 16].rearrange("p (t h) -> p t h", t=TT),
                                        head_rows[:, 0, :].unsqueeze(1).to_broadcast([P, TT, SSM_H]),
                                        ALU.add).then_inc(es["dt_raw"], 1)
                dve.wait_ge(es["ln_done"], 1)
                step(V.scalar_tensor_tensor(ev.dt, ev.dtr, 0.0, ev.ln1p, ALU.max, ALU.add))
                dve.wait_ge(es["ea_done"], 1)
                V.scalar_tensor_tensor(ev.dta.rearrange("p (t h) -> p t h", t=TT),
                                       ev.dt.rearrange("p (t h) -> p t h", t=TT), -1.0,
                                       ev.ea.unsqueeze(1).to_broadcast([P, TT, SSM_H]),
                                       ALU.mult, ALU.mult).then_inc(es["dta_done"], 1)
                for i in range(4):
                    rotate(3 + i, i)
                    lo_upto(E + 3 + i + 4)
                dve.wait_ge(es["xh_done"], TT)
                dve.wait_ge(es["rot_done"], 4)
                V.tensor_tensor(ev.xdt.rearrange("p t h c -> p (t h) c"), ev.xh.rearrange("p t h c -> p (t h) c"),
                                ev.dt.unsqueeze(2).to_broadcast([P, TT * SSM_H, HP]),
                                ALU.mult).then_inc(es["xdt_done"], 1)
                lo_upto(E + 7 + 4)
                for g in range(2):
                    dve.wait_ge(es["cb_mm"], g + 1)
                    V.tensor_tensor(ev.cbm[:, :, g, :], ps[:, 6 + g, 0:2 * P].rearrange("p (c l) -> p c l", c=TT),
                                    const("upto").unsqueeze(1).to_broadcast([P, TT, P]),
                                    ALU.mult).then_inc(es["cbm_done"], 1)
                lo_upto(E + 8 + 4)
                for q in range(4):
                    dve.wait_ge(es["seg_exp"], q + 1)
                    m = ev.mt[:, q // 2, 4 * (q % 2):4 * (q % 2) + 4, :]
                    V.tensor_tensor(m, m, ev.cbm[:, q // 2, q % 2, :].unsqueeze(1).to_broadcast([P, 4, P]),
                                    ALU.mult).then_inc(es["mt_done"], 1)
                dve.wait_ge(es["dec_done"], 1)
                V.tensor_tensor(ev.xdtd, ev.xdt[:, 0, :, :], ev.dec.unsqueeze(2).to_broadcast([P, SSM_H, HP]),
                                ALU.mult).then_inc(es["xdtd_done"], 1)
                for e in range(9, 13):
                    lo_upto(E + e + 4)
                dve.wait_ge(es["qkT_done"], 4)
                dve.wait_ge(es["kz_done"], 1)
                for t, bank in enumerate((7, 1)):
                    dve.wait_ge(es["ret_s_mm"], t + 1)
                    V.tensor_tensor(ev.s[:, t, :, :], ps[:, bank, :].rearrange("p (h i) -> p h i", h=RET_H),
                                    const("decayT", RET_H, P), ALU.mult).then_inc(es["s_done"], 1)
                dve.wait_ge(es["dx_done"], 1)
                hc = "p (h c) -> p h c"
                dve.wait_ge(es["y_mm"], 1)
                step(V.tensor_tensor(ev.xh[:, 0, :, :], ev.xh[:, 0, :, :], ps[:, 4, :].rearrange(hc, h=SSM_H), ALU.add))
                dve.wait_ge(es["act_read"], 9)
                V.tensor_tensor(ev.xh[:, 0, :, :], ev.xh[:, 0, :, :], xn[:, 0, 512:].rearrange(hc, h=SSM_H),
                                ALU.mult).then_inc(es["y_ready"], 1)
                dve.wait_ge(es["y_mm"], 2)
                step(V.tensor_tensor(ev.xh[:, 1, :, :], ev.xh[:, 1, :, :], ps[:, 5, :].rearrange(hc, h=SSM_H), ALU.add))
                dve.wait_ge(es["yoff_mm"], 1)
                for g, bank in enumerate((0, 2)):
                    ins = V.tensor_tensor(ev.yc[:, 4 * g:4 * g + 4, :], ps[:, bank, 0:256].rearrange(hc, h=4),
                                          ev.cum[:, 4 * g:4 * g + 4].unsqueeze(2).to_broadcast([P, 4, HP]), ALU.mult)
                step(ins)
                step(V.tensor_tensor(ev.xh[:, 1, :, :], ev.xh[:, 1, :, :], ev.yc, ALU.add))
                V.tensor_tensor(ev.xh[:, 1, :, :], ev.xh[:, 1, :, :], xn[:, 1, 512:].rearrange(hc, h=SSM_H),
                                ALU.mult).then_inc(es["y_ready"], 1)
                lo_upto(at["kv", 0, 0] + 4)
                dve.wait_ge(es["o_mm"], 1)
                V.tensor_copy(ev.o[:, 0, :, :], ps[:, 7, :].rearrange("p (h e) -> p h e", h=RET_H))\
                 .then_inc(es["y_read"], 1)
                dve.wait_ge(es["o_mm"], 2)
                step(V.tensor_tensor(ev.o[:, 1, :, :], ps[:, 4, :].rearrange("p (h e) -> p h e", h=RET_H),
                                     const("xi").unsqueeze(2).to_broadcast([P, RET_H, P]), ALU.mult))
                V.tensor_tensor(ev.o[:, 1, :, :], ev.o[:, 1, :, :], ps[:, 1, :].rearrange("p (h e) -> p h e", h=RET_H),
                                ALU.add).then_inc(es["o_read"], 1)
                dve.wait_ge(es["o_sq"], 1)
                V.tensor_reduce(ev.osq.rearrange("p (t h) -> p t h", t=TT),
                                ev.mt[:, :, 0:4, :], axis=AX.X, op=ALU.add).then_inc(es["o_ssq"], 1)
                lo_upto(at["kv", 0, 1] + 4)
                dve.wait_ge(es["y_rstd"], 1)
                for t in range(TT):
                    V.scalar_tensor_tensor(xn[:, t, 512:], ev.xh[:, t, :, :].rearrange("p h c -> p (h c)"),
                                           ev.rsr[:, t:t + 1], ssm_nw[:, :], ALU.mult, ALU.mult)
                dve.wait_ge(es["o_rstd"], 1)
                for t in range(TT):
                    ins = V.tensor_tensor(ev.o[:, t, :, :], ev.o[:, t, :, :],
                                          ev.ors[:, 4 * t:4 * t + 4].unsqueeze(2).to_broadcast([P, RET_H, P]), ALU.mult)
                step(ins)
                for t in range(TT):
                    g = xn[:, t, 0:512]
                    V.tensor_tensor(g, g, ev.o[:, t, :, :].rearrange("p h e -> p (h e)"), ALU.mult)\
                     .then_inc(es["mix_done"], 1)
                for i in range(2, 6):
                    lo_upto(at["kv", 0, i] + 3)
                evac_lo(SETS["mix0"], hT_hi, hT_lo)
                lo_upto(at["mixout", 0, 3] + 2)
                add_residual(at["mixout", 0, 3], 1.0)

            def odd():
                C = at["cmp", 0]
                for c, name in enumerate(ODD_ORDER):
                    lo_upto(at["odd", name] + 4)
                    if c == 2:
                        dve.wait_ge(os_["gates_done"], 1)
                        step(V.tensor_scalar(od.gates, od.gates, 1.0, None, ALU.add))
                        step(V.reciprocal(od.gates, od.gates))
                    if c == 4:
                        compress_in()
                lo_upto(C + 7)
                unit(0)
                lo_upto(C + 8)
                cm, cb = const("cmpmask", TT, N_CMP), const("cmpbias", TT, N_CMP)
                dve.wait_ge(os_["cs_mm"], 1)
                for g in range(2):
                    for t in range(TT):
                        ins = V.tensor_tensor(od.pc[:, t, 4 * g:4 * g + 4, :],
                                              ps[:, 4 + g, t * 64:t * 64 + 60].rearrange("p (h n) -> p h n", h=4),
                                              cm[:, t, :].unsqueeze(1).to_broadcast([P, 4, N_CMP]), ALU.mult)
                step(ins)
                for t in range(TT):
                    ins = V.tensor_tensor(od.pc[:, t, :, :], od.pc[:, t, :, :],
                                          cb[:, t, :].unsqueeze(1).to_broadcast([P, NH, N_CMP]), ALU.add)
                step(ins)
                pcf = od.pc.rearrange("p t h n -> p (t h) n")
                step(V.tensor_reduce(od.cmax, pcf, axis=AX.X, op=ALU.max, negate=True))
                V.tensor_tensor(pcf, pcf, od.cmax.unsqueeze(2).to_broadcast([P, 16, N_CMP]), ALU.add)\
                 .then_inc(os_["cs_in"], 1)
                dve.wait_ge(os_["cs_exp"], 1)
                for t in range(TT):
                    ins = V.tensor_tensor(od.pc[:, t, :, :], od.pc[:, t, :, :],
                                          cm[:, t, :].unsqueeze(1).to_broadcast([P, NH, N_CMP]), ALU.mult)
                step(ins)
                step(V.tensor_reduce(od.csum, pcf, axis=AX.X, op=ALU.add))
                step(V.tensor_scalar(od.csum, od.csum, 1e-30, None, ALU.max))
                step(V.reciprocal(od.csum, od.csum))
                g3 = od.gates.rearrange("p (q b) -> p q b", b=3)
                step(V.tensor_tensor(od.csum, od.csum, g3[:, :, 0], ALU.mult))
                V.tensor_tensor(pcf, pcf, od.csum.unsqueeze(2).to_broadcast([P, 16, N_CMP]), ALU.mult)\
                 .then_inc(os_["pc_done"], 1)
                lo_upto(at["kv", 1, 1] + 4)
                for u in range(6):
                    dve.wait_ge(os_["p_T"], 3 * u + 3)
                    if u >= 2:
                        dve.wait_ge(os_["pv_mm"], pv_before(u))
                    V.tensor_copy(od.pT[u % 2][:, 2, :, :], ps[:, 6, :].rearrange("p (h c) -> p h c", h=4))\
                     .then_inc(os_["pT_dve"], 1)
                    if u < 5:
                        unit(u + 1)
                    lo_upto(at["kv", 1, u + 2] + 4)
                    if u in PV_AFTER:
                        r = PV_AFTER.index(u)
                        oT_lo(OT_BASE["odd"] + r + 1, 2 * r, PV_BANK[r])
                lo_upto(at["mixout", 1, 3] + 2)
                add_residual(at["mixout", 1, 3], 1.0)

            def unit(u):
                a, g = UNITS[u]
                dve.wait_ge(os_["s_mm"], u + 1)
                V.tensor_reduce(od.nmax2[:, 0:4], ps[:, 0, :].rearrange("p (h c) -> p h c", h=4),
                                axis=AX.X, op=ALU.max, negate=True)
                ins = V.tensor_reduce(od.nmax2[:, 4:8], ps[:, 1:3, :].rearrange("p b (h c) -> p (b h) c", h=2),
                                      axis=AX.X, op=ALU.max, negate=True)
                step(ins)
                nm = od.nmax.rearrange("p (t h) -> p t h", t=TT)
                nm2 = od.nmax2.rearrange("p (t h) -> p t h", t=TT)
                if a == 2:
                    sink = head_rows[:, 3, 4 * g:4 * g + 4].unsqueeze(1).to_broadcast([P, TT, 4])
                    step(V.scalar_tensor_tensor(nm, sink, -1.0, nm2, ALU.mult, ALU.min))
                    V.tensor_tensor(od.es.rearrange("p (t h) -> p t h", t=TT), nm, sink, ALU.add)\
                     .then_inc(os_["nmax_done"], 1)
                else:
                    V.tensor_copy(od.nmax, od.nmax2).then_inc(os_["nmax_done"], 1)
                dve.wait_ge(os_["p_exp"], u + 1)
                if a == 2:
                    step(V.tensor_tensor(od.rs, od.rs, od.es, ALU.add))
                step(V.reciprocal(od.fac, od.rs))
                if a < 2:
                    gate = od.gates.rearrange("p (t h b) -> p t h b", t=TT, b=3)[:, :, 4 * g:4 * g + 4, 1 + a]
                    fac = od.fac.rearrange("p (t h) -> p t h", t=TT)
                    step(V.tensor_tensor(fac, fac, gate, ALU.mult))
                V.tensor_tensor(od.p0, od.p0, od.fac[:, 0:4].unsqueeze(2).to_broadcast([P, 4, P]), ALU.mult)
                V.tensor_tensor(od.p1, od.p1, od.fac[:, 4:8].unsqueeze(2).to_broadcast([P, 4, SEQ]),
                                ALU.mult).then_inc(os_["p_done"], 1)

            def compress_in():
                dve.wait_ge(os_["pick_mm"], 1)
                for kv in range(2):
                    pairs = ps[:, 4, kv * 256:(kv + 1) * 256].rearrange("p (g n i) -> p g n i", g=2, i=8)
                    for half in range(2):
                        for g in range(2):
                            ins = V.tensor_tensor(
                                od.xc[:, kv, 8 * half:8 * half + 8, g, :],
                                pairs[:, g, half:half + N_CMP, :].rearrange("p n i -> p i n"),
                                pe_pairs[:, kv, 8 * half:8 * half + 8].unsqueeze(2).to_broadcast([P, 8, N_CMP]),
                                ALU.add)
                ins.then_inc(os_["xc_done"], 1)
                dve.wait_ge(os_["xc_hi_done"], 1)
                V.tensor_tensor(od.xc_lo, od.xc.rearrange("p k i g n -> p (k i g n)"), od.xc_hi.bitcast(F32),
                                ALU.subtract).then_inc(os_["xc_lo_done"], 1)

            def mem_rows_done():
                norm_rows(1)
                dve.wait_ge(consts_made, 1)
                V.tensor_tensor(small_w_lo[:, :], small_w, small_w_hi[:, :].bitcast(F32),
                                ALU.subtract).then_inc(smalls_split, 1)

            norm(0, 0)
            ffn(0, 0)
            norm(0, 1)
            lo_upto(at["even", "x0"] + 3)
            even()
            norm(0, 2)
            lo_upto(at["wq", 0, 0] + 3)
            cross(0)
            norm(0, 3)
            ffn(0, 1)
            norm(1, 0)
            ffn(1, 0)
            norm(1, 1)
            lo_upto(at["odd", ODD_ORDER[0]] + 3)
            odd()
            norm(1, 2)
            lo_upto(at["wq", 1, 0] + 3)
            cross(1)
            norm(1, 3)
            ffn(1, 1)
            norm_rows(9)

        @block.gpsimd
        def _(pool):
            G = nc.gpsimd
            steps = [0]

            def step(ins):
                steps[0] += 1
                ins.then_inc(pool_step, 1)
                pool.wait_ge(pool_step, steps[0])

            def load_norm_w(v):
                if v:
                    pool.wait_ge(xn_done, 4 * v)
                src = d["mem_norm_w"] if v == 1 else d["final_norm_w"] if v == 9 else \
                    d["norm_w"][(v - 1) // 4, (v - 1) % 4] if v else d["norm_w"][0, 0]
                pool.dma_start(norm_w[:, :], src.partition_broadcast(P)).then_inc(norm_w_in, 16)

            def inv_rms(dst, tmp, src, width, count):
                step(G.tensor_scalar(tmp, src, 1.0 / count, EPS, ALU.mult, ALU.add))
                return G.tensor_tensor(dst, tmp, neg_half[:, 0:width], ALU.pow)

            def norm(v):
                for t in range(TT):
                    pool.wait_ge(sq_done, 4 * v + 2 * t + 2)
                    step(G.tensor_scalar(msq[:, t:t + 1], msum[:, 2 * t:2 * t + 1], msum[:, 2 * t + 1:2 * t + 2], EPS,
                                         ALU.add, ALU.add))
                    G.tensor_tensor(rstd[:, t:t + 1], msq[:, t:t + 1], neg_half[:, 0:1],
                                    ALU.pow).then_inc(rstd_done, 1)
                if v < 9:
                    load_norm_w(v + 1)

            def even():
                pool.wait_ge(x_added, 4)
                G.memset(ev.xpad[:, :, 0:CONV_W - 1], 0.0).then_inc(es["xpad_zero"], 1)
                for i in range(4):
                    pool.wait_ge(es["rot_read"], i + 1)
                    a, b, c, e = ev.rot
                    dst = ev.q_rot if i < 2 else ev.k_rot
                    for t in range(TT):
                        hs = slice(2 * (i % 2), 2 * (i % 2) + 2)
                        r = [v[:, t, :, :] for v in (a, b, c, e)]
                        G.tensor_tensor(dst[:, t, hs, 0, :], r[0], r[1], ALU.subtract)
                        ins = G.tensor_tensor(dst[:, t, hs, 1, :], r[2], r[3], ALU.add)
                    ins.then_inc(es["rot_done"], 1)
                    if i == 1:
                        seg_weights()
                pool.wait_ge(es["rot_done"], 4)
                G.tensor_tensor(ev.kz, ev.k_rot[:, 0, :, :, :].rearrange("p h a b -> p h (a b)"),
                                const("zeta").unsqueeze(2).to_broadcast([P, RET_H, P]),
                                ALU.mult).then_inc(es["kz_done"], 1)
                pool.wait_ge(es["xdt_done"], 1)
                G.tensor_tensor(ev.xh.rearrange("p t h c -> p t h c")[:, 0], ev.xh[:, 0],
                                head_rows[:, 2, :].unsqueeze(2).to_broadcast([P, SSM_H, HP]), ALU.mult)
                G.tensor_tensor(ev.xh[:, 1], ev.xh[:, 1],
                                head_rows[:, 2, :].unsqueeze(2).to_broadcast([P, SSM_H, HP]),
                                ALU.mult).then_inc(es["dx_done"], 1)
                pool.wait_ge(es["y_sq"], 2)
                inv_rms(ev.rsr, ev.msr, ev.ssr, 2, SSM_IN).then_inc(es["y_rstd"], 1)
                pool.wait_ge(es["o_ssq"], 1)
                inv_rms(ev.ors, ev.oms, ev.osq, 8, DK).then_inc(es["o_rstd"], 1)

            def seg_weights():
                pool.wait_ge(es["conv_done"], 3)
                pool.wait_ge(es["dta_done"], 1)
                for t in range(TT):
                    for h in range(SSM_H):
                        G.tensor_scalar(ev.ld[:, t, h, :], const("after"),
                                        ev.dta[:, 8 * t + h:8 * t + h + 1], None, ALU.mult)\
                         .then_inc(es["ld_done"], 1)

            load_norm_w(0)
            G.memset(neg_half[:, :], -0.5).then_inc(neg_half_set, 1)
            pool.wait_ge(neg_half_set, 1)
            G.memset(small_w[:, SMALL_W - 120:], 0.0).then_inc(small_w_set, 1)
            norm(0)
            norm(1)
            pool.wait_ge(small_in, SMALL)
            norm(2)
            even()
            for v in range(3, 10):
                norm(v)
                if v == norm_no(1, 1):
                    pool.wait_ge(hT_done, 4 * SETS["norm", 1, 1] + 4)
                    G.memset(od.xc_hi_wide[:, 960:].bitcast(F32), 0.0)
                    G.memset(od.xc_lo_wide[:, 960:].bitcast(F32), 0.0).then_inc(os_["xc_tail"], 1)

        @block.tensor
        def _(pe):
            mm = nc.tensor.matmul

            def product3(dst, l_hi, l_lo, r_hi, r_lo, start, stop):
                mm(dst, l_hi, r_hi, start=start, stop=False)
                mm(dst, l_hi, r_lo, start=False, stop=False)
                return mm(dst, l_lo, r_hi, start=False, stop=stop)

            def cols(w, n, k, width, lo, hi):
                return w[:, n % RING, k * width + lo:k * width + hi]

            def to_features(n, dst, a_hi, a_lo, tiles=2, col0=0):
                for m in range(tiles):
                    lo, hi = col0 + m * P, col0 + (m + 1) * P
                    for k in range(KT):
                        last = product3(dst[:, m * SEQ:(m + 1) * SEQ],
                                        cols(w_hi, n, k, CW, lo, hi), cols(w_lo, n, k, CW, lo, hi),
                                        a_hi[:, k, :], a_lo[:, k, :], k == 0, k == KT - 1)
                return last

            def to_tokens(n, dst, width, a_hi, a_lo, col0=0):
                for t in range(TT):
                    ts = slice(t * P, (t + 1) * P)
                    for k in range(KT):
                        last = product3(dst[:, t * width:(t + 1) * width], a_hi[:, k, ts], a_lo[:, k, ts],
                                        cols(w_hi, n, k, CW, col0, col0 + width),
                                        cols(w_lo, n, k, CW, col0, col0 + width), k == 0, k == KT - 1)
                return last

            def down(n, a_hi, a_lo, first, final):
                for t in range(TT):
                    ts = slice(t * P, (t + 1) * P)
                    for h in range(2):
                        for k in range(2):
                            last = product3(ps[:, 4 + 2 * t + h, :], a_hi[:, k, ts], a_lo[:, k, ts],
                                            cols(w_hi, n, k, D, h * 512, (h + 1) * 512),
                                            cols(w_lo, n, k, D, h * 512, (h + 1) * 512),
                                            first and k == 0, final and k == 1)
                        if final and 2 * t + h < 3:
                            last.then_inc(row_done, 1)
                return last

            def used(ins):
                return ins.then_inc(chunks_used, 1)

            def transposes(w, ready, tiles=(0, 1)):
                for t in tiles:
                    for kh in range(2):
                        ready(t, kh)
                        for k in range(4):
                            c = (4 * kh + k) * P
                            last = nc.tensor.transpose(ps[:, row_bank(w, t, kh), k * P:(k + 1) * P],
                                                       xn[:, t, c:c + P], ident)
                        last.then_inc(transposed, 1)

            def mem_turned(t):
                def ready(t, kh):
                    if t == 0:
                        pe.wait_ge(xn_done, 8)
                    else:
                        pe.wait_ge(hT_done, 4 * SETS["mem"] + kh + 1)
                transposes(SETS["mem"], ready, tiles=(t,))

            def norm(v, key):
                transposes(SETS[key], lambda t, kh: pe.wait_ge(xn_done, 4 * v + 2 * t + kh + 1))
                pe.wait_ge(hT_done, 4 * SETS[key] + 4)

            def small_features(w0, width):
                for k in range(KT):
                    c0 = w0 + k * width
                    last = product3(ps[:, 3, 0:SEQ], small_w_hi[:, c0:c0 + P], small_w_lo[:, c0:c0 + P],
                                    hT_hi[:, k, :], hT_lo[:, k, :], k == 0, k == KT - 1)
                return last

            def small_tokens(src, width):
                for t in range(TT):
                    c0 = SEQ + t * width
                    last = nc.tensor.transpose(ps[:, 3, c0:c0 + width], src[0:width, t * P:(t + 1) * P],
                                               ident[0:width, 0:width])
                return last

            def ffn(layer, which):
                f, base = 2 * layer + which, at["ffn", layer, which]

                def hidden_down(j, n, first, final):
                    pe.wait_ge(gu_done, j)
                    used(down(n, gu_hi_last if final else gu_hi, gu_lo_last if final else gu_lo, first, final))

                pe.wait_ge(lo_done, base + 1)
                used(to_features(base, ps[:, 0, :], hT_hi, hT_lo))
                pe.wait_ge(lo_done, base + 2)
                used(to_features(base + 1, ps[:, 1, :], hT_hi, hT_lo))

                def turn(j, first, between=lambda c: None):
                    n = base + 2
                    pe.wait_ge(silu_done, j + f * FJ)
                    pe.wait_ge(lo_done, j * 3 + (n + 1 - 3))
                    used(to_features(n, ps[:, 0, :], hT_hi, hT_lo))
                    between(0)
                    pe.wait_ge(mult_done, j + f * FJ)
                    pe.wait_ge(lo_done, j * 3 + (n + 2 - 3))
                    used(to_features(n + 1, ps[:, 1, :], hT_hi, hT_lo))
                    between(1)
                    pe.wait_ge(lo_done, j * 3 + (n + 3 - 3))
                    hidden_down(j + f * FJ, n + 2, first, False)

                turn(1, True)
                if f == 0:
                    turn(2, False, mem_turned)
                with pe.Fori(2 if f else 3, FJ) as j:
                    turn(j, False)
                n = base + FFN_CHUNKS - 1
                pe.wait_ge(lo_done, n + 1)
                hidden_down((f + 1) * FJ, n, False, True)

            def kv_chunk(layer, i):
                n, bank = at["kv", layer, i], KV_BANK[layer][i]
                pe.wait_ge(lo_done, n + 1)
                before = [m for m in range(i) if KV_BANK[layer][m] == bank]
                if before:
                    pe.wait_ge(kv_read, 8 * layer + before[-1] + 1)
                if i < 4:
                    used(to_features(n, ps[:, bank, :], memT_hi, memT_lo))
                else:
                    used(to_tokens(n, ps[:, bank, :], CW, memT_hi, memT_lo))

            def out_chunks(first_n, waits=None):
                for i in range(4):
                    if waits:
                        waits(i)
                    pe.wait_ge(lo_done, first_n + i + 1)
                    used(down(first_n + i, hT_hi[:, 2 * i:2 * i + 2, :], hT_lo[:, 2 * i:2 * i + 2, :],
                              i == 0, i == 3))

            def cross(layer):
                u = 4 * layer
                wq, wo = at["wq", layer, 0], at["wo", layer, 0]

                def project(i):
                    pe.wait_ge(lo_done, wq + i + 1)
                    if i == 3:
                        pe.wait_ge(xs_["q_read"], u + 1)
                    used(to_features(wq + i, ps[:, i % 3, :], hT_hi, hT_lo))

                def scores(h):
                    pe.wait_ge(xs_["q_read"], u + h + 1)
                    pe.wait_ge(kv_read, 8 * layer + 8)
                    for t in range(TT):
                        for k in range(2):
                            last = mm(ps[:, 4 + h, t * MEM:(t + 1) * MEM],
                                      cr.q[:, 2 * h + k, t * P:(t + 1) * P], xk[:, 2 * h + k, :],
                                      start=k == 0, stop=k == 1)
                    last.then_inc(xs_["s_mm"], 1)

                def turned(h):
                    pe.wait_ge(xs_["p_done"], u + h + 1)
                    pe.wait_ge(xs_["q_read"], u + 4)
                    if h == 3:
                        pe.wait_ge(xs_["pT_done"], u + 1)
                    bank = (3, 1, 2, 3)[h]
                    for kb in range(2):
                        for t in range(TT):
                            last = nc.tensor.transpose(ps[:, bank, kb * SEQ + t * P:kb * SEQ + (t + 1) * P],
                                                       cr.p[:, h, t, kb * P:(kb + 1) * P], ident)
                    last.then_inc(xs_["p_T"], 1)

                def values(h):
                    pe.wait_ge(xs_["pT_done"], u + h + 1)
                    for m in range(2):
                        for kb in range(2):
                            last = mm(ps[:, h, m * SEQ:(m + 1) * SEQ],
                                      xv[:, kb, h * XD + m * P:h * XD + (m + 1) * P], cr.pT[:, h, kb, :],
                                      start=kb == 0, stop=kb == 1)
                    last.then_inc(xs_["pv_mm"], 1)

                project(0)
                project(1)
                scores(0)
                project(2)
                scores(1)
                project(3)
                scores(2)
                scores(3)
                for h in range(XH):
                    turned(h)
                    if h:
                        values(h - 1)
                values(XH - 1)
                b = OT_BASE[f"cross{layer}"]
                out_chunks(wo, lambda i: pe.wait_ge(oT_done, b + i + 1))

            def even():
                E = at["even", "x0"]

                def project(e, bank_free=None):
                    n = E + e
                    pe.wait_ge(lo_done, n + 1)
                    if bank_free:
                        pe.wait_ge(es[bank_free[0]], bank_free[1])
                    if e < 3:
                        used(to_features(n, ps[:, e % 3, :], hT_hi, hT_lo))
                    else:
                        used(to_tokens(n, ps[:, e % 3, :], CW, hT_hi, hT_lo))

                small_features(DT_AT, SSM_H).then_inc(es["dt_mm"], 1)
                project(0)
                pe.wait_ge(es["dtT_done"], 1)
                small_tokens(ev.dtT, SSM_H).then_inc(es["dt_T"], 1)
                project(1)
                project(2)
                project(3, ("act_read", 1))
                project(4, ("act_read", 2))
                project(5, ("act_read", 3))
                project(6, ("rot_read", 1))
                pe.wait_ge(es["xbc_done"], 3)
                pe.wait_ge(es["dt_raw"], 1)
                for t in range(TT):
                    for k in range(4):
                        last = nc.tensor.transpose(ps[:, 4 + t, k * P:(k + 1) * P],
                                                   ev.xbcT[:, k, t * P:(t + 1) * P], ident)
                    last.then_inc(es["xs_T"], 1)
                nc.tensor.transpose(ps[:, 3, 0:P], ev.xbcT[:, 4, 0:P], ident).then_inc(es["xs_T"], 1)
                for g in range(2):
                    gs = slice(64 * g, 64 * g + 64)
                    for c in range(TT):
                        cs = slice(c * P, (c + 1) * P)
                        last = mm(ps[:, 6 + g, cs], ev.xbcT[gs, 4, cs], ev.xbcT[gs, 5, cs], start=True, stop=True)
                    last.then_inc(es["cb_mm"], 1)
                project(7, ("rot_read", 2))
                pe.wait_ge(es["dta_done"], 1)
                pe.wait_ge(es["xh_done"], 3)
                mm(ps[:, 3, P:P + 8], const("after"), ev.dta[:, 0:8], start=True, stop=True)
                mm(ps[:, 3, P + 8:P + 16], const("upto"), ev.dta[:, 8:16], start=True, stop=True)\
                    .then_inc(es["dec_mm"], 1)
                for q in range(4):
                    pe.wait_ge(es["ld_done"], 4 * q + 4)
                    if q == 2:
                        pe.wait_ge(es["cbm_done"], 2)
                    for h in range(4):
                        last = mm(ps[:, 4 + q, h * P:(h + 1) * P], ev.ld[:, q // 2, 4 * (q % 2) + h, :],
                                  const("upto"), start=True, stop=True)
                    last.then_inc(es["seg_mm"], 1)
                project(8, ("rot_read", 3))
                project(9, ("rot_read", 4))
                project(10, ("act_read", 4))
                pe.wait_ge(es["rot_done"], 4)
                for i, src in enumerate((ev.q_rot, ev.k_rot)):
                    for t in range(TT):
                        pe.wait_ge(es["seg_exp"], 2 * i + t + 1)
                        for h in range(RET_H):
                            last = nc.tensor.transpose(ps[:, 4 + 2 * i + t, h * P:(h + 1) * P],
                                                       src[:, t, h, :, :].rearrange("p a b -> p (a b)"), ident)
                        last.then_inc(es["qk_T"], 1)
                project(11, ("act_read", 5))
                project(12, ("act_read", 6))
                for t in range(TT):
                    pe.wait_ge(es["mt_done"], 2 * t + 2)
                    pe.wait_ge(es["qkT_done"], t + 1)
                    for h in range(SSM_H):
                        last = mm(ps[:, 4 + t, h * HP:(h + 1) * HP], ev.mt[:, t, h, :], ev.xdt[:, t, h, :],
                                  start=True, stop=True)
                    last.then_inc(es["y_mm"], 1)
                pe.wait_ge(es["xdtd_done"], 1)
                pe.wait_ge(es["qkT_done"], 4)
                mm(ps[:, 6, :], ev.b_tok, ev.xdtd.rearrange("p h c -> p (h c)"), start=True, stop=True)\
                    .then_inc(es["st_mm"], 1)
                for t, bank in enumerate((7, 1)):
                    if t:
                        pe.wait_ge(es["act_read"], 7)
                    for h in range(RET_H):
                        last = mm(ps[:, bank, h * P:(h + 1) * P], ev.kT[:, t, h, :], ev.qT[:, t, h, :],
                                  start=True, stop=True)
                    last.then_inc(es["ret_s_mm"], 1)
                pe.wait_ge(es["dec_done"], 1)
                kv_chunk(0, 0)
                pe.wait_ge(es["st_done"], 1)
                pe.wait_ge(es["act_read"], 9)
                for g, bank in enumerate((0, 2)):
                    gs = slice(64 * g, 64 * g + 64)
                    last = mm(ps[:, bank, 0:256], ev.xbcT[gs, 5, P:2 * P], ev.sT[gs, 256 * g:256 * g + 256],
                              start=True, stop=True)
                last.then_inc(es["yoff_mm"], 1)
                pe.wait_ge(es["kz_done"], 1)
                for h in range(RET_H):
                    last = mm(ps[:, 6, h * P:(h + 1) * P], ev.kz[:, h, :], ev.v[:, 0, h * P:(h + 1) * P],
                              start=True, stop=True)
                last.then_inc(es["ret_kv_mm"], 1)
                kv_chunk(0, 1)
                for t, bank in enumerate((7, 1)):
                    pe.wait_ge(es["s_done"], t + 1)
                    for h in range(RET_H):
                        last = mm(ps[:, bank, h * P:(h + 1) * P], ev.s[:, t, h, :], ev.v[:, t, h * P:(h + 1) * P],
                                  start=True, stop=True)
                    if t == 0:
                        last.then_inc(es["o_mm"], 1)
                pe.wait_ge(es["kvs_done"], 1)
                pe.wait_ge(es["y_ready"], 1)
                for h in range(RET_H):
                    last = mm(ps[:, 4, h * P:(h + 1) * P], ev.qT[:, 1, h, :], ev.kv[:, h, :], start=True, stop=True)
                last.then_inc(es["o_mm"], 1)
                pe.wait_ge(es["y_ready"], 2)
                for i in range(2, 6):
                    kv_chunk(0, i)
                pe.wait_ge(kv_read, 2)
                transposes(SETS["mix0"], lambda t, kh: pe.wait_ge(es["mix_done"], t + 1))
                kv_chunk(0, 6)
                pe.wait_ge(hT_done, 4 * SETS["mix0"] + 4)
                kv_chunk(0, 7)
                pe.wait_ge(kv_read, 7)
                out_chunks(at["mixout", 0, 0])

            def odd():
                def project(name, bank):
                    n = at["odd", name]
                    pe.wait_ge(lo_done, n + 1)
                    if name[0] == "q":
                        last = to_features(n, bank, hT_hi, hT_lo)
                    elif name == "c":
                        last = to_tokens(n, bank, CW, hT_hi, hT_lo)
                    else:
                        to_features(n, bank, hT_hi, hT_lo, tiles=1)
                        last = to_tokens(n, bank[:, SEQ:], P, hT_hi, hT_lo, col0=P)
                    used(last)

                def weights_turned(b):
                    for i in range(2):
                        for t in range(TT):
                            last = nc.tensor.transpose(ps[0:N_CMP, 7, i * SEQ + t * P:i * SEQ + (t + 1) * P],
                                                       od.pc[:, t, 2 * b + i, :], ident)
                    last.then_inc(os_["pc_T"], 1)

                small_features(GATE_AT, 3 * NH).then_inc(os_["gate_mm"], 1)
                for c, name in enumerate(ODD_ORDER):
                    if c >= 3:
                        pe.wait_ge(os_["read"], c - 2)
                    project(name, ps[:, c % 3, :])
                    if c == 1:
                        pe.wait_ge(os_["gT_done"], 1)
                        small_tokens(od.gT, 3 * NH).then_inc(os_["gate_T"], 1)
                    if c == 3:
                        pe.wait_ge(os_["read"], 3)
                        for kv in range(2):
                            for g in range(2):
                                for t in range(TT):
                                    for par in range(2):
                                        c0 = (2 * kv + g) * P + t * 64
                                        f0 = kv * P + g * HD
                                        last = mm(ps[64 * par:64 * par + 64, 4, c0:c0 + 64],
                                                  od.kc[:, t, f0:f0 + HD],
                                                  const("pick", 2, 64)[:, par, :], start=True, stop=True)
                        last.then_inc(os_["pick_mm"], 1)
                pe.wait_ge(os_["xc_lo_done"], 1)
                pe.wait_ge(os_["xc_tail"], 1)
                for i in range(4):
                    kv, half = i // 2, i % 2
                    n = at["cmp", i]
                    pe.wait_ge(lo_done, n + 1)
                    for k in range(8):
                        pair = 8 * half + k
                        c0 = (kv * CMP_PAIRS + pair) * 2 * N_CMP
                        last = product3(ps[:, 5 + kv, 0:2 * P], od.xc_hi_wide[:, c0:c0 + P], od.xc_lo_wide[:, c0:c0 + P],
                                        cols(w_hi, n, k, CW, 0, CW), cols(w_lo, n, k, CW, 0, CW),
                                        pair == 0, pair == 15)
                    used(last)
                pe.wait_ge(os_["gates_done"], 1)
                project("a", ps[:, 3, :])
                for kv in range(2):
                    pe.wait_ge(os_["hr_done"], kv + 1)
                    for ht in range(2):
                        q = 2 * kv + ht
                        last = nc.tensor.transpose(ps[:, 4, 32 * q:32 * q + 2 * N_CMP],
                                                   od.hid_rows[0:2 * N_CMP, kv, ht * P:(ht + 1) * P],
                                                   ident[0:2 * N_CMP, 0:2 * N_CMP])
                last.then_inc(os_["hid_T"], 1)
                scores(0)
                pe.wait_ge(os_["hid_done"], 1)
                for g in range(2):
                    for ht in range(2):
                        last = mm(ps[64 * g:64 * g + 64, 7, 0:N_CMP], w2[:, 0, ht, :],
                                  od.hid[:, 0, ht, g * N_CMP:(g + 1) * N_CMP], start=ht == 0, stop=ht == 1)
                for g in range(2):
                    for ht in range(2):
                        last = mm(ps[0:N_CMP, 7, 64 + 64 * g:128 + 64 * g],
                                  od.hid[:, 1, ht, g * N_CMP:(g + 1) * N_CMP], w2[:, 1, ht, :],
                                  start=ht == 0, stop=ht == 1)
                last.then_inc(os_["c2_mm"], 1)
                pe.wait_ge(os_["read"], 8)
                kv_chunk(1, 0)
                pe.wait_ge(os_["c2_read"], 1)
                for g in range(2):
                    gs = slice(64 * g, 64 * g + 64)
                    for t in range(TT):
                        for m in range(4):
                            c0 = 64 * t + N_CMP * m
                            last = mm(ps[:, 4 + g, c0:c0 + N_CMP], od.qn[gs, m, t * P:(t + 1) * P],
                                      od.kcT[gs, 0:N_CMP], start=True, stop=True)
                last.then_inc(os_["cs_mm"], 1)
                kv_chunk(1, 1)
                for u in range(6):
                    if u < 5:
                        scores(u + 1)
                    turned(u)
                    if u == 0:
                        pe.wait_ge(os_["pc_done"], 1)
                        weights_turned(0)
                    elif u == 2:
                        pe.wait_ge(oT_done, OT_BASE["odd"] + 1)
                        weights_turned(2)
                    kv_chunk(1, u + 2)
                    if u in (0, 2):
                        pe.wait_ge(os_["pcT_done"], u + 1)
                        weights_turned(u + 1)
                    if u in PV_AFTER:
                        values(PV_AFTER.index(u))
                pe.wait_ge(oT_done, OT_BASE["odd"] + 3)
                out_chunks(at["mixout", 1, 0], lambda i: pe.wait_ge(oT_done, OT_BASE["odd"] + i + 1))

            def scores(u):
                a, g = UNITS[u]
                if u == 0:
                    pe.wait_ge(os_["read"], 7)
                else:
                    pe.wait_ge(os_["p_exp"], u)
                gs = slice(64 * g, 64 * g + 64)
                q = od.qs if a == 2 else od.qn
                eye = mask("eye")
                mm(ps[:, 0, :].rearrange("p (h c) -> p h c", h=4), eye,
                   mask("causal0").unsqueeze(1).to_broadcast([P, 4, P]), start=True, stop=False)
                for m in range(4):
                    mm(ps[:, 0, m * P:(m + 1) * P], q[gs, m, 0:P], od.kT[gs, a, 0:P], start=False, stop=m == 3)
                for b in range(2):
                    mm(ps[:, 1 + b, :].rearrange("p (h c) -> p h c", h=2), eye,
                       mask("band1" if a == 2 else "causal1").unsqueeze(1).to_broadcast([P, 2, SEQ]),
                       start=True, stop=False)
                    for i in range(2):
                        last = mm(ps[:, 1 + b, i * SEQ:(i + 1) * SEQ], q[gs, 2 * b + i, P:2 * P], od.kT[gs, a, :],
                                  start=False, stop=i == 1)
                last.then_inc(os_["s_mm"], 1)

            def turned(u):
                pe.wait_ge(os_["p_done"], u + 1)
                if u == 0:
                    pe.wait_ge(os_["cs_in"], 1)
                else:
                    pe.wait_ge(os_["pT_act"], 2 * u)
                    pe.wait_ge(os_["pT_dve"], u)
                for b in range(3):
                    for h in range(4):
                        src = od.p0[:, h, :] if b == 0 else od.p1[:, h, (b - 1) * P:b * P]
                        last = nc.tensor.transpose(ps[:, 4 + b, h * P:(h + 1) * P], src, ident)
                    last.then_inc(os_["p_T"], 1)

            def values(r):
                u, bank = PV_AFTER[r], PV_BANK[r]
                pe.wait_ge(os_["pT_act"], 2 * (u + 1))
                pe.wait_ge(os_["pT_dve"], u + 1)
                if r < 2:
                    pe.wait_ge(os_["pcT_done"], 2 * r + 2)
                elif r == 2:
                    pe.wait_ge(oT_done, OT_BASE["odd"] + 2)
                a, g = UNITS[u]
                units = [u - 1, u] if a == 1 else [u]
                for h in range(4):
                    out_ps = ps[64 * (h % 2):64 * (h % 2) + 64, bank, (h // 2) * SEQ:(h // 2 + 1) * SEQ]
                    first = True
                    for w in units:
                        a_w = UNITS[w][0]
                        pT = od.pT[w % 2]
                        last_unit = w == units[-1] and a == 2
                        mm(out_ps, od.v[:, a_w, 0, g * HD:(g + 1) * HD], pT[:, 0:2, h, :], start=first, stop=False)
                        last = mm(out_ps[:, P:], od.v[:, a_w, 1, g * HD:(g + 1) * HD], pT[:, 2, h, :],
                                  start=False, stop=last_unit)
                        first = False
                    if a == 1:
                        last = mm(out_ps, od.vc[0:N_CMP, g, :], od.pcT[0:N_CMP, 4 * g + h, :], start=False, stop=True)
                last.then_inc(os_["pv_mm"], 1)

            pe.wait_ge(ident_in, 16)
            norm(0, ("norm", 0, 0))
            ffn(0, 0)
            norm(2, ("norm", 0, 1))
            pe.wait_ge(smalls_split, 1)
            even()
            norm(3, ("norm", 0, 2))
            cross(0)
            norm(4, ("norm", 0, 3))
            ffn(0, 1)
            norm(5, ("norm", 1, 0))
            ffn(1, 0)
            norm(6, ("norm", 1, 1))
            odd()
            norm(7, ("norm", 1, 2))
            cross(1)
            norm(8, ("norm", 1, 3))
            ffn(1, 1)


INPUTS = ["x", "mem", "norm_w", "final_norm_w", "mem_norm_w", "ffn_w_gate", "ffn_w_up", "ffn_w_down",
          "xattn_wq", "xattn_wkv", "xattn_wo", "even_w_in", "even_w_out", "ssm_conv_w", "ssm_conv_b",
          "ssm_dt_bias", "ssm_a_log", "ssm_d", "ssm_norm_w", "odd_w_in", "odd_w_out", "nsa_cmp_pe",
          "nsa_cmp_w1", "nsa_cmp_w2", "swa_sinks"]


def kernel(**inputs):
    import concourse.bacc as bacc
    from concourse.bass_utils import run_bass_kernel_spmd

    nc = bacc.Bacc("TRN2", target_bir_lowering=False, num_devices=1)
    arrays, d = {}, {}
    consts, masks = shape_constants()
    for name, a in [(n, inputs[n]) for n in INPUTS] + [("consts", consts), ("masks", masks)]:
        a = np.ascontiguousarray(a)
        arrays["in_" + name] = a
        d[name] = nc.dram_tensor("in_" + name, a.shape, mybir.dt.from_np(a.dtype), kind="ExternalInput").ap()
    out = nc.dram_tensor("out_0", (1, SEQ, D), F32, kind="ExternalOutput").ap()
    build(nc, d, out)
    r = run_bass_kernel_spmd(nc, [arrays], core_ids=[0])
    return r.results[0]["out_0"]
```

```python
from contextlib import ExitStack

import numpy as np

import concourse.bass as bass
from concourse import mybir

F32 = mybir.dt.float32
F32R = mybir.dt.float32r
BF16 = mybir.dt.bfloat16
ALU = mybir.AluOpType
ACT = mybir.ActivationFunctionType
AX = mybir.AxisListType

P = 128
SEQ, MEM, D = 256, 256, 1024
TT = SEQ // P
KT = D // P
DFF = 2816
CW = 256
FJ = DFF // CW
CHUNK = KT * CW
EPS = 1e-6
RING = 3
BIG = 1e30

RET_H, DK = 4, 128
SSM_H, HP, NS, SSM_IN = 8, 64, 64, 512
CONV_CH, CONV_W = 768, 4
XT = CONV_CH // P
EVEN_IN = 3336
HD, NH = 64, 8
N_CMP, CMP_STRIDE, CMP_BLK = 15, 16, 32
CMP_PAIRS = CMP_BLK // 2
XH, XD = 4, 256

CONSTS = {}
_at = 0
for _name, _w in (("ident", P), ("upto", P), ("after", P), ("cos", TT * 64), ("sin", TT * 64),
                  ("decayT", RET_H * P), ("zeta", RET_H), ("xi", RET_H), ("pick", P),
                  ("cmpmask", TT * N_CMP), ("cmpbias", TT * N_CMP)):
    CONSTS[_name] = (_at, _w)
    _at += _w
CONST_W = _at
MASKS = {"causal0": (0, P), "causal1": (P, 2 * P), "band1": (3 * P, 2 * P), "eye": (5 * P, P)}
MASK_W = 6 * P


def shape_constants():
    f = np.float32
    c = np.zeros((P, CONST_W), f)

    def put(name, a):
        at, w = CONSTS[name]
        c[:, at:at + w] = np.asarray(a, f).reshape(P, w)

    i = np.arange(P)
    put("ident", np.eye(P))
    put("upto", i[:, None] <= i[None, :])
    put("after", i[:, None] > i[None, :])
    pos = np.arange(SEQ, dtype=f)
    inv = (f(1.0) / (f(10000.0) ** np.linspace(0.0, 1.0, DK // 2, dtype=f))).astype(f)
    ang = (pos[:, None] * inv[None, :]).astype(f).reshape(TT, P, 64).transpose(1, 0, 2)
    put("cos", np.cos(ang))
    put("sin", np.sin(ang))
    log_g = np.log1p(-np.exp2(-5.0 - np.arange(RET_H)))
    diff = i[None, :] - i[:, None]
    scale = DK ** -0.5
    put("decayT", np.where(diff[:, None, :] >= 0,
                           np.exp(np.maximum(diff, 0)[:, None, :] * log_g[None, :, None]), 0.0) * scale)
    put("zeta", np.exp((P - 1 - i)[:, None] * log_g[None, :]) * scale)
    put("xi", np.exp((i + 1)[:, None] * log_g[None, :]))
    pick = np.zeros((P, 2, P // 2))
    for par in range(2):
        pick[2 * np.arange(P // 2) + par, par, np.arange(P // 2)] = 1
    put("pick", pick)
    tok = np.arange(SEQ).reshape(TT, P).T
    seen = (np.arange(N_CMP) * CMP_STRIDE + CMP_BLK - 1)[None, None, :] <= tok[:, :, None]
    put("cmpmask", seen)
    put("cmpbias", np.where(seen, 0.0, -BIG))
    m = np.zeros((P, MASK_W), f)
    causal = np.where(i[:, None] >= i[None, :], 0.0, -BIG)
    m[:, 0:P] = causal
    m[:, 2 * P:3 * P] = causal
    m[:, 3 * P:4 * P] = np.where(i[None, :] > i[:, None], 0.0, -BIG)
    m[:, 4 * P:5 * P] = causal
    m[:, 5 * P:6 * P] = np.eye(P)
    return c, m


FFN_CHUNKS = 3 * FJ
EVEN_ORDER = ["x0", "x1", "x2", "q0", "q1", "k0", "k1", "v0", "v1", "g0", "g1", "z0", "z1"]
ODD_ORDER = ["s", "w", "c", "qn0", "qn1", "qs0"]


def chunk_plan():
    at, n = {}, 0

    def take(names):
        nonlocal n
        for x in names:
            at[x] = n
            n += 1

    for layer in range(2):
        at["ffn", layer, 0] = n
        n += FFN_CHUNKS
        kv = [("kv", layer, i) for i in range(8)]
        if layer == 0:
            take([("even", x) for x in EVEN_ORDER])
            take(kv[:7])
            take([("mixout", layer, i) for i in range(4)])
        else:
            take([kv[2]])
            take([("odd", x) for x in ODD_ORDER])
            take([("cmp", 0), ("odd", "qs1"), ("cmp", 1), ("odd", "a"), ("cmp", 2), ("cmp", 3)])
            take(kv[3:7])
            take([("mixout", layer, i) for i in range(4)])
        take([kv[7]])
        take([("wq", layer, i) for i in range(4)])
        take([("wo", layer, i) for i in range(4)])
        if layer == 0:
            take([("kv", 1, 0)])
        at["ffn", layer, 1] = n
        n += FFN_CHUNKS
        if layer == 0:
            take([("kv", 1, 1)])
    return at, n


def build(nc, d, out):
    at, n_chunks = chunk_plan()
    ctx = ExitStack()
    with ctx:
        def sb(name, shape, dt=F32):
            return ctx.enter_context(nc.sbuf_tensor(name, shape, dt))

        def sem(name):
            return ctx.enter_context(nc.semaphore(name))

        ps = ctx.enter_context(nc.psum_tensor("ps", [P, 8, 512], F32))
        x = sb("x", [P, TT, D])
        xn = sb("xn", [P, TT, D])
        hT_hi = sb("hT_hi", [P, KT, SEQ], F32R)
        hT_lo = sb("hT_lo", [P, KT, SEQ], F32R)
        memT_hi = sb("memT_hi", [P, KT, MEM], F32R)
        memT_lo = sb("memT_lo", [P, KT, MEM], F32R)
        raw = sb("raw", [P, RING, CHUNK])
        w_hi = sb("w_hi", [P, RING, CHUNK], F32R)
        w_lo = sb("w_lo", [P, RING, CHUNK], F32R)
        xk = sb("xk", [P, KT, MEM])
        xv = sb("xv", [P, TT, D])
        norm_w = sb("norm_w_rows", [P, D])
        consts = sb("consts", [P, CONST_W])
        masks_f = xk[:, 0:3, :].rearrange("p a b -> p (a b)")
        masks = sb("masks", [P, MASK_W], BF16)
        msum = sb("msum", [P, 4])
        msq = sb("msq", [P, 16])
        rstd = sb("rstd", [P, 2])
        neg_half = sb("neg_half", [P, 8])
        DT_AT, GATE_AT, SMALL_W = 0, KT * SSM_H, KT * SSM_H + KT * 3 * NH + 120
        small_w = xk[:, :, :].rearrange("p k c -> p (k c)")[:, 1024:1024 + SMALL_W]
        small_w_hi = sb("small_w_hi", [P, SMALL_W], F32R)
        small_w_lo = sb("small_w_lo", [P, SMALL_W], F32R)
        conv_w = sb("conv_w", [P, CONV_W, XT])
        conv_b = sb("conv_b", [P, XT])
        head_rows = sb("head_rows", [P, 4, SSM_H])
        w2 = sb("w2", [P, 2, 2, HD])
        pe_pairs = sb("pe_pairs", [P, 2, CMP_PAIRS])
        ssm_nw = sb("ssm_nw", [P, SSM_IN])
        ARENA = 11760
        XC_W = 2 * CMP_PAIRS * 2 * N_CMP + P - 2 * N_CMP + 2
        arena_r = sb("arena_r", [P, 2 * XC_W], F32R)
        arena = sb("arena", [P, ARENA])

        def part(at_, shape):
            size = int(np.prod(shape))
            assert at_ + size <= ARENA, (at_, shape)
            v = arena[:, at_:at_ + size]
            if len(shape) == 1:
                return v
            names = "abcde"[:len(shape)]
            sizes = {k: s for k, s in zip(names[1:], shape[1:])}
            return v.rearrange(f"p ({' '.join(names)}) -> p {' '.join(names)}", **sizes)

        def const(name, *dims):
            a, w = CONSTS[name]
            v = consts[:, a:a + w]
            if len(dims) > 1:
                names = "abc"[:len(dims)]
                v = v.rearrange(f"p ({' '.join(names)}) -> p {' '.join(names)}",
                                **{k: s for k, s in zip(names[1:], dims[1:])})
            return v

        def mask(name):
            a, w = MASKS[name]
            return masks[:, a:a + w]

        ident = const("ident")
        mem_rows = xv[:, :, :]

        raw_in = [sem(f"raw_in{i}") for i in range(RING)]
        hi_done = sem("hi_done")
        lo_done = sem("lo_done")
        chunks_used = sem("chunks_used")
        small_in = sem("small_in")
        x_in = [sem(f"x_in{t}") for t in range(TT)]
        ident_in = sem("ident_in")
        mem_in = sem("mem_in")
        norm_w_in = sem("norm_w_in")
        out_sent = sem("out_sent")
        consts_made = sem("consts_made")
        small_w_set = sem("small_w_set")
        row_done = sem("row_done")
        smalls_split = sem("smalls_split")
        neg_half_set = sem("neg_half_set")
        sq_done = sem("sq_done")
        rstd_done = sem("rstd_done")
        xn_done = sem("xn_done")
        transposed = sem("transposed")
        hT_hi_done = sem("hT_hi_done")
        hT_done = sem("hT_done")
        x_added = sem("x_added")
        silu_done = sem("silu_done")
        mult_done = sem("mult_done")
        gu_hi_done = sem("gu_hi_done")
        gu_done = sem("gu_done")
        oT_hi_done = sem("oT_hi_done")
        oT_done = sem("oT_done")
        kv_read = sem("kv_read")
        act_step, dve_step, pool_step = sem("act_step"), sem("dve_step"), sem("pool_step")

        SETS = {("norm", 0, 0): 0, "mem": 1, ("norm", 0, 1): 2, "mix0": 3, ("norm", 0, 2): 4,
                ("norm", 0, 3): 5, ("norm", 1, 0): 6, ("norm", 1, 1): 7, ("norm", 1, 2): 8,
                ("norm", 1, 3): 9}

        def row_bank(w, t, kh):
            return 2 + kh if w == SETS["mem"] else 2 * t + kh

        def norm_no(layer, i):
            return 1 + 4 * layer + i if layer or i else 0

        def w_view(ap):
            return ap.rearrange("(k p) c -> p k c", p=P)

        def pieces_of(name):
            kind = name[0]
            if kind == "even":
                s = name[1]
                col = {"q": 0, "k": 512, "v": 1024, "g": 1536, "z": 2048, "x": 2560}[s[0]] + CW * int(s[1])
                return [(("k", CW), w_view(d["even_w_in"][0][:, col:col + CW]))]
            if kind == "odd":
                s = name[1]
                if s[0] == "q":
                    base = {"n": 0, "s": 1304}[s[1]] + P * int(s[2])
                    return [(("run", g * P), w_view(d["odd_w_in"][0][:, base + g * 256:base + g * 256 + P]))
                            for g in range(2)]
                col = {"c": 512, "s": 768, "w": 1024, "a": 1816}[s]
                return [(("k", CW), w_view(d["odd_w_in"][0][:, col:col + CW]))]
            if kind == "cmp":
                kv, half = name[1] // 2, name[1] % 2
                return [(("k", CW), d["nsa_cmp_w1"][0, kv].rearrange("(k p) c -> p k c", p=P)
                         [:, 8 * half:8 * half + 8, :])]
            layer, i = name[1], name[2]
            if kind == "kv":
                return [(("k", CW), w_view(d["xattn_wkv"][layer][:, i * CW:(i + 1) * CW]))]
            if kind == "wq":
                return [(("k", CW), w_view(d["xattn_wq"][layer][:, i * CW:(i + 1) * CW]))]
            src = d["xattn_wo"][layer] if kind == "wo" else d["even_w_out" if layer == 0 else "odd_w_out"][0]
            return [(("k", D), src[2 * P * i:2 * P * (i + 1), :].rearrange("(k p) c -> p k c", p=P))]

        order = sorted((v, k) for k, v in at.items() if k[0] != "ffn")
        named = {v: k for v, k in order}
        pieces = [len(pieces_of(named[n])) if n in named else 1 for n in range(n_chunks)]

        def landed(n):
            return 16 * sum(pieces[m] for m in range(n % RING, n + 1, RING))

        def parts_of(n):
            slot = n % RING
            if n in named and named[n][0] == "odd" and named[n][1][0] == "q":
                src = raw[:, slot, :].rearrange("p (k g i c) -> p k g i c", g=2, i=2, c=HD)
                hi, lo = (w[:, slot, :].rearrange("p (k i g c) -> p k i g c", g=2, i=2, c=HD) for w in (w_hi, w_lo))
                return [(hi[:, :, i, :, :], lo[:, :, i, :, :], src[:, :, :, i, :]) for i in range(2)]
            return [(w_hi[:, slot, :], w_lo[:, slot, :], raw[:, slot, :])]

        def slot_k(n, width):
            return raw[:, n % RING, :].rearrange("p (k c) -> p k c", c=width)

        g_act = part(0, [512])
        gu = part(512, [512])
        gu_hi, gu_lo, gu_hi_last, gu_lo_last = (
            arena_r[:, i * 512:(i + 1) * 512].rearrange("p (k c) -> p k c", k=2) for i in range(4))

        class Even:
            xpad = part(0, [XT, SEQ + 3])
            ld = xk[:, :, :].rearrange("p k c -> p (k c)").rearrange("p (t h s) -> p t h s", t=TT, h=SSM_H)
            xbcT = part(1920, [XT, SEQ])
            q_rot = part(3456, [TT, RET_H, 2, 64])
            o = part(3456, [TT, RET_H, P])
            k_rot = part(4480, [TT, RET_H, 2, 64])
            s = part(4480, [TT, RET_H, P])
            rot = [part(5504 + 256 * i, [TT, 2, 64]) for i in range(4)]
            cbm = part(512, [TT, 2, P])
            kz = part(6016, [RET_H, P])
            qT = part(6528, [TT, RET_H, P])
            kT = part(7552, [TT, RET_H, P])
            v = part(8576, [TT, RET_H * DK])
            xh = part(9600, [TT, SSM_H, HP])
            xdt = part(10624, [TT, SSM_H, HP])
            mt = xv[:, :, :].rearrange("p t (h s) -> p t h s", h=SSM_H)
            b_tok = part(1664, [P])
            dtT = part(4480, [SEQ])
            small = part(11648, [112])
            dtr = small[:, 0:16]
            ln1p = small[:, 16:32]
            dt = small[:, 32:48]
            dta = small[:, 48:64]
            ea = small[:, 64:72]
            dec = small[:, 72:80]
            cum = small[:, 80:88]
            ssr = small[:, 88:90]
            rsr = small[:, 90:92]
            msr = small[:, 92:94]
            osq = small[:, 96:104]
            ors = small[:, 104:112]
            oms = msq[:, 8:16]
            yc = part(5504, [SSM_H, HP])
            xdtd = part(0, [SSM_H, HP])
            kv = part(512, [RET_H, P])
            sT = part(1024, [SSM_IN])
        ev = Even

        even_sems = {}
        for name in ("xpad_zero", "act_read", "conv_done", "xbc_done", "dt_mm", "dtT_done", "dt_T",
                     "dt_raw", "ln_done", "dta_done", "ea_done", "ld_done", "rot_read",
                     "rot_done", "xs_T", "xh_done", "cb_mm", "cbm_done", "dec_mm", "dec_done",
                     "seg_mm", "seg_exp", "mt_done", "xdt_done", "xdtd_done", "qk_T", "qkT_done",
                     "kz_done", "ret_s_mm", "s_done", "st_mm", "st_done", "ret_kv_mm", "kvs_done",
                     "y_mm", "yoff_mm", "y_read", "o_mm", "o_read", "dx_done", "y_sq", "o_sq", "o_ssq",
                     "y_rstd", "o_rstd", "mix_done", "y_ready"):
            even_sems[name] = sem("e_" + name)
        es = even_sems

        class Odd:
            qn = part(0, [4, SEQ])
            qs = part(1024, [4, SEQ])
            kT = part(2048, [3, SEQ])
            v = part(2816, [3, TT, P])
            kc = part(3584, [TT, 2 * P])
            xc = part(4096, [2, CMP_PAIRS, 2, N_CMP])
            xc_hi, xc_lo = (arena_r[:, i * XC_W:i * XC_W + 960] for i in range(2))
            xc_hi_wide, xc_lo_wide = (arena_r[:, i * XC_W:(i + 1) * XC_W] for i in range(2))
            hid = part(5632, [2, 2, 2 * N_CMP])
            kcT = part(11448, [2, N_CMP])
            vc = part(5776, [2, HD])
            pc = part(5904, [TT, NH, N_CMP])
            pcT = part(6144, [NH, SEQ])
            xn_flat = xn[:, :, :].rearrange("p t c -> p (t c)")
            p0 = [part(8192, [4, P]), xn_flat[:, 0:512].rearrange("p (h c) -> p h c", h=4)]
            p1 = [part(8704, [4, SEQ]), xn_flat[:, 512:1536].rearrange("p (h c) -> p h c", h=4)]
            hid_rows = part(8704, [2, 2 * P])
            gT = part(9216, [SEQ])
            pT = [part(9728, [3, 4, P]), part(4096, [3, 4, P])]
            small = part(11264, [120])
            gates = small[:, 0:48]
            nmax, rs, fac, es = ([part(11384 + 16 * j, [8]), part(11392 + 16 * j, [8])] for j in range(4))
            cmax = small[:, 80:96]
            csum = small[:, 96:112]
            nmax2 = small[:, 112:120]

        od = Odd
        os_ = {name: sem("o_" + name) for name in (
            "read", "gate_mm", "gT_done", "gate_T", "gates_done", "zeros_set", "hr_done", "hid_T",
            "pick_mm", "xc_done", "xc_hi_done", "xc_lo_done",
            "hid_done", "c2_mm", "c2_read", "cs_mm", "cs_in", "cs_exp", "pc_done", "pc_T", "pcT_done",
            "s_mm", "nmax_done", "p_exp", "p_done", "p_T", "pT_act", "pT_dve", "pv_mm")}

        class Cross:
            q = part(0, [KT, SEQ])
            p = part(2048, [XH, TT, MEM])
            pT = part(4096, [XH, 2, SEQ])
            small = part(6144, [32])
            nmax = small[:, 0:8]
            rs = small[:, 8:16]
            fac = small[:, 16:24]

        cr = Cross
        xs_ = {name: sem("x_" + name) for name in (
            "q_read", "s_mm", "nmax", "p_exp", "p_done", "p_T", "pT_done", "pv_mm")}
        KV_BANK = [(3, 3, 5, 6, 5, 6, 7, 4), (4, 4, 4, 3, 3, 3, 3, 4)]
        FILL = {("norm", 0, 2): (0, 7), ("norm", 0, 3): (1, 0), ("norm", 1, 0): (1, 1), ("norm", 1, 1): (1, 2),
                ("norm", 1, 2): (1, 7)}
        CS_FILL, UNIT_FILL = 3, [(4, 0), (4, 1), (5, 0), (5, 1), (6, 0), (6, 1)]

        OT_BASE = {"cross0": 0, "odd": 4, "cross1": 8}
        UNITS = [(0, 0), (1, 0), (0, 1), (1, 1), (2, 0), (2, 1)]
        PV_AFTER = [1, 3, 4, 5]
        PV_BANK = [7, 7, 7, 0]

        def pv_before(u):
            return 1 if u < 4 else 2

        block = ctx.enter_context(nc.Block())

        def small_loads():
            rows = [d["ssm_dt_bias"][0], d["ssm_a_log"][0], d["ssm_d"][0], d["swa_sinks"][0]]
            w_in = {"dt": d["even_w_in"][0][:, EVEN_IN - SSM_H:EVEN_IN], "gate": d["odd_w_in"][0][:, 1280:1304]}
            loads = [(consts[:, P:], d["consts"][:, P:]), (masks_f, d["masks"]),
                     (small_w[:, DT_AT:GATE_AT].rearrange("p (k c) -> p k c", k=KT), w_view(w_in["dt"])),
                     (small_w[:, GATE_AT:GATE_AT + KT * 3 * NH].rearrange("p (k c) -> p k c", k=KT),
                      w_view(w_in["gate"])),
                     (w2[:, 0, :, :], d["nsa_cmp_w2"][0, 0].rearrange("(t p) c -> p t c", p=P)),
                     (w2[:, 1, :, :], d["nsa_cmp_w2"][0, 1].rearrange("(t p) c -> p t c", p=P)),
                     (ssm_nw[:, :], d["ssm_norm_w"][0].partition_broadcast(P))]
            loads += [(head_rows[:, i, :], r.partition_broadcast(P)) for i, r in enumerate(rows)]
            return loads

        def strided_loads():
            loads = [(conv_b[:, :], d["ssm_conv_b"][0].rearrange("(t p) -> p t", p=P))]
            loads += [(conv_w[:, w, :], d["ssm_conv_w"][0, w].rearrange("(t p) -> p t", p=P))
                      for w in range(CONV_W)]
            loads += [(pe_pairs[:, kv, :], d["nsa_cmp_pe"][0, kv].rearrange("(i r) c -> (r c) i", r=2))
                      for kv in range(2)]
            return loads

        SMALL = 16 * (len(small_loads()) + len(strided_loads()))

        @block.sync
        def _(sp):
            def load(n, dst_view, src):
                if n >= RING:
                    sp.wait_ge(lo_done, n - RING + 1)
                sp.dma_start(dst_view, src).then_inc(raw_in[n % RING], 16)

            def named_chunks(first, last):
                for n in range(first, last):
                    if n >= RING:
                        sp.wait_ge(lo_done, n - RING + 1)
                    for (kind, arg), src in pieces_of(named[n]):
                        dst = slot_k(n, arg) if kind == "k" else slot_k(n, CW)[:, :, arg:arg + P]
                        sp.dma_start(dst, src).then_inc(raw_in[n % RING], 16)

            def ffn(layer, which, first=False):
                base = at["ffn", layer, which]
                gate, up = (d[w][layer, which].rearrange("(k p) (j c) -> j p k c", p=P, c=CW)
                            for w in ("ffn_w_gate", "ffn_w_up"))
                down = d["ffn_w_down"][layer, which].rearrange("(j k p) c -> j p k c", k=2, p=P)
                load(base, slot_k(base, CW), gate[0])
                load(base + 1, slot_k(base + 1, CW), up[0])

                def turn(j):
                    for c, (w, width, row) in enumerate(((gate, CW, j + 1), (up, CW, j + 1), (down, D, j))):
                        n = base + 2 + c
                        if not (first and isinstance(j, int) and c == 0):
                            sp.wait_ge(lo_done, j * 3 + (n - RING + 1))
                        sp.dma_start(slot_k(n, width), w[bass.ds(row, 1)].rearrange("a p k c -> (a p) k c"))\
                          .then_inc(raw_in[n % RING], 16)

                if first:
                    turn(0)
                    sp.dma_start(mem_rows, d["mem"][0].rearrange("(t p) c -> p t c", p=P)).then_inc(mem_in, 16)
                    for dst, src in small_loads():
                        sp.dma_start(dst, src).then_inc(small_in, 16)
                    with nc.allow_non_contiguous_dma(reason="a few KB of per-channel columns"):
                        for dst, src in strided_loads():
                            sp.dma_start(dst, src).then_inc(small_in, 16)
                with sp.Fori(1 if first else 0, FJ - 1) as j:
                    turn(j)
                n = base + FFN_CHUNKS - 1
                load(n, slot_k(n, D), down[FJ - 1])

            for t in range(TT):
                sp.dma_start(x[:, t, :], d["x"][0, t * P:(t + 1) * P, :]).then_inc(x_in[t], 16)
            ffn(0, 0, first=True)
            named_chunks(at["ffn", 0, 0] + FFN_CHUNKS, at["ffn", 0, 1])
            ffn(0, 1)
            named_chunks(at["ffn", 0, 1] + FFN_CHUNKS, at["ffn", 1, 0])
            ffn(1, 0)
            named_chunks(at["ffn", 1, 0] + FFN_CHUNKS, at["ffn", 1, 1])
            ffn(1, 1)
            for t in range(TT):
                for h in range(2):
                    sp.wait_ge(xn_done, 4 * 9 + 2 * t + h + 1)
                    hs = slice(h * 512, (h + 1) * 512)
                    sp.dma_start(out[0, t * P:(t + 1) * P, hs], xn[:, t, hs]).then_inc(out_sent, 16)
            sp.wait_ge(out_sent, 2 * 16 * TT)

        @block.scalar
        def _(act):
            made, steps = [0], [0]

            def step(ins):
                steps[0] += 1
                ins.then_inc(act_step, 1)
                act.wait_ge(act_step, steps[0])

            def hi_upto(limit):
                for n in range(made[0], min(limit, n_chunks)):
                    act.wait_ge(raw_in[n % RING], landed(n))
                    if n >= RING:
                        act.wait_ge(chunks_used, n - RING + 1)
                    for hi, _, src in parts_of(n):
                        ins = nc.scalar.activation(hi, src, ACT.Copy)
                    ins.then_inc(hi_done, 1)
                    made[0] = n + 1

            def squares(v, src, ready, ahead=0, tiles=(0, 1)):
                for t in tiles:
                    if t:
                        hi_upto(ahead)
                    for h in range(2):
                        ready(t, h)
                        bank = 2 * t + h if v != 1 else 2 + h
                        if v == 1 and t:
                            act.wait_ge(sq_done, 4 * v + h + 1)
                        nc.scalar.activation(ps[:, bank, :], src[:, t, h * 512:(h + 1) * 512], ACT.Square,
                                             scale=D ** -0.5, accum_out=msum[:, 2 * t + h:2 * t + h + 1])\
                          .then_inc(sq_done, 1)

            def evac_hi(w, dst, tiles=(0, 1)):
                for t in tiles:
                    for kh in range(2):
                        act.wait_ge(transposed, 4 * w + 2 * t + kh + 1)
                        nc.scalar.activation(dst[:, 4 * kh:4 * kh + 4, t * P:(t + 1) * P],
                                             ps[:, row_bank(w, t, kh), :].rearrange("p (k c) -> p k c", c=P),
                                             ACT.Copy).then_inc(hT_hi_done, 1)

            def norm(layer, i, ahead=0):
                v = norm_no(layer, i)

                def ready(t, h):
                    if v == 0:
                        act.wait_ge(x_in[t], 16)
                    else:
                        act.wait_ge(x_added, 4 * (v - 2) + 2 * t + h + 1)
                squares(v, x, ready, ahead)
                if v == 0:
                    evac_hi(0, hT_hi, tiles=(0,))
                    hi_upto(1)
                    evac_hi(0, hT_hi, tiles=(1,))
                else:
                    evac_hi(SETS["norm", layer, i], hT_hi)
                if ("norm", layer, i) in FILL:
                    kv_chunk(*FILL["norm", layer, i])

            def kv_chunk(layer, i):
                act.wait_ge(chunks_used, at["kv", layer, i] + 1)
                pv = ps[:, KV_BANK[layer][i], :].rearrange("p (a c) -> p a c", a=2)
                dst = xk[:, 2 * i:2 * i + 2, :] if i < 4 else xv[:, :, (i - 4) * CW:(i - 3) * CW]
                nc.scalar.activation(dst, pv, ACT.Copy).then_inc(kv_read, 1)
                hi_upto(at["kv", layer, i] + 4)

            def ffn(layer, which):
                f, base = 2 * layer + which, at["ffn", layer, which]

                def silu(j, cell):
                    act.wait_ge(chunks_used, j * 3 + cell)
                    nc.scalar.activation(g_act, ps[:, 0, :], ACT.Silu).then_inc(silu_done, 1)

                def hidden(count, dst):
                    act.wait_ge(mult_done, count)
                    nc.scalar.activation(dst, gu.rearrange("p (k c) -> p k c", k=2),
                                         ACT.Copy).then_inc(gu_hi_done, 1)

                def turn(j, between=lambda c: None):
                    for c in range(3):
                        n = base + 2 + c
                        if c == 0:
                            act.wait_ge(mult_done, j + f * FJ)
                            silu(j, base)
                        if c == 2:
                            act.wait_ge(chunks_used, j * 3 + (base + 2))
                            hidden(j + (f * FJ + 1), gu_hi)
                        m = n + RING
                        act.wait_ge(raw_in[m % RING], (j - 1) * 16 + landed(m))
                        act.wait_ge(chunks_used, (j - 1) * 3 + (m - RING + 1))
                        nc.scalar.activation(w_hi[:, m % RING, :], raw[:, m % RING, :], ACT.Copy).then_inc(hi_done, 1)
                        between(c)

                hi_upto(base + 3)
                silu(0, base + 1)
                hi_upto(base + 5)
                hidden(f * FJ + 1, gu_hi)
                if f == 0:
                    turn(1, lambda c: c and squares(1, mem_rows, lambda t, h: act.wait_ge(mem_in, 16), tiles=(c - 1,)))
                    turn(2, small_tables)
                    turn(3, lambda c: c < 2 and evac_hi(SETS["mem"], memT_hi, tiles=(c,)))
                with act.Fori(1 if f else 4, FJ - 1) as j:
                    turn(j)
                made[0] = base + FFN_CHUNKS - 1
                act.wait_ge(mult_done, FJ - 1 + f * FJ)
                silu(FJ - 1, base)
                hi_upto(base + FFN_CHUNKS)
                hidden((f + 1) * FJ, gu_hi_last)
                hi_upto(base + FFN_CHUNKS + 2)

            def cross(layer):
                u = 4 * layer
                wq, wo = at["wq", layer, 0], at["wo", layer, 0]

                def queries_read(i):
                    act.wait_ge(chunks_used, wq + i + 1)
                    nc.scalar.activation(cr.q[:, 2 * i:2 * i + 2, :],
                                         ps[:, i % 3, :].rearrange("p (a c) -> p a c", a=2),
                                         ACT.Copy, scale=XD ** -0.5).then_inc(xs_["q_read"], 1)
                    if i < 3:
                        hi_upto(wq + i + 4)

                def exponentials(h):
                    act.wait_ge(xs_["nmax"], u + h + 1)
                    for t in range(TT):
                        nc.scalar.activation(cr.p[:, h, t, :], ps[:, 4 + h, t * MEM:(t + 1) * MEM],
                                             ACT.Exp, bias=cr.nmax[:, 2 * h + t:2 * h + t + 1],
                                             accum_out=cr.rs[:, 2 * h + t:2 * h + t + 1]).then_inc(xs_["p_exp"], 1)

                hi_upto(wq + 3)
                for i in range(XH):
                    queries_read(i)
                    if i >= 2:
                        exponentials(i - 2)
                exponentials(2)
                probs_out(u, 0)
                exponentials(3)
                for h in range(1, XH):
                    probs_out(u, h)
                for h in range(XH):
                    act.wait_ge(xs_["pv_mm"], u + h + 1)
                    nc.scalar.activation(hT_hi[:, 2 * h:2 * h + 2, :],
                                         ps[:, h, :].rearrange("p (a c) -> p a c", a=2),
                                         ACT.Copy).then_inc(oT_hi_done, 1)
                hi_upto(wq + 4 + 3)
                for i in range(3):
                    hi_upto(wo + i + 4)

            def probs_out(u, h):
                act.wait_ge(xs_["p_T"], u + h + 1)
                nc.scalar.activation(cr.pT[:, h, :, :], ps[:, (3, 1, 2, 3)[h], :].rearrange("p (a c) -> p a c", a=2),
                                     ACT.Copy).then_inc(xs_["pT_done"], 1)

            def even():
                E = at["even", "x0"]
                for c in range(3):
                    act.wait_ge(chunks_used, E + c + 1)
                    if c == 0:
                        act.wait_ge(es["xpad_zero"], 1)
                    nc.scalar.activation(ev.xpad[:, 2 * c:2 * c + 2, CONV_W - 1:],
                                         ps[:, c, :].rearrange("p (a c) -> p a c", a=2),
                                         ACT.Copy)
                    for m in range(2):
                        k = 2 * c + m
                        ins = nc.scalar.activation(ev.xbcT[:, k, :], ps[:, c, m * SEQ:(m + 1) * SEQ], ACT.Identity,
                                                   bias=conv_b[:, k:k + 1], scale=conv_w[:, CONV_W - 1, k:k + 1])
                    ins.then_inc(es["act_read"], 1)
                    hi_upto(E + c + 4)
                    if c:
                        conv_silu(c - 1)
                conv_silu(2)
                act.wait_ge(es["dt_raw"], 1)
                step(nc.scalar.activation(ev.ln1p, ev.dtr, ACT.Abs))
                step(nc.scalar.activation(ev.ln1p, ev.ln1p, ACT.Exp, scale=-1.0))
                nc.scalar.activation(ev.ea, head_rows[:, 1, :], ACT.Exp).then_inc(es["ea_done"], 1)
                nc.scalar.activation(ev.ln1p, ev.ln1p, ACT.Ln, bias=1.0).then_inc(es["ln_done"], 1)
                for e in range(3, 7):
                    hi_upto(E + e + 4)
                for t in range(TT):
                    act.wait_ge(es["xs_T"], t + 1)
                    nc.scalar.activation(ev.xh[:, t, :, :], ps[:, 4 + t, :].rearrange("p (h c) -> p h c", h=SSM_H),
                                         ACT.Copy).then_inc(es["xh_done"], 1)
                act.wait_ge(es["xs_T"], 3)
                nc.scalar.activation(ev.b_tok, ps[:, 3, 0:P], ACT.Copy).then_inc(es["xh_done"], 1)
                for i, e in enumerate((7, 8)):
                    act.wait_ge(chunks_used, E + e + 1)
                    nc.scalar.activation(ev.v[:, :, i * CW:(i + 1) * CW],
                                         ps[:, e % 3, :].rearrange("p (a c) -> p a c", a=2),
                                         ACT.Copy).then_inc(es["act_read"], 1)
                    hi_upto(E + e + 4)
                act.wait_ge(es["dec_mm"], 1)
                nc.scalar.activation(ev.small[:, 72:88], ps[:, 3, P:P + 16], ACT.Exp).then_inc(es["dec_done"], 1)
                for q in range(4):
                    act.wait_ge(es["seg_mm"], q + 1)
                    nc.scalar.activation(ev.mt[:, q // 2, 4 * (q % 2):4 * (q % 2) + 4, :],
                                         ps[:, 4 + q, :].rearrange("p (a c) -> p a c", a=4),
                                         ACT.Exp).then_inc(es["seg_exp"], 1)
                for i, e in enumerate((9, 10)):
                    act.wait_ge(chunks_used, E + e + 1)
                    nc.scalar.activation(xn[:, :, i * CW:(i + 1) * CW],
                                         ps[:, e % 3, :].rearrange("p (a c) -> p a c", a=2),
                                         ACT.Silu).then_inc(es["act_read"], 1)
                    hi_upto(E + e + 4)
                for i, dst in enumerate((ev.qT, ev.kT)):
                    for t in range(TT):
                        act.wait_ge(es["qk_T"], 2 * i + t + 1)
                        nc.scalar.activation(dst[:, t, :, :], ps[:, 4 + 2 * i + t, :].rearrange("p (a c) -> p a c", a=4),
                                             ACT.Copy).then_inc(es["qkT_done"], 1)
                for i, e in enumerate((11, 12)):
                    act.wait_ge(chunks_used, E + e + 1)
                    nc.scalar.activation(xn[:, :, 512 + i * CW:512 + (i + 1) * CW],
                                         ps[:, e % 3, :].rearrange("p (a c) -> p a c", a=2),
                                         ACT.Silu).then_inc(es["act_read"], 1)
                    hi_upto(E + e + 4)
                act.wait_ge(es["st_mm"], 1)
                nc.scalar.activation(ev.sT, ps[:, 6, :], ACT.Copy).then_inc(es["st_done"], 1)
                kv_chunk(0, 0)
                act.wait_ge(es["ret_kv_mm"], 1)
                nc.scalar.activation(ev.kv, ps[:, 6, :].rearrange("p (a c) -> p a c", a=4),
                                     ACT.Copy).then_inc(es["kvs_done"], 1)
                kv_chunk(0, 1)
                for t in range(TT):
                    act.wait_ge(es["y_ready"], t + 1)
                    nc.scalar.activation(ev.xdt[:, t, :, :], ev.xh[:, t, :, :], ACT.Square,
                                         accum_out=ev.ssr[:, t:t + 1]).then_inc(es["y_sq"], 1)
                kv_chunk(0, 2)
                act.wait_ge(es["o_read"], 1)
                act.wait_ge(es["y_read"], 1)
                nc.scalar.activation(ev.mt[:, :, 0:4, :], ev.o, ACT.Square).then_inc(es["o_sq"], 1)
                kv_chunk(0, 3)
                act.wait_ge(es["o_ssq"], 1)
                for i in range(4, 6):
                    kv_chunk(0, i)
                evac_hi(SETS["mix0"], hT_hi)
                kv_chunk(0, 6)

            def conv_silu(c):
                act.wait_ge(es["conv_done"], c + 1)
                nc.scalar.activation(ev.xbcT[:, 2 * c:2 * c + 2, :], ev.xbcT[:, 2 * c:2 * c + 2, :],
                                     ACT.Silu).then_inc(es["xbc_done"], 1)

            def odd():
                def read(name, b):
                    n = at["odd", name]
                    act.wait_ge(chunks_used, n + 1)
                    bank = ps[:, b, :].rearrange("p (a c) -> p a c", a=2)
                    if name[0] == "q":
                        dst = od.qn if name[1] == "n" else od.qs
                        m = 2 * int(name[2])
                        nc.scalar.activation(dst[:, m:m + 2, :], bank, ACT.Copy, scale=HD ** -0.5)\
                          .then_inc(os_["read"], 1)
                    elif name == "c":
                        nc.scalar.activation(od.kc, bank, ACT.Copy).then_inc(os_["read"], 1)
                    else:
                        j = "swa".index(name)
                        nc.scalar.activation(od.kT[:, j, :], bank[:, 0, :], ACT.Copy)
                        nc.scalar.activation(od.v[:, j, :, :], bank[:, 1, :].rearrange("p (a c) -> p a c", a=2),
                                             ACT.Copy).then_inc(os_["read"], 1)

                def weights_read(b):
                    act.wait_ge(os_["pc_T"], b + 1)
                    nc.scalar.activation(od.pcT[0:N_CMP, 2 * b:2 * b + 2, :],
                                         ps[0:N_CMP, 7, :].rearrange("p (h c) -> p h c", h=2),
                                         ACT.Copy).then_inc(os_["pcT_done"], 1)

                act.wait_ge(os_["gate_mm"], 1)
                nc.scalar.activation(od.gT[0:3 * NH, :], ps[0:3 * NH, 3, 0:SEQ], ACT.Copy).then_inc(os_["gT_done"], 1)
                for c, name in enumerate(ODD_ORDER):
                    read(name, c % 3)
                    hi_upto(at["odd", name] + 4)
                    if c == 1:
                        act.wait_ge(os_["gate_T"], 1)
                        nc.scalar.activation(od.gates, ps[:, 3, SEQ:SEQ + 48], ACT.Exp, scale=-1.0)\
                          .then_inc(os_["gates_done"], 1)
                    if c == 3:
                        act.wait_ge(os_["xc_done"], 1)
                        nc.scalar.activation(od.xc_hi, od.xc.rearrange("p k i g n -> p (k i g n)"), ACT.Copy)\
                          .then_inc(os_["xc_hi_done"], 1)
                for kv, (name, bank) in enumerate((("qs1", 0), ("a", 3))):
                    hi_upto(at["cmp", kv] + 4)
                    read(name, bank)
                    hi_upto(at["odd", name] + 4)
                    if kv:
                        hi_upto(at["cmp", 2] + 4)
                    act.wait_ge(chunks_used, at["cmp", 2 * kv + 1] + 1)
                    nc.scalar.activation(od.hid_rows[0:2 * N_CMP, kv, :], ps[0:2 * N_CMP, 5 + kv, 0:2 * P],
                                         ACT.Silu).then_inc(os_["hr_done"], 1)
                act.wait_ge(os_["hid_T"], 1)
                nc.scalar.activation(od.hid.rearrange("p k t c -> p (k t) c"),
                                     ps[:, 4, 0:P].rearrange("p (q c) -> p q c", q=4)[:, :, 0:2 * N_CMP],
                                     ACT.Copy).then_inc(os_["hid_done"], 1)
                hi_upto(at["cmp", 3] + 4)
                act.wait_ge(os_["c2_mm"], 1)
                act.wait_ge(os_["zeros_set"], 1)
                for g in range(2):
                    gs = slice(64 * g, 64 * g + 64)
                    nc.scalar.activation(od.kcT[gs, g, :], ps[gs, 7, 0:N_CMP], ACT.Copy)
                nc.scalar.activation(od.vc[0:N_CMP, :, :], ps[0:N_CMP, 7, 64:192].rearrange("p (g c) -> p g c", g=2),
                                     ACT.Copy).then_inc(os_["c2_read"], 1)
                unit_exp(0, 0)
                unit_exp(0, 1)
                act.wait_ge(os_["cs_in"], 1)
                nc.scalar.activation(od.pc, od.pc, ACT.Exp).then_inc(os_["cs_exp"], 1)
                kv_chunk(1, CS_FILL)
                for u in range(6):
                    if u < 5:
                        unit_exp(u + 1, 0)
                    for b in range(2):
                        act.wait_ge(os_["p_T"], 3 * u + b + 1)
                        if b == 0 and u >= 2:
                            act.wait_ge(os_["pv_mm"], pv_before(u))
                        nc.scalar.activation(od.pT[u % 2][:, b, :, :], ps[:, 4 + b, :].rearrange("p (h c) -> p h c", h=4),
                                             ACT.Copy).then_inc(os_["pT_act"], 1)
                    if u in (0, 2):
                        weights_read(u)
                    if u < 5:
                        unit_exp(u + 1, 1)
                    if UNIT_FILL[u][1]:
                        kv_chunk(1, UNIT_FILL[u][0])
                    if u in (0, 2):
                        weights_read(u + 1)
                    if u in PV_AFTER:
                        r = PV_AFTER.index(u)
                        act.wait_ge(os_["pv_mm"], r + 1)
                        nc.scalar.activation(hT_hi[:, 2 * r:2 * r + 2, :],
                                             ps[:, PV_BANK[r], :].rearrange("p (a c) -> p a c", a=2),
                                             ACT.Copy).then_inc(oT_hi_done, 1)

            def unit_exp(u, t):
                i = u % 2
                act.wait_ge(os_["nmax_done"], 2 * u + t + 1)
                if u >= 2 and t == 0:
                    act.wait_ge(os_["p_T"], 3 * (u - 1))
                for h in range(4):
                    if t == 0:
                        dst, src = od.p0[i][:, h, :], ps[:, 0, h * P:(h + 1) * P]
                    else:
                        dst, src = od.p1[i][:, h, :], ps[:, 1 + h // 2, (h % 2) * SEQ:(h % 2 + 1) * SEQ]
                    c = 4 * t + h
                    ins = nc.scalar.activation(dst, src, ACT.Exp, bias=od.nmax[i][:, c:c + 1],
                                               accum_out=od.rs[i][:, c:c + 1])
                if u >= 4 and t:
                    ins = nc.scalar.activation(od.es[i], od.es[i], ACT.Exp)
                ins.then_inc(os_["p_exp"], 1)

            def small_tables(c):
                if c == 0:
                    act.wait_ge(small_in, SMALL)
                    act.wait_ge(small_w_set, 1)
                    nc.scalar.activation(small_w_hi[:, :], small_w, ACT.Copy)
                elif c == 1:
                    nc.scalar.activation(masks[:, :], masks_f, ACT.Copy).then_inc(consts_made, 1)

            act.dma_start(consts[:, 0:P], d["consts"][:, 0:P]).then_inc(ident_in, 16)
            norm(0, 0)
            ffn(0, 0)
            norm(0, 1)
            hi_upto(at["even", "x0"] + 3)
            even()
            hi_upto(at["wq", 0, 0])
            norm(0, 2, ahead=at["wq", 0, 0] + 1)
            cross(0)
            norm(0, 3)
            ffn(0, 1)
            norm(1, 0)
            ffn(1, 0)
            norm(1, 1)
            hi_upto(at["odd", ODD_ORDER[0]] + 3)
            odd()
            hi_upto(at["wq", 1, 0])
            norm(1, 2, ahead=at["wq", 1, 0] + 1)
            cross(1)
            norm(1, 3)
            ffn(1, 1)
            squares(9, x, lambda t, h: act.wait_ge(x_added, 4 * 7 + 2 * t + h + 1))

        @block.vector
        def _(dve):
            made, steps, r = [0], [0], [0]
            V = nc.vector

            def step(ins):
                steps[0] += 1
                ins.then_inc(dve_step, 1)
                dve.wait_ge(dve_step, steps[0])

            def lo_upto(limit):
                for n in range(made[0], min(limit, n_chunks)):
                    dve.wait_ge(hi_done, n + 1)
                    for hi, lo, src in parts_of(n):
                        ins = V.tensor_tensor(lo, src, hi.bitcast(F32), ALU.subtract)
                    ins.then_inc(lo_done, 1)
                    made[0] = n + 1

            def norm_rows(v, ahead=0, tiles=(0, 1)):
                src = mem_rows if v == 1 else x
                dve.wait_ge(norm_w_in, 16 * (v + 1))
                for t in tiles:
                    if t:
                        lo_upto(ahead)
                    dve.wait_ge(rstd_done, 2 * v + t + 1)
                    if v == 1:
                        dve.wait_ge(transposed, 2 * t + 2)
                    for h in range(2):
                        hs = slice(h * 512, (h + 1) * 512)
                        V.scalar_tensor_tensor(xn[:, t, hs], src[:, t, hs], rstd[:, t:t + 1], norm_w[:, hs],
                                               ALU.mult, ALU.mult).then_inc(xn_done, 1)

            def evac_lo(w, hi, lo, tiles=(0, 1)):
                for t in tiles:
                    for kh in range(2):
                        dve.wait_ge(hT_hi_done, 4 * w + 2 * t + kh + 1)
                        ks, ts = slice(4 * kh, 4 * kh + 4), slice(t * P, (t + 1) * P)
                        V.tensor_tensor(lo[:, ks, ts], ps[:, row_bank(w, t, kh), :].rearrange("p (k c) -> p k c", c=P),
                                        hi[:, ks, ts].bitcast(F32), ALU.subtract).then_inc(hT_done, 1)

            def norm(layer, i, ahead=0):
                norm_rows(norm_no(layer, i), ahead)
                if layer == 0 and i == 0:
                    evac_lo(0, hT_hi, hT_lo, tiles=(0,))
                    lo_upto(1)
                    evac_lo(0, hT_hi, hT_lo, tiles=(1,))
                else:
                    evac_lo(SETS["norm", layer, i], hT_hi, hT_lo)

            def oT_lo(count, k0, bank):
                dve.wait_ge(oT_hi_done, count)
                V.tensor_tensor(hT_lo[:, k0:k0 + 2, :], ps[:, bank, :].rearrange("p (a c) -> p a c", a=2),
                                hT_hi[:, k0:k0 + 2, :].bitcast(F32), ALU.subtract).then_inc(oT_done, 1)

            def add_residual(last_chunk, coef, norm=None):
                r[0] += 1
                lo_upto(last_chunk + 2)
                for t in range(TT):
                    for h in range(2):
                        if t == 0 or h == 0:
                            dve.wait_ge(row_done, 3 * (r[0] - 1) + 2 * t + h + 1)
                        else:
                            dve.wait_ge(chunks_used, last_chunk + 1)
                        xs = x[:, t, h * 512:(h + 1) * 512]
                        V.scalar_tensor_tensor(xs, ps[:, 4 + 2 * t + h, :], coef, xs,
                                               ALU.mult, ALU.add).then_inc(x_added, 1)
                        if t == 0 and h == 0 and norm in FILL:
                            lo_upto(last_chunk + 3)

            def ffn(layer, which):
                f, base = 2 * layer + which, at["ffn", layer, which]

                def product(j, used):
                    dve.wait_ge(silu_done, j + (f * FJ + 1))
                    dve.wait_ge(chunks_used, used)
                    V.tensor_tensor(gu, g_act, ps[:, 1, :], ALU.mult).then_inc(mult_done, 1)

                def hidden_lo(j, hi, lo):
                    dve.wait_ge(gu_hi_done, j + (f * FJ + 1))
                    V.tensor_tensor(lo, gu.rearrange("p (k c) -> p k c", k=2), hi.bitcast(F32),
                                    ALU.subtract).then_inc(gu_done, 1)

                def turn(j, between=lambda c: None):
                    for c in range(3):
                        m = base + 2 + c + RING
                        if c == 1:
                            dve.wait_ge(gu_done, j + f * FJ)
                            product(j, j * 3 + (base + 1))
                        if c == 2:
                            hidden_lo(j, gu_hi, gu_lo)
                        dve.wait_ge(hi_done, (j - 1) * 3 + (m + 1))
                        V.tensor_tensor(w_lo[:, m % RING, :], raw[:, m % RING, :],
                                        w_hi[:, m % RING, :].bitcast(F32), ALU.subtract).then_inc(lo_done, 1)
                        between(c)

                lo_upto(base + 4)
                product(0, base + 2)
                lo_upto(base + 5)
                hidden_lo(0, gu_hi, gu_lo)
                if f == 0:
                    turn(1)
                    turn(2, mem_rows_done)
                    turn(3, lambda c: c < 2 and evac_lo(SETS["mem"], memT_hi, memT_lo, tiles=(c,)))
                with dve.Fori(1 if f else 4, FJ - 1) as j:
                    turn(j)
                made[0] = base + FFN_CHUNKS - 1
                j = FJ - 1
                dve.wait_ge(gu_done, j + f * FJ)
                lo_upto(base + FFN_CHUNKS)
                product(j, j * 3 + base + 1)
                hidden_lo(j, gu_hi_last, gu_lo_last)
                add_residual(base + FFN_CHUNKS - 1, 0.5, ("norm", layer + which, 1 - which))

            def cross(layer):
                u = 4 * layer
                wq, wo = at["wq", layer, 0], at["wo", layer, 0]

                def maxima(h):
                    dve.wait_ge(xs_["s_mm"], u + h + 1)
                    V.tensor_reduce(cr.nmax[:, 2 * h:2 * h + 2], ps[:, 4 + h, :].rearrange("p (t c) -> p t c", t=2),
                                    axis=AX.X, op=ALU.max, negate=True).then_inc(xs_["nmax"], 1)

                def probabilities(h):
                    dve.wait_ge(xs_["p_exp"], 2 * (u + h + 1))
                    step(V.reciprocal(cr.fac[:, 2 * h:2 * h + 2], cr.rs[:, 2 * h:2 * h + 2]))
                    V.tensor_tensor(cr.p[:, h, :, :], cr.p[:, h, :, :],
                                    cr.fac[:, 2 * h:2 * h + 2].unsqueeze(2).to_broadcast([P, 2, MEM]),
                                    ALU.mult).then_inc(xs_["p_done"], 1)

                lo_upto(wq + 5)
                maxima(0)
                for h in range(1, XH):
                    maxima(h)
                    probabilities(h - 1)
                probabilities(XH - 1)
                lo_upto(wq + 6)
                for h in range(XH):
                    oT_lo(OT_BASE[f"cross{layer}"] + h + 1, 2 * h, h)
                add_residual(wo + 3, 1.0, ("norm", layer, 3))

            def rotate(e, i):
                E = at["even", "x0"]
                dve.wait_ge(chunks_used, E + e + 1)
                if i:
                    dve.wait_ge(es["rot_done"], i)
                pair = ps[:, e % 3, :].rearrange("p (t h i two) -> p t h i two", t=TT, h=2, two=2)
                cosr, sinr = const("cos", TT, 64), const("sin", TT, 64)
                for t in range(TT):
                    c, s = (v[:, t, :].unsqueeze(1).to_broadcast([P, 2, 64]) for v in (cosr, sinr))
                    for r, (which, table) in enumerate(((0, c), (1, s), (0, s), (1, c))):
                        ins = V.tensor_tensor(ev.rot[r][:, t, :, :],
                                              pair[:, t, :, :, which], table, ALU.mult)
                ins.then_inc(es["rot_read"], 1)

            def even():
                E = at["even", "x0"]
                dve.wait_ge(es["dt_mm"], 1)
                V.tensor_copy(ev.dtT[0:SSM_H, :], ps[0:SSM_H, 3, 0:SEQ]).then_inc(es["dtT_done"], 1)
                for c in range(3):
                    dve.wait_ge(es["act_read"], c + 1)
                    for tap in (2, 1, 0):
                        for m in range(2):
                            k = 2 * c + m
                            ins = V.scalar_tensor_tensor(ev.xbcT[:, k, :], ev.xpad[:, k, tap:tap + SEQ],
                                                         conv_w[:, tap, k:k + 1], ev.xbcT[:, k, :],
                                                         ALU.mult, ALU.add)
                            if tap:
                                if m:
                                    step(ins)
                            elif m:
                                ins.then_inc(es["conv_done"], 1)
                    lo_upto(E + c + 4)
                    if c == 0:
                        dve.wait_ge(es["dt_T"], 1)
                        V.tensor_tensor(ev.dtr.rearrange("p (t h) -> p t h", t=TT),
                                        ps[:, 3, SEQ:SEQ + 16].rearrange("p (t h) -> p t h", t=TT),
                                        head_rows[:, 0, :].unsqueeze(1).to_broadcast([P, TT, SSM_H]),
                                        ALU.add).then_inc(es["dt_raw"], 1)
                dve.wait_ge(es["ln_done"], 1)
                step(V.scalar_tensor_tensor(ev.dt, ev.dtr, 0.0, ev.ln1p, ALU.max, ALU.add))
                dve.wait_ge(es["ea_done"], 1)
                V.scalar_tensor_tensor(ev.dta.rearrange("p (t h) -> p t h", t=TT),
                                       ev.dt.rearrange("p (t h) -> p t h", t=TT), -1.0,
                                       ev.ea.unsqueeze(1).to_broadcast([P, TT, SSM_H]),
                                       ALU.mult, ALU.mult).then_inc(es["dta_done"], 1)
                for i in range(4):
                    if i == 3:
                        for g in range(2):
                            dve.wait_ge(es["cb_mm"], g + 1)
                            V.tensor_tensor(ev.cbm[:, :, g, :],
                                            ps[:, 6 + g, 0:2 * P].rearrange("p (c l) -> p c l", c=TT),
                                            const("upto").unsqueeze(1).to_broadcast([P, TT, P]),
                                            ALU.mult).then_inc(es["cbm_done"], 1)
                    rotate(3 + i, i)
                    lo_upto(E + 3 + i + 4)
                dve.wait_ge(es["xh_done"], TT)
                dve.wait_ge(es["rot_done"], 4)
                V.tensor_tensor(ev.xdt.rearrange("p t h c -> p (t h) c"), ev.xh.rearrange("p t h c -> p (t h) c"),
                                ev.dt.unsqueeze(2).to_broadcast([P, TT * SSM_H, HP]),
                                ALU.mult).then_inc(es["xdt_done"], 1)
                lo_upto(E + 7 + 4)
                lo_upto(E + 8 + 4)
                for q in range(4):
                    dve.wait_ge(es["seg_exp"], q + 1)
                    m = ev.mt[:, q // 2, 4 * (q % 2):4 * (q % 2) + 4, :]
                    V.tensor_tensor(m, m, ev.cbm[:, q // 2, q % 2, :].unsqueeze(1).to_broadcast([P, 4, P]),
                                    ALU.mult).then_inc(es["mt_done"], 1)
                dve.wait_ge(es["dec_done"], 1)
                dve.wait_ge(es["xdt_done"], 1)
                V.tensor_tensor(ev.xdtd, ev.xdt[:, 0, :, :], ev.dec.unsqueeze(2).to_broadcast([P, SSM_H, HP]),
                                ALU.mult).then_inc(es["xdtd_done"], 1)
                for e in range(9, 13):
                    lo_upto(E + e + 4)
                dve.wait_ge(es["qkT_done"], 4)
                dve.wait_ge(es["kz_done"], 1)
                for t, bank in enumerate((7, 1)):
                    dve.wait_ge(es["ret_s_mm"], t + 1)
                    V.tensor_tensor(ev.s[:, t, :, :], ps[:, bank, :].rearrange("p (h i) -> p h i", h=RET_H),
                                    const("decayT", RET_H, P), ALU.mult).then_inc(es["s_done"], 1)
                dve.wait_ge(es["dx_done"], 1)
                hc = "p (h c) -> p h c"
                dve.wait_ge(es["y_mm"], 1)
                step(V.tensor_tensor(ev.xh[:, 0, :, :], ev.xh[:, 0, :, :], ps[:, 4, :].rearrange(hc, h=SSM_H), ALU.add))
                dve.wait_ge(es["act_read"], 9)
                V.tensor_tensor(ev.xh[:, 0, :, :], ev.xh[:, 0, :, :], xn[:, 0, 512:].rearrange(hc, h=SSM_H),
                                ALU.mult).then_inc(es["y_ready"], 1)
                dve.wait_ge(es["y_mm"], 2)
                step(V.tensor_tensor(ev.xh[:, 1, :, :], ev.xh[:, 1, :, :], ps[:, 5, :].rearrange(hc, h=SSM_H), ALU.add))
                dve.wait_ge(es["yoff_mm"], 1)
                for g, bank in enumerate((0, 2)):
                    ins = V.tensor_tensor(ev.yc[:, 4 * g:4 * g + 4, :], ps[:, bank, 0:256].rearrange(hc, h=4),
                                          ev.cum[:, 4 * g:4 * g + 4].unsqueeze(2).to_broadcast([P, 4, HP]), ALU.mult)
                step(ins)
                step(V.tensor_tensor(ev.xh[:, 1, :, :], ev.xh[:, 1, :, :], ev.yc, ALU.add))
                V.tensor_tensor(ev.xh[:, 1, :, :], ev.xh[:, 1, :, :], xn[:, 1, 512:].rearrange(hc, h=SSM_H),
                                ALU.mult).then_inc(es["y_ready"], 1)
                lo_upto(at["kv", 0, 0] + 4)
                dve.wait_ge(es["o_mm"], 1)
                V.tensor_copy(ev.o[:, 0, :, :], ps[:, 7, :].rearrange("p (h e) -> p h e", h=RET_H))\
                 .then_inc(es["y_read"], 1)
                dve.wait_ge(es["o_mm"], 2)
                step(V.tensor_tensor(ev.o[:, 1, :, :], ps[:, 4, :].rearrange("p (h e) -> p h e", h=RET_H),
                                     const("xi").unsqueeze(2).to_broadcast([P, RET_H, P]), ALU.mult))
                V.tensor_tensor(ev.o[:, 1, :, :], ev.o[:, 1, :, :], ps[:, 1, :].rearrange("p (h e) -> p h e", h=RET_H),
                                ALU.add).then_inc(es["o_read"], 1)
                lo_upto(at["kv", 0, 1] + 4)
                dve.wait_ge(es["o_sq"], 1)
                V.tensor_reduce(ev.osq.rearrange("p (t h) -> p t h", t=TT),
                                ev.mt[:, :, 0:4, :], axis=AX.X, op=ALU.add).then_inc(es["o_ssq"], 1)
                dve.wait_ge(es["y_rstd"], 1)
                for t in range(TT):
                    V.scalar_tensor_tensor(xn[:, t, 512:], ev.xh[:, t, :, :].rearrange("p h c -> p (h c)"),
                                           ev.rsr[:, t:t + 1], ssm_nw[:, :], ALU.mult, ALU.mult)
                lo_upto(at["kv", 0, 2] + 4)
                dve.wait_ge(es["o_rstd"], 1)
                for t in range(TT):
                    ins = V.tensor_tensor(ev.o[:, t, :, :], ev.o[:, t, :, :],
                                          ev.ors[:, 4 * t:4 * t + 4].unsqueeze(2).to_broadcast([P, RET_H, P]), ALU.mult)
                step(ins)
                for t in range(TT):
                    g = xn[:, t, 0:512]
                    V.tensor_tensor(g, g, ev.o[:, t, :, :].rearrange("p h e -> p (h e)"), ALU.mult)\
                     .then_inc(es["mix_done"], 1)
                lo_upto(at["kv", 0, 5] + 3)
                evac_lo(SETS["mix0"], hT_hi, hT_lo)
                add_residual(at["mixout", 0, 3], 1.0)

            def odd():
                for c, name in enumerate(ODD_ORDER):
                    lo_upto(at["odd", name] + 4)
                    if c == 2:
                        dve.wait_ge(os_["gates_done"], 1)
                        step(V.tensor_scalar(od.gates, od.gates, 1.0, None, ALU.add))
                        step(V.reciprocal(od.gates, od.gates))
                    if c == 3:
                        compress_in()
                lo_upto(at["cmp", 3] + 3)
                maxima(0)
                probabilities(0)
                lo_upto(at["cmp", 3] + 4)
                cm, cb = const("cmpmask", TT, N_CMP), const("cmpbias", TT, N_CMP)
                dve.wait_ge(os_["cs_mm"], 1)
                for t in range(TT):
                    for g in range(2):
                        src = ps[:, 4, t * 128:(t + 1) * 128].rearrange("p (m n) -> p m n", m=4)
                        ins = V.tensor_tensor(od.pc[:, t, 4 * g:4 * g + 4, :], src[:, :, g * N_CMP:(g + 1) * N_CMP],
                                              cm[:, t, :].unsqueeze(1).to_broadcast([P, 4, N_CMP]), ALU.mult)
                step(ins)
                for t in range(TT):
                    ins = V.tensor_tensor(od.pc[:, t, :, :], od.pc[:, t, :, :],
                                          cb[:, t, :].unsqueeze(1).to_broadcast([P, NH, N_CMP]), ALU.add)
                step(ins)
                pcf = od.pc.rearrange("p t h n -> p (t h) n")
                step(V.tensor_reduce(od.cmax, pcf, axis=AX.X, op=ALU.max, negate=True))
                V.tensor_tensor(pcf, pcf, od.cmax.unsqueeze(2).to_broadcast([P, 16, N_CMP]), ALU.add)\
                 .then_inc(os_["cs_in"], 1)
                dve.wait_ge(os_["cs_exp"], 1)
                for t in range(TT):
                    ins = V.tensor_tensor(od.pc[:, t, :, :], od.pc[:, t, :, :],
                                          cm[:, t, :].unsqueeze(1).to_broadcast([P, NH, N_CMP]), ALU.mult)
                step(ins)
                step(V.tensor_reduce(od.csum, pcf, axis=AX.X, op=ALU.add))
                step(V.tensor_scalar(od.csum, od.csum, 1e-30, None, ALU.max))
                step(V.reciprocal(od.csum, od.csum))
                g3 = od.gates.rearrange("p (q b) -> p q b", b=3)
                step(V.tensor_tensor(od.csum, od.csum, g3[:, :, 0], ALU.mult))
                V.tensor_tensor(pcf, pcf, od.csum.unsqueeze(2).to_broadcast([P, 16, N_CMP]), ALU.mult)\
                 .then_inc(os_["pc_done"], 1)
                for u in range(6):
                    if u < 5:
                        maxima(u + 1)
                    dve.wait_ge(os_["p_T"], 3 * u + 3)
                    if u >= 2:
                        dve.wait_ge(os_["pv_mm"], pv_before(u))
                    V.tensor_copy(od.pT[u % 2][:, 2, :, :], ps[:, 6, :].rearrange("p (h c) -> p h c", h=4))\
                     .then_inc(os_["pT_dve"], 1)
                    if u < 5:
                        probabilities(u + 1)
                    if u == 0:
                        lo_upto(at["kv", 1, CS_FILL] + 4)
                    if UNIT_FILL[u][1]:
                        lo_upto(at["kv", 1, UNIT_FILL[u][0]] + 4)
                    if u in PV_AFTER:
                        r = PV_AFTER.index(u)
                        oT_lo(OT_BASE["odd"] + r + 1, 2 * r, PV_BANK[r])
                add_residual(at["mixout", 1, 3], 1.0)

            def maxima(u):
                a, g = UNITS[u]
                for t in range(TT):
                    dve.wait_ge(os_["s_mm"], 2 * u + t + 1)
                    rows = slice(4 * t, 4 * t + 4)
                    src = ps[:, 0, :].rearrange("p (h c) -> p h c", h=4) if t == 0 else \
                        ps[:, 1:3, :].rearrange("p b (h c) -> p (b h) c", h=2)
                    nm = od.nmax[u % 2][:, rows]
                    ins = V.tensor_reduce(od.nmax2[:, rows] if a == 2 else nm, src, axis=AX.X, op=ALU.max, negate=True)
                    if a == 2:
                        step(ins)
                        sink = head_rows[:, 3, 4 * g:4 * g + 4]
                        step(V.scalar_tensor_tensor(nm, sink, -1.0, od.nmax2[:, rows], ALU.mult, ALU.min))
                        ins = V.tensor_tensor(od.es[u % 2][:, rows], nm, sink, ALU.add)
                    ins.then_inc(os_["nmax_done"], 1)

            def probabilities(u):
                a, g = UNITS[u]
                i = u % 2
                fac = od.fac[i]
                dve.wait_ge(os_["p_exp"], 2 * u + 2)
                if a == 2:
                    step(V.tensor_tensor(od.rs[i], od.rs[i], od.es[i], ALU.add))
                step(V.reciprocal(fac, od.rs[i]))
                if a < 2:
                    gate = od.gates.rearrange("p (t h b) -> p t h b", t=TT, b=3)[:, :, 4 * g:4 * g + 4, 1 + a]
                    f2 = fac.rearrange("p (t h) -> p t h", t=TT)
                    step(V.tensor_tensor(f2, f2, gate, ALU.mult))
                for p, f, n in ((od.p0[i], fac[:, 0:4], P), (od.p1[i], fac[:, 4:8], SEQ)):
                    V.tensor_tensor(p, p, f.unsqueeze(2).to_broadcast([P, 4, n]), ALU.mult).then_inc(os_["p_done"], 1)

            def compress_in():
                dve.wait_ge(os_["pick_mm"], 1)
                for kv in range(2):
                    pairs = ps[:, 4, kv * 256:(kv + 1) * 256].rearrange("p (g n i) -> p g n i", g=2, i=8)
                    for half in range(2):
                        for g in range(2):
                            ins = V.tensor_tensor(
                                od.xc[:, kv, 8 * half:8 * half + 8, g, :],
                                pairs[:, g, half:half + N_CMP, :].rearrange("p n i -> p i n"),
                                pe_pairs[:, kv, 8 * half:8 * half + 8].unsqueeze(2).to_broadcast([P, 8, N_CMP]),
                                ALU.add)
                ins.then_inc(os_["xc_done"], 1)
                dve.wait_ge(os_["xc_hi_done"], 1)
                V.tensor_tensor(od.xc_lo, od.xc.rearrange("p k i g n -> p (k i g n)"), od.xc_hi.bitcast(F32),
                                ALU.subtract).then_inc(os_["xc_lo_done"], 1)

            def mem_rows_done(c):
                if c < 2:
                    norm_rows(1, tiles=(c,))
                else:
                    dve.wait_ge(consts_made, 1)
                    V.tensor_tensor(small_w_lo[:, :], small_w, small_w_hi[:, :].bitcast(F32),
                                    ALU.subtract).then_inc(smalls_split, 1)

            norm(0, 0)
            ffn(0, 0)
            norm(0, 1)
            lo_upto(at["even", "x0"] + 3)
            even()
            norm(0, 2, ahead=at["wq", 0, 0] + 1)
            lo_upto(at["wq", 0, 0] + 3)
            cross(0)
            norm(0, 3)
            ffn(0, 1)
            norm(1, 0)
            ffn(1, 0)
            norm(1, 1)
            lo_upto(at["odd", ODD_ORDER[0]] + 3)
            odd()
            norm(1, 2, ahead=at["wq", 1, 0] + 1)
            lo_upto(at["wq", 1, 0] + 3)
            cross(1)
            norm(1, 3)
            ffn(1, 1)
            norm_rows(9)

        @block.gpsimd
        def _(pool):
            G = nc.gpsimd
            steps = [0]

            def step(ins):
                steps[0] += 1
                ins.then_inc(pool_step, 1)
                pool.wait_ge(pool_step, steps[0])

            def load_norm_w(v):
                if v:
                    pool.wait_ge(xn_done, 4 * v)
                src = d["mem_norm_w"] if v == 1 else d["final_norm_w"] if v == 9 else \
                    d["norm_w"][(v - 1) // 4, (v - 1) % 4] if v else d["norm_w"][0, 0]
                pool.dma_start(norm_w[:, :], src.partition_broadcast(P)).then_inc(norm_w_in, 16)

            def inv_rms(dst, tmp, src, width, count):
                step(G.tensor_scalar(tmp, src, 1.0 / count, EPS, ALU.mult, ALU.add))
                return G.tensor_tensor(dst, tmp, neg_half[:, 0:width], ALU.pow)

            def norm(v):
                for t in range(TT):
                    pool.wait_ge(sq_done, 4 * v + 2 * t + 2)
                    step(G.tensor_scalar(msq[:, t:t + 1], msum[:, 2 * t:2 * t + 1], msum[:, 2 * t + 1:2 * t + 2], EPS,
                                         ALU.add, ALU.add))
                    G.tensor_tensor(rstd[:, t:t + 1], msq[:, t:t + 1], neg_half[:, 0:1],
                                    ALU.pow).then_inc(rstd_done, 1)
                if v < 9:
                    load_norm_w(v + 1)

            def even():
                pool.wait_ge(x_added, 4)
                G.memset(ev.xpad[:, :, 0:CONV_W - 1], 0.0).then_inc(es["xpad_zero"], 1)
                for i in range(4):
                    pool.wait_ge(es["rot_read"], i + 1)
                    a, b, c, e = ev.rot
                    dst = ev.q_rot if i < 2 else ev.k_rot
                    for t in range(TT):
                        hs = slice(2 * (i % 2), 2 * (i % 2) + 2)
                        r = [v[:, t, :, :] for v in (a, b, c, e)]
                        G.tensor_tensor(dst[:, t, hs, 0, :], r[0], r[1], ALU.subtract)
                        ins = G.tensor_tensor(dst[:, t, hs, 1, :], r[2], r[3], ALU.add)
                    ins.then_inc(es["rot_done"], 1)
                    if i in (1, 2):
                        seg_weights(i - 1)
                pool.wait_ge(es["rot_done"], 4)
                G.tensor_tensor(ev.kz, ev.k_rot[:, 0, :, :, :].rearrange("p h a b -> p h (a b)"),
                                const("zeta").unsqueeze(2).to_broadcast([P, RET_H, P]),
                                ALU.mult).then_inc(es["kz_done"], 1)
                pool.wait_ge(es["xdt_done"], 1)
                G.tensor_tensor(ev.xh[:, 0], ev.xh[:, 0],
                                head_rows[:, 2, :].unsqueeze(2).to_broadcast([P, SSM_H, HP]), ALU.mult)
                G.tensor_tensor(ev.xh[:, 1], ev.xh[:, 1],
                                head_rows[:, 2, :].unsqueeze(2).to_broadcast([P, SSM_H, HP]),
                                ALU.mult).then_inc(es["dx_done"], 1)
                pool.wait_ge(es["y_sq"], 2)
                inv_rms(ev.rsr, ev.msr, ev.ssr, 2, SSM_IN).then_inc(es["y_rstd"], 1)
                pool.wait_ge(es["o_ssq"], 1)
                inv_rms(ev.ors, ev.oms, ev.osq, 8, DK).then_inc(es["o_rstd"], 1)

            def seg_weights(t):
                pool.wait_ge(es["conv_done"], 3)
                pool.wait_ge(es["dta_done"], 1)
                for h in range(SSM_H):
                    G.tensor_scalar(ev.ld[:, t, h, :], const("after"),
                                    ev.dta[:, 8 * t + h:8 * t + h + 1], None, ALU.mult).then_inc(es["ld_done"], 1)

            load_norm_w(0)
            G.memset(neg_half[:, :], -0.5).then_inc(neg_half_set, 1)
            pool.wait_ge(neg_half_set, 1)
            G.memset(small_w[:, SMALL_W - 120:], 0.0).then_inc(small_w_set, 1)
            norm(0)
            norm(1)
            pool.wait_ge(small_in, SMALL)
            norm(2)
            even()
            for v in range(3, 10):
                norm(v)
                if v == norm_no(1, 1):
                    pool.wait_ge(hT_done, 4 * SETS["norm", 1, 1] + 4)
                    G.memset(od.kcT, 0.0)
                    G.memset(od.xc_hi_wide[:, 960:].bitcast(F32), 0.0)
                    G.memset(od.xc_lo_wide[:, 960:].bitcast(F32), 0.0).then_inc(os_["zeros_set"], 1)

        @block.tensor
        def _(pe):
            mm = nc.tensor.matmul

            def product3(dst, l_hi, l_lo, r_hi, r_lo, start, stop):
                mm(dst, l_hi, r_hi, start=start, stop=False)
                mm(dst, l_hi, r_lo, start=False, stop=False)
                return mm(dst, l_lo, r_hi, start=False, stop=stop)

            def cols(w, n, k, width, lo, hi):
                return w[:, n % RING, k * width + lo:k * width + hi]

            def to_features(n, dst, a_hi, a_lo, tiles=(0, 1), col0=0):
                for m in tiles:
                    lo, hi = col0 + m * P, col0 + (m + 1) * P
                    for k in range(KT):
                        last = product3(dst[:, m * SEQ:(m + 1) * SEQ],
                                        cols(w_hi, n, k, CW, lo, hi), cols(w_lo, n, k, CW, lo, hi),
                                        a_hi[:, k, :], a_lo[:, k, :], k == 0, k == KT - 1)
                return last

            def to_tokens(n, dst, width, a_hi, a_lo, col0=0, tiles=(0, 1)):
                for t in tiles:
                    ts = slice(t * P, (t + 1) * P)
                    for k in range(KT):
                        last = product3(dst[:, t * width:(t + 1) * width], a_hi[:, k, ts], a_lo[:, k, ts],
                                        cols(w_hi, n, k, CW, col0, col0 + width),
                                        cols(w_lo, n, k, CW, col0, col0 + width), k == 0, k == KT - 1)
                return last

            def down(n, a_hi, a_lo, first, final, last_bank=None):
                for t in range(TT):
                    ts = slice(t * P, (t + 1) * P)
                    for h in range(2):
                        if last_bank and t and h:
                            last_bank()
                        for k in range(2):
                            last = product3(ps[:, 4 + 2 * t + h, :], a_hi[:, k, ts], a_lo[:, k, ts],
                                            cols(w_hi, n, k, D, h * 512, (h + 1) * 512),
                                            cols(w_lo, n, k, D, h * 512, (h + 1) * 512),
                                            first and k == 0, final and k == 1)
                        if final and 2 * t + h < 3:
                            last.then_inc(row_done, 1)
                return last

            def used(ins):
                return ins.then_inc(chunks_used, 1)

            def transposes(w, ready, tiles=(0, 1)):
                for t in tiles:
                    for kh in range(2):
                        ready(t, kh)
                        for k in range(4):
                            c = (4 * kh + k) * P
                            last = nc.tensor.transpose(ps[:, row_bank(w, t, kh), k * P:(k + 1) * P],
                                                       xn[:, t, c:c + P], ident)
                        last.then_inc(transposed, 1)

            def mem_turned(t):
                def ready(t, kh):
                    if t == 0:
                        pe.wait_ge(xn_done, 8)
                    else:
                        pe.wait_ge(hT_done, 4 * SETS["mem"] + kh + 1)
                transposes(SETS["mem"], ready, tiles=(t,))

            def norm(v, key):
                def ready(t, kh):
                    pe.wait_ge(xn_done, 4 * v + 2 * t + kh + 1)
                if key in FILL:
                    layer, i = FILL[key]
                    pe.wait_ge(x_added, 4 * (v - 2) + 1)
                    kv_half(layer, i, 0)
                    transposes(SETS[key], ready)
                    used(kv_half(layer, i, 1))
                else:
                    transposes(SETS[key], ready)
                pe.wait_ge(hT_done, 4 * SETS[key] + 4)

            def small_features(w0, width):
                for k in range(KT):
                    c0 = w0 + k * width
                    last = product3(ps[:, 3, 0:SEQ], small_w_hi[:, c0:c0 + P], small_w_lo[:, c0:c0 + P],
                                    hT_hi[:, k, :], hT_lo[:, k, :], k == 0, k == KT - 1)
                return last

            def small_tokens(src, width):
                for t in range(TT):
                    c0 = SEQ + t * width
                    last = nc.tensor.transpose(ps[:, 3, c0:c0 + width], src[0:width, t * P:(t + 1) * P],
                                               ident[0:width, 0:width])
                return last

            def ffn(layer, which):
                f, base = 2 * layer + which, at["ffn", layer, which]

                def hidden_down(j, n, first, final):
                    pe.wait_ge(gu_done, j)
                    used(down(n, gu_hi_last if final else gu_hi, gu_lo_last if final else gu_lo, first, final))

                pe.wait_ge(lo_done, base + 1)
                used(to_features(base, ps[:, 0, :], hT_hi, hT_lo))
                pe.wait_ge(lo_done, base + 2)
                used(to_features(base + 1, ps[:, 1, :], hT_hi, hT_lo))

                def turn(j, first, between=lambda c: None):
                    n = base + 2
                    pe.wait_ge(silu_done, j + f * FJ)
                    pe.wait_ge(lo_done, j * 3 + (n + 1 - 3))
                    used(to_features(n, ps[:, 0, :], hT_hi, hT_lo))
                    between(0)
                    pe.wait_ge(mult_done, j + f * FJ)
                    pe.wait_ge(lo_done, j * 3 + (n + 2 - 3))
                    used(to_features(n + 1, ps[:, 1, :], hT_hi, hT_lo))
                    between(1)
                    pe.wait_ge(lo_done, j * 3 + (n + 3 - 3))
                    if first and 0 < f < 3:
                        pe.wait_ge(kv_read, 8 + f)
                    hidden_down(j + f * FJ, n + 2, first, False)

                turn(1, True)
                if f == 0:
                    turn(2, False)
                    turn(3, False, mem_turned)
                with pe.Fori(2 if f else 4, FJ) as j:
                    turn(j, False)
                n = base + FFN_CHUNKS - 1
                pe.wait_ge(lo_done, n + 1)
                hidden_down((f + 1) * FJ, n, False, True)

            def kv_half(layer, i, half):
                n, bank = at["kv", layer, i], ps[:, KV_BANK[layer][i], :]
                pe.wait_ge(lo_done, n + 1)
                before = [m for m in range(i) if KV_BANK[layer][m] == KV_BANK[layer][i]]
                if before:
                    pe.wait_ge(kv_read, 8 * layer + before[-1] + 1)
                if i < 4:
                    return to_features(n, bank, memT_hi, memT_lo, tiles=(half,))
                return to_tokens(n, bank, CW, memT_hi, memT_lo, tiles=(half,))

            def kv_chunk(layer, i):
                kv_half(layer, i, 0)
                used(kv_half(layer, i, 1))

            def out_chunks(first_n, waits=None, last_bank=None):
                for i in range(4):
                    if waits:
                        waits(i)
                    pe.wait_ge(lo_done, first_n + i + 1)
                    used(down(first_n + i, hT_hi[:, 2 * i:2 * i + 2, :], hT_lo[:, 2 * i:2 * i + 2, :],
                              i == 0, i == 3, last_bank if i == 0 else None))

            def cross(layer):
                u = 4 * layer
                wq, wo = at["wq", layer, 0], at["wo", layer, 0]

                def project(i):
                    pe.wait_ge(lo_done, wq + i + 1)
                    if i == 3:
                        pe.wait_ge(xs_["q_read"], u + 1)
                    used(to_features(wq + i, ps[:, i % 3, :], hT_hi, hT_lo))

                def scores(h):
                    pe.wait_ge(xs_["q_read"], u + h + 1)
                    pe.wait_ge(kv_read, 8 * layer + 8)
                    for t in range(TT):
                        for k in range(2):
                            last = mm(ps[:, 4 + h, t * MEM:(t + 1) * MEM],
                                      cr.q[:, 2 * h + k, t * P:(t + 1) * P], xk[:, 2 * h + k, :],
                                      start=k == 0, stop=k == 1)
                    last.then_inc(xs_["s_mm"], 1)

                def turned(h):
                    pe.wait_ge(xs_["p_done"], u + h + 1)
                    pe.wait_ge(xs_["q_read"], u + 4)
                    if h == 3:
                        pe.wait_ge(xs_["pT_done"], u + 1)
                    bank = (3, 1, 2, 3)[h]
                    for kb in range(2):
                        for t in range(TT):
                            last = nc.tensor.transpose(ps[:, bank, kb * SEQ + t * P:kb * SEQ + (t + 1) * P],
                                                       cr.p[:, h, t, kb * P:(kb + 1) * P], ident)
                    last.then_inc(xs_["p_T"], 1)

                def values(h):
                    pe.wait_ge(xs_["pT_done"], u + h + 1)
                    for m in range(2):
                        for kb in range(2):
                            last = mm(ps[:, h, m * SEQ:(m + 1) * SEQ],
                                      xv[:, kb, h * XD + m * P:h * XD + (m + 1) * P], cr.pT[:, h, kb, :],
                                      start=kb == 0, stop=kb == 1)
                    last.then_inc(xs_["pv_mm"], 1)

                project(0)
                project(1)
                scores(0)
                project(2)
                scores(1)
                project(3)
                scores(2)
                scores(3)
                for h in range(XH):
                    turned(h)
                    if h:
                        values(h - 1)
                values(XH - 1)
                b = OT_BASE[f"cross{layer}"]
                out_chunks(wo, lambda i: pe.wait_ge(oT_done, b + i + 1))

            def even():
                E = at["even", "x0"]

                def project(e, bank_free=None):
                    n = E + e
                    pe.wait_ge(lo_done, n + 1)
                    if bank_free:
                        pe.wait_ge(es[bank_free[0]], bank_free[1])
                    if e < 3:
                        used(to_features(n, ps[:, e % 3, :], hT_hi, hT_lo))
                    else:
                        used(to_tokens(n, ps[:, e % 3, :], CW, hT_hi, hT_lo))

                small_features(DT_AT, SSM_H).then_inc(es["dt_mm"], 1)
                project(0)
                pe.wait_ge(es["dtT_done"], 1)
                small_tokens(ev.dtT, SSM_H).then_inc(es["dt_T"], 1)
                project(1)
                project(2)
                project(3, ("act_read", 1))
                project(4, ("act_read", 2))
                project(5, ("act_read", 3))
                project(6, ("rot_read", 1))
                pe.wait_ge(es["xbc_done"], 3)
                pe.wait_ge(es["dt_raw"], 1)
                for t in range(TT):
                    for k in range(4):
                        last = nc.tensor.transpose(ps[:, 4 + t, k * P:(k + 1) * P],
                                                   ev.xbcT[:, k, t * P:(t + 1) * P], ident)
                    last.then_inc(es["xs_T"], 1)
                nc.tensor.transpose(ps[:, 3, 0:P], ev.xbcT[:, 4, 0:P], ident).then_inc(es["xs_T"], 1)
                for g in range(2):
                    gs = slice(64 * g, 64 * g + 64)
                    for c in range(TT):
                        cs = slice(c * P, (c + 1) * P)
                        last = mm(ps[:, 6 + g, cs], ev.xbcT[gs, 4, cs], ev.xbcT[gs, 5, cs], start=True, stop=True)
                    last.then_inc(es["cb_mm"], 1)
                project(7, ("rot_read", 2))
                pe.wait_ge(es["dta_done"], 1)
                pe.wait_ge(es["xh_done"], 3)
                mm(ps[:, 3, P:P + 8], const("after"), ev.dta[:, 0:8], start=True, stop=True)
                mm(ps[:, 3, P + 8:P + 16], const("upto"), ev.dta[:, 8:16], start=True, stop=True)\
                    .then_inc(es["dec_mm"], 1)
                for q in range(4):
                    pe.wait_ge(es["ld_done"], 4 * q + 4)
                    if q == 2:
                        pe.wait_ge(es["cbm_done"], 2)
                    for h in range(4):
                        last = mm(ps[:, 4 + q, h * P:(h + 1) * P], ev.ld[:, q // 2, 4 * (q % 2) + h, :],
                                  const("upto"), start=True, stop=True)
                    last.then_inc(es["seg_mm"], 1)
                project(8, ("rot_read", 3))
                project(9, ("rot_read", 4))
                project(10, ("act_read", 4))
                pe.wait_ge(es["rot_done"], 4)
                for i, src in enumerate((ev.q_rot, ev.k_rot)):
                    for t in range(TT):
                        pe.wait_ge(es["seg_exp"], 2 * i + t + 1)
                        for h in range(RET_H):
                            last = nc.tensor.transpose(ps[:, 4 + 2 * i + t, h * P:(h + 1) * P],
                                                       src[:, t, h, :, :].rearrange("p a b -> p (a b)"), ident)
                        last.then_inc(es["qk_T"], 1)
                project(11, ("act_read", 5))
                project(12, ("act_read", 6))
                for t in range(TT):
                    pe.wait_ge(es["mt_done"], 2 * t + 2)
                    pe.wait_ge(es["qkT_done"], t + 1)
                    for h in range(SSM_H):
                        last = mm(ps[:, 4 + t, h * HP:(h + 1) * HP], ev.mt[:, t, h, :], ev.xdt[:, t, h, :],
                                  start=True, stop=True)
                    last.then_inc(es["y_mm"], 1)
                pe.wait_ge(es["xdtd_done"], 1)
                pe.wait_ge(es["qkT_done"], 4)
                mm(ps[:, 6, :], ev.b_tok, ev.xdtd.rearrange("p h c -> p (h c)"), start=True, stop=True)\
                    .then_inc(es["st_mm"], 1)
                for t, bank in enumerate((7, 1)):
                    if t:
                        pe.wait_ge(es["act_read"], 7)
                    for h in range(RET_H):
                        last = mm(ps[:, bank, h * P:(h + 1) * P], ev.kT[:, t, h, :], ev.qT[:, t, h, :],
                                  start=True, stop=True)
                    last.then_inc(es["ret_s_mm"], 1)
                pe.wait_ge(es["dec_done"], 1)
                kv_chunk(0, 0)
                pe.wait_ge(es["st_done"], 1)
                pe.wait_ge(es["act_read"], 9)
                for g, bank in enumerate((0, 2)):
                    gs = slice(64 * g, 64 * g + 64)
                    last = mm(ps[:, bank, 0:256], ev.xbcT[gs, 5, P:2 * P], ev.sT[gs, 256 * g:256 * g + 256],
                              start=True, stop=True)
                last.then_inc(es["yoff_mm"], 1)
                pe.wait_ge(es["kz_done"], 1)
                for h in range(RET_H):
                    last = mm(ps[:, 6, h * P:(h + 1) * P], ev.kz[:, h, :], ev.v[:, 0, h * P:(h + 1) * P],
                              start=True, stop=True)
                last.then_inc(es["ret_kv_mm"], 1)
                kv_chunk(0, 1)
                for t, bank in enumerate((7, 1)):
                    pe.wait_ge(es["s_done"], t + 1)
                    for h in range(RET_H):
                        last = mm(ps[:, bank, h * P:(h + 1) * P], ev.s[:, t, h, :], ev.v[:, t, h * P:(h + 1) * P],
                                  start=True, stop=True)
                    if t == 0:
                        last.then_inc(es["o_mm"], 1)
                pe.wait_ge(es["kvs_done"], 1)
                pe.wait_ge(es["y_ready"], 1)
                for h in range(RET_H):
                    last = mm(ps[:, 4, h * P:(h + 1) * P], ev.qT[:, 1, h, :], ev.kv[:, h, :], start=True, stop=True)
                last.then_inc(es["o_mm"], 1)
                pe.wait_ge(es["y_ready"], 2)
                for i in range(2, 6):
                    kv_chunk(0, i)
                pe.wait_ge(kv_read, 2)
                transposes(SETS["mix0"], lambda t, kh: pe.wait_ge(es["mix_done"], t + 1))
                kv_chunk(0, 6)
                pe.wait_ge(hT_done, 4 * SETS["mix0"] + 4)
                pe.wait_ge(kv_read, 6)
                out_chunks(at["mixout", 0, 0], last_bank=lambda: pe.wait_ge(kv_read, 7))

            def odd():
                def project(name, bank):
                    n = at["odd", name]
                    pe.wait_ge(lo_done, n + 1)
                    if name[0] == "q":
                        last = to_features(n, bank, hT_hi, hT_lo)
                    elif name == "c":
                        last = to_tokens(n, bank, CW, hT_hi, hT_lo)
                    else:
                        to_features(n, bank, hT_hi, hT_lo, tiles=(0,))
                        last = to_tokens(n, bank[:, SEQ:], P, hT_hi, hT_lo, col0=P)
                    used(last)

                def weights_turned(b):
                    for i in range(2):
                        for t in range(TT):
                            last = nc.tensor.transpose(ps[0:N_CMP, 7, i * SEQ + t * P:i * SEQ + (t + 1) * P],
                                                       od.pc[:, t, 2 * b + i, :], ident)
                    last.then_inc(os_["pc_T"], 1)

                small_features(GATE_AT, 3 * NH).then_inc(os_["gate_mm"], 1)
                for c, name in enumerate(ODD_ORDER):
                    if c >= 3:
                        pe.wait_ge(os_["read"], c - 2)
                    project(name, ps[:, c % 3, :])
                    if c == 1:
                        pe.wait_ge(os_["gT_done"], 1)
                        small_tokens(od.gT, 3 * NH).then_inc(os_["gate_T"], 1)
                    if c == 3:
                        pe.wait_ge(os_["read"], 3)
                        pe.wait_ge(kv_read, 8 + 3)
                        for kv in range(2):
                            for g in range(2):
                                for t in range(TT):
                                    for par in range(2):
                                        c0 = (2 * kv + g) * P + t * 64
                                        f0 = kv * P + g * HD
                                        last = mm(ps[64 * par:64 * par + 64, 4, c0:c0 + 64],
                                                  od.kc[:, t, f0:f0 + HD],
                                                  const("pick", 2, 64)[:, par, :], start=True, stop=True)
                        last.then_inc(os_["pick_mm"], 1)
                pe.wait_ge(os_["xc_lo_done"], 1)
                pe.wait_ge(os_["zeros_set"], 1)

                def compress(i):
                    kv, half = i // 2, i % 2
                    n = at["cmp", i]
                    pe.wait_ge(lo_done, n + 1)
                    for k in range(8):
                        pair = 8 * half + k
                        c0 = (kv * CMP_PAIRS + pair) * 2 * N_CMP
                        last = product3(ps[:, 5 + kv, 0:2 * P], od.xc_hi_wide[:, c0:c0 + P], od.xc_lo_wide[:, c0:c0 + P],
                                        cols(w_hi, n, k, CW, 0, CW), cols(w_lo, n, k, CW, 0, CW),
                                        pair == 0, pair == 15)
                    used(last)

                compress(0)
                pe.wait_ge(os_["read"], 4)
                project("qs1", ps[:, 0, :])
                compress(1)
                pe.wait_ge(os_["gates_done"], 1)
                project("a", ps[:, 3, :])
                compress(2)
                compress(3)
                scores(0)
                for kv in range(2):
                    pe.wait_ge(os_["hr_done"], kv + 1)
                    for ht in range(2):
                        q = 2 * kv + ht
                        last = nc.tensor.transpose(ps[:, 4, 32 * q:32 * q + 2 * N_CMP],
                                                   od.hid_rows[0:2 * N_CMP, kv, ht * P:(ht + 1) * P],
                                                   ident[0:2 * N_CMP, 0:2 * N_CMP])
                last.then_inc(os_["hid_T"], 1)
                pe.wait_ge(os_["hid_done"], 1)
                for g in range(2):
                    for ht in range(2):
                        last = mm(ps[64 * g:64 * g + 64, 7, 0:N_CMP], w2[:, 0, ht, :],
                                  od.hid[:, 0, ht, g * N_CMP:(g + 1) * N_CMP], start=ht == 0, stop=ht == 1)
                for g in range(2):
                    for ht in range(2):
                        last = mm(ps[0:N_CMP, 7, 64 + 64 * g:128 + 64 * g],
                                  od.hid[:, 1, ht, g * N_CMP:(g + 1) * N_CMP], w2[:, 1, ht, :],
                                  start=ht == 0, stop=ht == 1)
                last.then_inc(os_["c2_mm"], 1)
                pe.wait_ge(os_["read"], 8)
                pe.wait_ge(os_["c2_read"], 1)
                for t in range(TT):
                    for m in range(4):
                        c0 = 128 * t + 32 * m
                        last = mm(ps[:, 4, c0:c0 + 2 * N_CMP], od.qn[:, m, t * P:(t + 1) * P],
                                  od.kcT.rearrange("p g n -> p (g n)"), start=True, stop=True)
                last.then_inc(os_["cs_mm"], 1)
                kv_chunk(1, CS_FILL)
                for u in range(6):
                    if u < 5:
                        scores(u + 1)
                    turned(u)
                    if u == 0:
                        pe.wait_ge(os_["pc_done"], 1)
                        weights_turned(0)
                    elif u == 2:
                        pe.wait_ge(oT_done, OT_BASE["odd"] + 1)
                        weights_turned(2)
                    i, half = UNIT_FILL[u]
                    last = kv_half(1, i, half)
                    if half:
                        used(last)
                    if u in (0, 2):
                        pe.wait_ge(os_["pcT_done"], u + 1)
                        weights_turned(u + 1)
                    if u in PV_AFTER:
                        values(PV_AFTER.index(u))
                pe.wait_ge(oT_done, OT_BASE["odd"] + 3)
                out_chunks(at["mixout", 1, 0], lambda i: pe.wait_ge(oT_done, OT_BASE["odd"] + i + 1))

            def scores(u):
                a, g = UNITS[u]
                if u == 0:
                    pe.wait_ge(os_["read"], 7)
                else:
                    pe.wait_ge(os_["p_exp"], 2 * u - 1)
                gs = slice(64 * g, 64 * g + 64)
                q = od.qs if a == 2 else od.qn
                eye = mask("eye")
                mm(ps[:, 0, :].rearrange("p (h c) -> p h c", h=4), eye,
                   mask("causal0").unsqueeze(1).to_broadcast([P, 4, P]), start=True, stop=False)
                for m in range(4):
                    last = mm(ps[:, 0, m * P:(m + 1) * P], q[gs, m, 0:P], od.kT[gs, a, 0:P],
                              start=False, stop=m == 3)
                last.then_inc(os_["s_mm"], 1)
                if u:
                    pe.wait_ge(os_["p_exp"], 2 * u)
                for b in range(2):
                    mm(ps[:, 1 + b, :].rearrange("p (h c) -> p h c", h=2), eye,
                       mask("band1" if a == 2 else "causal1").unsqueeze(1).to_broadcast([P, 2, SEQ]),
                       start=True, stop=False)
                    for i in range(2):
                        last = mm(ps[:, 1 + b, i * SEQ:(i + 1) * SEQ], q[gs, 2 * b + i, P:2 * P], od.kT[gs, a, :],
                                  start=False, stop=i == 1)
                last.then_inc(os_["s_mm"], 1)

            def turned(u):
                if u == 0:
                    pe.wait_ge(os_["cs_in"], 1)
                else:
                    pe.wait_ge(os_["pT_act"], 2 * u)
                    pe.wait_ge(os_["pT_dve"], u)
                i = u % 2
                for b in range(3):
                    pe.wait_ge(os_["p_done"], 2 * u + min(b, 1) + 1)
                    for h in range(4):
                        src = od.p0[i][:, h, :] if b == 0 else od.p1[i][:, h, (b - 1) * P:b * P]
                        last = nc.tensor.transpose(ps[:, 4 + b, h * P:(h + 1) * P], src, ident)
                    last.then_inc(os_["p_T"], 1)

            def values(r):
                u, bank = PV_AFTER[r], PV_BANK[r]
                pe.wait_ge(os_["pT_act"], 2 * (u + 1))
                pe.wait_ge(os_["pT_dve"], u + 1)
                if r < 2:
                    pe.wait_ge(os_["pcT_done"], 2 * r + 2)
                elif r == 2:
                    pe.wait_ge(oT_done, OT_BASE["odd"] + 2)
                a, g = UNITS[u]
                units = [u - 1, u] if a == 1 else [u]
                for h in range(4):
                    out_ps = ps[64 * (h % 2):64 * (h % 2) + 64, bank, (h // 2) * SEQ:(h // 2 + 1) * SEQ]
                    first = True
                    for w in units:
                        a_w = UNITS[w][0]
                        pT = od.pT[w % 2]
                        last_unit = w == units[-1] and a == 2
                        mm(out_ps, od.v[:, a_w, 0, g * HD:(g + 1) * HD], pT[:, 0:2, h, :], start=first, stop=False)
                        last = mm(out_ps[:, P:], od.v[:, a_w, 1, g * HD:(g + 1) * HD], pT[:, 2, h, :],
                                  start=False, stop=last_unit)
                        first = False
                    if a == 1:
                        last = mm(out_ps, od.vc[0:N_CMP, g, :], od.pcT[0:N_CMP, 4 * g + h, :], start=False, stop=True)
                last.then_inc(os_["pv_mm"], 1)

            pe.wait_ge(ident_in, 16)
            norm(0, ("norm", 0, 0))
            ffn(0, 0)
            norm(2, ("norm", 0, 1))
            pe.wait_ge(smalls_split, 1)
            even()
            norm(3, ("norm", 0, 2))
            cross(0)
            norm(4, ("norm", 0, 3))
            ffn(0, 1)
            norm(5, ("norm", 1, 0))
            ffn(1, 0)
            norm(6, ("norm", 1, 1))
            odd()
            norm(7, ("norm", 1, 2))
            cross(1)
            norm(8, ("norm", 1, 3))
            ffn(1, 1)


INPUTS = ["x", "mem", "norm_w", "final_norm_w", "mem_norm_w", "ffn_w_gate", "ffn_w_up", "ffn_w_down",
          "xattn_wq", "xattn_wkv", "xattn_wo", "even_w_in", "even_w_out", "ssm_conv_w", "ssm_conv_b",
          "ssm_dt_bias", "ssm_a_log", "ssm_d", "ssm_norm_w", "odd_w_in", "odd_w_out", "nsa_cmp_pe",
          "nsa_cmp_w1", "nsa_cmp_w2", "swa_sinks"]


def kernel(**inputs):
    import concourse.bacc as bacc
    from concourse.bass_utils import run_bass_kernel_spmd

    nc = bacc.Bacc("TRN2", target_bir_lowering=False, num_devices=1)
    arrays, d = {}, {}
    consts, masks = shape_constants()
    for name, a in [(n, inputs[n]) for n in INPUTS] + [("consts", consts), ("masks", masks)]:
        a = np.ascontiguousarray(a)
        arrays["in_" + name] = a
        d[name] = nc.dram_tensor("in_" + name, a.shape, mybir.dt.from_np(a.dtype), kind="ExternalInput").ap()
    out = nc.dram_tensor("out_0", (1, SEQ, D), F32, kind="ExternalOutput").ap()
    build(nc, d, out)
    r = run_bass_kernel_spmd(nc, [arrays], core_ids=[0])
    return r.results[0]["out_0"]
```
